# Optimizing a Trainium2 kernel written in Bass

```python
import jax
import jax.numpy as jnp
from jax import lax
import numpy as np

D_MODEL = 1024
BATCH = 1
SEQ = 256
DEPTH = 2
DEC_BATCH = 1
DEC_SEQ = 64
PAST_LEN = 256

CHUNK = 64
D_PLE = 256
N_ATT = (DEPTH + 1) // 2
N_REC = DEPTH // 2
HEAD_DIM = 64
FOX_HEADS = 8
Q_BLOCK = 128
SWA_HEADS = 8
SWA_KV_HEADS = 2
SWA_GROUP = SWA_HEADS // SWA_KV_HEADS
WINDOW = 128
WINDOW_CHUNKS = WINDOW // CHUNK
ML_HEADS = 4
ML_QK = 128
ML_V = 256
D_FF = 4096
CONV_W = 3
EPS = 1e-6
NEG = -1e30
ATT_SIZES = (FOX_HEADS * HEAD_DIM, FOX_HEADS * HEAD_DIM, FOX_HEADS * HEAD_DIM, FOX_HEADS, SWA_HEADS * HEAD_DIM, SWA_KV_HEADS * HEAD_DIM, SWA_KV_HEADS * HEAD_DIM)
REC_SIZES = (ML_HEADS * ML_QK, ML_HEADS * ML_QK, ML_HEADS * ML_V, ML_HEADS, ML_HEADS, ML_HEADS * ML_V)
ATT_IN = 3 * FOX_HEADS * HEAD_DIM + FOX_HEADS + SWA_HEADS * HEAD_DIM + 2 * SWA_KV_HEADS * HEAD_DIM
REC_IN = 2 * ML_HEADS * ML_QK + 2 * ML_HEADS * ML_V + 2 * ML_HEADS
ATT_OUT = (FOX_HEADS + SWA_HEADS) * HEAD_DIM
REC_OUT = ML_HEADS * ML_V

kernel_name = 'hybrid_fox_swa_mlstm_stream_step'

def rmsnorm(x, g):
    xf = x.astype(jnp.float32)
    y = xf * lax.rsqrt(jnp.mean(xf * xf, axis=-1, keepdims=True) + EPS)
    return (y * g.astype(jnp.float32)).astype(x.dtype)

def split_cols(z, sizes):
    idx, acc = [], 0
    for s in sizes[:-1]:
        acc += s
        idx.append(acc)
    return jnp.split(z, idx, axis=-1)

def fox_block(q, k, v, fq, fk, qpos, kpos):
    s = jnp.einsum('bqhd,bkhd->bhqk', q, k, preferred_element_type=jnp.float32) * (HEAD_DIM ** -0.5)
    s = s + (jnp.transpose(fq, (0, 2, 1))[..., :, None] - jnp.transpose(fk, (0, 2, 1))[..., None, :])
    s = jnp.where(kpos[None, :] <= qpos[:, None], s, NEG)
    w = jax.nn.softmax(s, axis=-1)
    return jnp.einsum('bhqk,bkhd->bqhd', w.astype(v.dtype), v)

def fox_prompt(q, k, v, logf):
    b, S, h, d = q.shape
    nb = S // Q_BLOCK
    F = jnp.cumsum(logf, axis=1)
    pos = jnp.arange(S)
    qb = jnp.swapaxes(q.reshape(b, nb, Q_BLOCK, h, d), 0, 1)
    fb = jnp.swapaxes(F.reshape(b, nb, Q_BLOCK, h), 0, 1)
    pb = pos.reshape(nb, Q_BLOCK)
    o = lax.map(lambda a: fox_block(a[0], k, v, a[1], F, a[2], pos), (qb, fb, pb))
    return jnp.swapaxes(o, 0, 1).reshape(b, S, h, d)

def fox_sample(q, k, v, logf, ck, cv, clogf):
    P, S = ck.shape[1], q.shape[1]
    k_all = jnp.concatenate([ck.astype(k.dtype), k], axis=1)
    v_all = jnp.concatenate([cv.astype(v.dtype), v], axis=1)
    F = jnp.cumsum(jnp.concatenate([clogf.astype(jnp.float32), logf], axis=1), axis=1)
    return fox_block(q, k_all, v_all, F[:, P:], F, P + jnp.arange(S), jnp.arange(P + S))

def sink_attend(q, k, v, sink, valid):
    s = jnp.einsum('bnqhgd,bnkhd->bnhgqk', q, k, preferred_element_type=jnp.float32) * (HEAD_DIM ** -0.5)
    s = jnp.where(valid[None, :, None, None, None, :], s, NEG)
    sk = sink.astype(jnp.float32)[None, None, :, :, None, None]
    m = jnp.maximum(jnp.max(s, axis=-1, keepdims=True), sk)
    e = jnp.exp(s - m)
    w = e / (jnp.sum(e, axis=-1, keepdims=True) + jnp.exp(sk - m))
    return jnp.einsum('bnhgqk,bnkhd->bnqhgd', w.astype(v.dtype), v)

def swa_prompt(q, k, v, sink):
    b, S = q.shape[:2]
    nc = S // CHUNK
    qc = q.reshape(b, nc, CHUNK, SWA_KV_HEADS, SWA_GROUP, HEAD_DIM)

    def band(a):
        ac = a.reshape(b, nc, CHUNK, SWA_KV_HEADS, HEAD_DIM)
        ap = jnp.pad(ac, ((0, 0), (WINDOW_CHUNKS, 0), (0, 0), (0, 0), (0, 0)))
        return jnp.concatenate([ap[:, j:j + nc] for j in range(WINDOW_CHUNKS + 1)], axis=2)

    key_chunk = jnp.arange(nc)[:, None] - WINDOW_CHUNKS + (jnp.arange((WINDOW_CHUNKS + 1) * CHUNK) // CHUNK)[None, :]
    o = sink_attend(qc, band(k), band(v), sink, key_chunk >= 0)
    return o.reshape(b, S, SWA_HEADS * HEAD_DIM)

def swa_sample(q, k, v, sink, ck, cv):
    b, S = q.shape[:2]
    rows = ck.shape[1]
    k_all = jnp.concatenate([ck.astype(k.dtype), k], axis=1)
    v_all = jnp.concatenate([cv.astype(v.dtype), v], axis=1)
    valid = jnp.ones((1, k_all.shape[1]), dtype=bool)
    o = sink_attend(q[:, None], k_all[:, None], v_all[:, None], sink, valid)
    return o.reshape(b, S, SWA_HEADS * HEAD_DIM), k_all[:, -rows:], v_all[:, -rows:]

def att_mixer(h, w_in, fox_fb, swa_sink, w_out, fox_cache, swa_cache):
    b, S, _ = h.shape
    qa, ka, va, fa, qb, kb, vb = split_cols(h @ w_in, ATT_SIZES)
    qa = qa.reshape(b, S, FOX_HEADS, HEAD_DIM)
    ka = ka.reshape(b, S, FOX_HEADS, HEAD_DIM)
    va = va.reshape(b, S, FOX_HEADS, HEAD_DIM)
    logf = jax.nn.log_sigmoid(fa.astype(jnp.float32) + fox_fb.astype(jnp.float32))
    qb = qb.reshape(b, S, SWA_KV_HEADS, SWA_GROUP, HEAD_DIM)
    kb = kb.reshape(b, S, SWA_KV_HEADS, HEAD_DIM)
    vb = vb.reshape(b, S, SWA_KV_HEADS, HEAD_DIM)
    sink = swa_sink.reshape(SWA_KV_HEADS, SWA_GROUP)
    if fox_cache is None:
        oa = fox_prompt(qa, ka, va, logf)
        ob = swa_prompt(qb, kb, vb, sink)
        rows = min(WINDOW, S)
        swa_state = (kb[:, S - rows:], vb[:, S - rows:])
    else:
        oa = fox_sample(qa, ka, va, logf, fox_cache[0], fox_cache[1], fox_cache[2])
        ob, sk, sv = swa_sample(qb, kb, vb, sink, swa_cache[0], swa_cache[1])
        swa_state = (sk, sv)
    out = jnp.concatenate([oa.reshape(b, S, FOX_HEADS * HEAD_DIM), ob], axis=-1) @ w_out
    return out, (ka, va, logf.astype(h.dtype)), swa_state

def mlstm_chunk(state, inp):
    C, n, m = state
    q, k, v, ig, lf = inp
    L = q.shape[1]
    bt = jnp.transpose(jnp.cumsum(lf, axis=1), (0, 2, 1))
    it = jnp.transpose(ig, (0, 2, 1))
    causal = jnp.tril(jnp.ones((L, L), dtype=bool))
    log_d = jnp.where(causal, bt[..., :, None] - bt[..., None, :] + it[..., None, :], NEG)
    log_s = bt + m[..., None]
    m_t = jnp.maximum(log_s, jnp.max(log_d, axis=-1))
    d = jnp.exp(log_d - m_t[..., None])
    s_dec = jnp.exp(log_s - m_t)
    w = jnp.einsum('blhk,bshk->bhls', q, k) * d
    num = jnp.einsum('bhls,bshv->blhv', w, v) + jnp.einsum('bhl,blhk,bhkv->blhv', s_dec, q, C)
    den = jnp.sum(w, axis=-1) + s_dec * jnp.einsum('blhk,bhk->bhl', q, n)
    den = jnp.maximum(jnp.abs(den), jnp.exp(-m_t))
    hh = num / jnp.transpose(den, (0, 2, 1))[..., None]
    m_new = m_t[..., -1]
    g = jnp.exp(bt[..., -1:] - bt + it - m_new[..., None])
    sc = jnp.exp(bt[..., -1] + m - m_new)
    C_new = sc[..., None, None] * C + jnp.einsum('bhs,bshk,bshv->bhkv', g, k, v)
    n_new = sc[..., None] * n + jnp.einsum('bhs,bshk->bhk', g, k)
    return (C_new, n_new, m_new), hh

def mlstm_mixer(h, w_in, ig_b, fg_b, norm_g, w_out, state):
    b, S, _ = h.shape
    f32 = jnp.float32
    q, k, v, ig, fg, og = split_cols(h @ w_in, REC_SIZES)
    q = q.reshape(b, S, ML_HEADS, ML_QK).astype(f32)
    k = k.reshape(b, S, ML_HEADS, ML_QK).astype(f32) * (ML_QK ** -0.5)
    v = v.reshape(b, S, ML_HEADS, ML_V).astype(f32)
    ig = ig.astype(f32) + ig_b.astype(f32)
    lf = jax.nn.log_sigmoid(fg.astype(f32) + fg_b.astype(f32))
    if state is None:
        nc = S // CHUNK

        def to_chunks(a):
            return jnp.swapaxes(a.reshape((b, nc, CHUNK) + a.shape[2:]), 0, 1)

        init = (jnp.zeros((b, ML_HEADS, ML_QK, ML_V), f32), jnp.zeros((b, ML_HEADS, ML_QK), f32), jnp.zeros((b, ML_HEADS), f32))
        new_state, hs = lax.scan(mlstm_chunk, init, (to_chunks(q), to_chunks(k), to_chunks(v), to_chunks(ig), to_chunks(lf)))
        hh = jnp.swapaxes(hs, 0, 1).reshape(b, S, ML_HEADS, ML_V)
    else:
        st = (state[0].astype(f32), state[1].astype(f32), state[2].astype(f32))
        new_state, hh = mlstm_chunk(st, (q, k, v, ig, lf))
    hh = rmsnorm(hh, norm_g.reshape(ML_HEADS, ML_V)).reshape(b, S, REC_OUT)
    out = (jax.nn.sigmoid(og.astype(f32)) * hh).astype(h.dtype) @ w_out
    return out, (new_state[0].astype(h.dtype), new_state[1].astype(h.dtype), new_state[2].astype(h.dtype))

def conv_ffn(h, w_up, conv_w, conv_b, w_down, conv_state):
    b, S, _ = h.shape
    g, u = jnp.split(h @ w_up, 2, axis=-1)
    hist = jnp.zeros((b, CONV_W - 1, D_FF), g.dtype) if conv_state is None else conv_state.astype(g.dtype)
    gp = jnp.concatenate([hist, g], axis=1)
    gc = conv_b
    for j in range(CONV_W):
        gc = gc + gp[:, j:j + S] * conv_w[j]
    y = (jax.nn.gelu(gc) * u) @ w_down
    return y, gp[:, S:]

def trunk(x, pe, prm, fox_cache, swa_cache, ml_state, conv_state):
    fox_new, swa_new, ml_new, conv_new = [], [], [], []
    for i in range(DEPTH):
        h = rmsnorm(x, prm['ln_mix_pre'][i])
        if i % 2 == 0:
            a = i // 2
            fc = None if fox_cache is None else (fox_cache[0][a], fox_cache[1][a], fox_cache[2][a])
            sc = None if swa_cache is None else (swa_cache[0][a], swa_cache[1][a])
            mix, fs, ss = att_mixer(h, prm['w_att_in'][a], prm['fox_fb'][a], prm['swa_sink'][a], prm['w_att_out'][a], fc, sc)
            fox_new.append(fs)
            swa_new.append(ss)
        else:
            r = i // 2
            st = None if ml_state is None else (ml_state[0][r], ml_state[1][r], ml_state[2][r])
            mix, ms = mlstm_mixer(h, prm['w_rec_in'][r], prm['rec_ig_b'][r], prm['rec_fg_b'][r], prm['rec_norm'][r], prm['w_rec_out'][r], st)
            ml_new.append(ms)
        x = x + rmsnorm(mix, prm['ln_mix_post'][i])
        cst = None if conv_state is None else conv_state[i]
        f, cs = conv_ffn(rmsnorm(x, prm['ln_ffn_pre'][i]), prm['w_ffn_up'][i], prm['ffn_conv_w'][i], prm['ffn_conv_b'][i], prm['w_ffn_down'][i], cst)
        conv_new.append(cs)
        x = x + rmsnorm(f, prm['ln_ffn_post'][i])
        x = x + jax.nn.sigmoid(x @ prm['w_ple_gate'][i]) * (pe[i] @ prm['w_ple'][i])

    def stack(states):
        return tuple(jnp.stack(list(parts)) for parts in zip(*states))

    return x, stack(fox_new), stack(swa_new), stack(ml_new), jnp.stack(conv_new)

def setup_inputs(seed: int = 0) -> dict:
    key = jax.random.key(seed)
    ks = iter(jax.random.split(key, 40))

    def nrm(shape, scale):
        return scale * jax.random.normal(next(ks), shape, jnp.float32)

    swa_rows = min(WINDOW, PAST_LEN)
    return {
        'x_prompt': nrm((BATCH, SEQ, D_MODEL), 1.0),
        'x_sample': nrm((DEC_BATCH, DEC_SEQ, D_MODEL), 1.0),
        'p_prompt': nrm((DEPTH, BATCH, SEQ, D_PLE), 1.0),
        'p_sample': nrm((DEPTH, DEC_BATCH, DEC_SEQ, D_PLE), 1.0),
        'cache_fox_k': nrm((N_ATT, DEC_BATCH, PAST_LEN, FOX_HEADS, HEAD_DIM), 1.0),
        'cache_fox_v': nrm((N_ATT, DEC_BATCH, PAST_LEN, FOX_HEADS, HEAD_DIM), 1.0),
        'cache_fox_logf': jax.nn.log_sigmoid(3.0 + nrm((N_ATT, DEC_BATCH, PAST_LEN, FOX_HEADS), 0.5)),
        'cache_swa_k': nrm((N_ATT, DEC_BATCH, swa_rows, SWA_KV_HEADS, HEAD_DIM), 1.0),
        'cache_swa_v': nrm((N_ATT, DEC_BATCH, swa_rows, SWA_KV_HEADS, HEAD_DIM), 1.0),
        'state_mlstm_c': nrm((N_REC, DEC_BATCH, ML_HEADS, ML_QK, ML_V), 0.1),
        'state_mlstm_n': nrm((N_REC, DEC_BATCH, ML_HEADS, ML_QK), 0.5),
        'state_mlstm_m': nrm((N_REC, DEC_BATCH, ML_HEADS), 1.0),
        'state_ffn_conv': nrm((DEPTH, DEC_BATCH, CONV_W - 1, D_FF), 1.0),
        'ln_mix_pre': 1.0 + nrm((DEPTH, D_MODEL), 0.02),
        'ln_mix_post': 1.0 + nrm((DEPTH, D_MODEL), 0.02),
        'ln_ffn_pre': 1.0 + nrm((DEPTH, D_MODEL), 0.02),
        'ln_ffn_post': 1.0 + nrm((DEPTH, D_MODEL), 0.02),
        'w_att_in': nrm((N_ATT, D_MODEL, ATT_IN), D_MODEL ** -0.5),
        'fox_fb': 2.0 + nrm((N_ATT, FOX_HEADS), 0.5),
        'swa_sink': nrm((N_ATT, SWA_HEADS), 0.5),
        'w_att_out': nrm((N_ATT, ATT_OUT, D_MODEL), ATT_OUT ** -0.5),
        'w_rec_in': nrm((N_REC, D_MODEL, REC_IN), D_MODEL ** -0.5),
        'rec_ig_b': nrm((N_REC, ML_HEADS), 0.1),
        'rec_fg_b': 3.0 + nrm((N_REC, ML_HEADS), 0.5),
        'rec_norm': 1.0 + nrm((N_REC, REC_OUT), 0.02),
        'w_rec_out': nrm((N_REC, REC_OUT, D_MODEL), REC_OUT ** -0.5),
        'w_ffn_up': nrm((DEPTH, D_MODEL, 2 * D_FF), D_MODEL ** -0.5),
        'ffn_conv_w': nrm((DEPTH, CONV_W, D_FF), CONV_W ** -0.5),
        'ffn_conv_b': nrm((DEPTH, D_FF), 0.02),
        'w_ffn_down': nrm((DEPTH, D_FF, D_MODEL), D_FF ** -0.5),
        'w_ple': nrm((DEPTH, D_PLE, D_MODEL), D_PLE ** -0.5),
        'w_ple_gate': nrm((DEPTH, D_MODEL, D_MODEL), D_MODEL ** -0.5),
    }

def reference(x_prompt, x_sample, p_prompt, p_sample, cache_fox_k, cache_fox_v, cache_fox_logf, cache_swa_k, cache_swa_v, state_mlstm_c, state_mlstm_n, state_mlstm_m, state_ffn_conv, ln_mix_pre, ln_mix_post, ln_ffn_pre, ln_ffn_post, w_att_in, fox_fb, swa_sink, w_att_out, w_rec_in, rec_ig_b, rec_fg_b, rec_norm, w_rec_out, w_ffn_up, ffn_conv_w, ffn_conv_b, w_ffn_down, w_ple, w_ple_gate):
    prm = {
        'ln_mix_pre': ln_mix_pre, 'ln_mix_post': ln_mix_post, 'ln_ffn_pre': ln_ffn_pre, 'ln_ffn_post': ln_ffn_post,
        'w_att_in': w_att_in, 'fox_fb': fox_fb, 'swa_sink': swa_sink, 'w_att_out': w_att_out,
        'w_rec_in': w_rec_in, 'rec_ig_b': rec_ig_b, 'rec_fg_b': rec_fg_b, 'rec_norm': rec_norm, 'w_rec_out': w_rec_out,
        'w_ffn_up': w_ffn_up, 'ffn_conv_w': ffn_conv_w, 'ffn_conv_b': ffn_conv_b, 'w_ffn_down': w_ffn_down,
        'w_ple': w_ple, 'w_ple_gate': w_ple_gate,
    }
    y_prompt, p_fox, p_swa, p_ml, p_conv = trunk(x_prompt, p_prompt, prm, None, None, None, None)
    y_sample, s_fox, s_swa, s_ml, s_conv = trunk(
        x_sample, p_sample, prm,
        (cache_fox_k, cache_fox_v, cache_fox_logf),
        (cache_swa_k, cache_swa_v),
        (state_mlstm_c, state_mlstm_n, state_mlstm_m),
        state_ffn_conv)
    return (y_prompt, y_sample,
            p_fox[0], p_fox[1], p_fox[2], p_swa[0], p_swa[1], p_ml[0], p_ml[1], p_ml[2], p_conv,
            s_fox[0], s_fox[1], s_fox[2], s_swa[0], s_swa[1], s_ml[0], s_ml[1], s_ml[2], s_conv)


_drawn_inputs = setup_inputs


def setup_inputs(seed=0):
    import zlib

    import numpy as np

    out = dict(_drawn_inputs(seed))
    spreads = {}
    factors = {'cache_fox_logf': 3.061, 'ln_ffn_post': 2.853, 'swa_sink': 8.0, 'rec_norm': 5.449}
    for name, (base, spread) in spreads.items():
        noise = np.random.default_rng([zlib.crc32(name.encode()), seed]).standard_normal(out[name].shape)
        drawn = base * np.exp(spread * noise) if base else spread * noise
        out[name] = jnp.asarray(drawn.astype(out[name].dtype))
    for name, factor in factors.items():
        out[name] = (out[name] * factor).astype(out[name].dtype)
    return out
```

```python
from contextlib import ExitStack

import concourse.bass as bass
from concourse import mybir

ACT = mybir.ActivationFunctionType
ALU = mybir.AluOpType
F32 = mybir.dt.float32
F32R = mybir.dt.float32r
X = mybir.AxisListType.X

P = 128
D = 1024
KT = D // P
TP, TS = 256, 64
T = TP + TS
CH = 64
FF = 4096
FT = FF // P
PAST = 256
HD = 64
NH = 8
MH, DK, DV = 4, 128, 256
EPS = 1e-6
NEG = -1e30
R = 4
LEAD = 3
TOK = [(0, 128), (128, 128), (256, 64)]

ATT_COLS = [P * j for j in range(12)] + [1544 + P * j for j in range(6)]
REC_COLS = [P * j for j in range(16)] + [2056 + P * j for j in range(8)]
UNITS, at = {}, 0
for l, n_in in ((0, len(ATT_COLS)), (1, len(REC_COLS))):
    for name, n in ((f"in{l}", n_in), (f"out{l}", 8), (f"up{l}", 2 * FT), (f"down{l}", FT), (f"ple{l}", 2), (f"gate{l}", 8)):
        UNITS[name] = at
        at += n
N_UNITS = at

GROUPS, GROUP_COUNT, at = {}, {}, 0
for name, n in (
    ("x", 8), ("par", 4), ("pe", 4), ("cache", 5),
    ("in0", 12), ("narrow0", 1), ("swin", 6), ("tok", 9), ("o", 8), ("out0", 8),
    ("up0", 64), ("cs0", 1), ("down0", 8), ("ple0", 8), ("gate0", 8),
    ("in1", 24), ("narrow1", 1), ("mtok", 9), ("inter0", 4), ("mo0", 4), ("inter1", 4), ("mo1", 4), ("inter2", 4), ("mo2", 4), ("out1", 8),
    ("up1", 64), ("cs1", 1), ("down1", 8), ("ple1", 8), ("gate1", 8), ("y", 6),
):
    GROUPS[name] = at
    GROUP_COUNT[name] = n
    at += n
N_GROUPS = at


NORMS = {f"{stage}{l}": 4 * l + i for l in range(2) for i, stage in enumerate(("mixpre", "mixpost", "ffnpre", "ffnpost"))}


def eights(stage, j):
    return 8 * (NORMS[stage] // 2) + j + 1


def attention_tasks():
    return [(fox, h, t) for fox in (True, False) for h in range(NH) for t in range(3)]


def encoder_step(nc, I, O):
    ctx = ExitStack()
    with ctx:
        def sb(name, shape, dt=F32):
            return ctx.enter_context(nc.sbuf_tensor(name, shape, dt))

        made = {}

        def sem(name):
            if name not in made:
                made[name] = ctx.enter_context(nc.semaphore(name))

            return made[name]

        ARENA = 2 * FT * T * 4
        arena = sb("arena", [P, ARENA // 4])
        nc_at = nc.alloc_sbuf_tensor_at
        base = nc.sbuf_base - ARENA
        FH = nc_at("hidden_hi", [P, FT, T], F32R, offset=base)
        FL = nc_at("hidden_lo", [P, FT, T], F32R, offset=base + FT * T * 4)
        scr0 = base + 8 * T * 4
        scr1 = base + FT * T * 4 + 24 * T * 4
        OH, OL = FH[:, 0:8, :], FL[:, 24:32, :]
        cursor = [scr0]

        def scratch(name, shape):
            n = 4
            for s in shape[1:]:
                n *= s
            a = cursor[0]
            cursor[0] += (n + 31) // 32 * 32
            assert cursor[0] <= scr1, (name, cursor[0] - scr1)
            return nc_at(name, shape, F32, offset=a)

        xtok = scratch("xtok", [P, 3, D])
        petok = scratch("petok", [P, 2, 3, 256])
        prow = scratch("prow", [P, 2, P])
        nrow = scratch("nrow", [P, 2, P])
        pef = scratch("pef", [P, 4, T])
        wnr = scratch("wnr", [P, 2, KT, 8])
        kcache = scratch("kcache", [P, 2, 512])
        startup_end = cursor[0]
        cursor[0] = scr0
        kT = scratch("kT", [P, 4, T])
        kdup = scratch("kdup", [P, 2, T])
        kplain = scratch("kplain", [P, T])
        kcT = scratch("kcT", [P, 4, PAST])
        kcdup = scratch("kcdup", [P, 2, P])
        Ktok = scratch("Ktok", [P, 3, 512])
        Vtok = scratch("Vtok", [P, 3, 512])
        Stok = scratch("Stok", [P, 3, 256])
        Frow = scratch("Frow", [NH, TP + PAST + TS])
        lfz = scratch("lfz", [NH, 3, T])
        lftok = scratch("lftok", [P, 3, NH])
        Ftok = scratch("Ftok", [P, 3, NH])
        S_sb = scratch("S_sb", [P, 2, T + 2])
        PT = scratch("PT", [P, 2, 384])
        amax = scratch("amax", [P, 2, 1])
        aden = scratch("aden", [P, 2, 1])
        ainv = scratch("ainv", [P, 2, 1])
        assert cursor[0] > startup_end
        MFox = scratch("MFox", [P, 384])
        MSwa = scratch("MSwa", [P, 256])
        vcache = scratch("vcache", [P, 2, 512])
        kcs = scratch("kcs", [P, P])
        vcs = scratch("vcs", [P, P])
        clf = scratch("clf", [P, 2, NH])
        sinkb = scratch("sinkb", [P, NH])
        cursor[0] = scr0
        sig = scratch("sig", [P, 8, T])
        Vaug = scratch("Vaug", [P, 3, MH, DV + 1])
        KmT = scratch("Ktok1", [P, 3, 512])
        Dm = scratch("Dm", [P, 3, MH, P])
        wT = scratch("wT", [P, 2, 512])
        C = scratch("C", [P, 2, MH, DV + 1])
        mz = scratch("mz", [8, 4, T])
        gt = scratch("gates_tok", [P, 3, 16])
        ml = {n: scratch("ml_" + n, [P, 3, MH]) for n in
              ("bt", "a", "M", "mp", "muL", "mu", "nmu", "sdec", "em", "g", "t0", "t1", "lf")}
        MF = scratch("MF", [P, 3, MH, 2])
        BL = scratch("BL", [P, 2, 12])
        mprev = scratch("mprev", [P, 6, MH])
        muc = scratch("muc", [P, 5, MH])
        scd = scratch("scd", [P, 5, MH])
        aT = scratch("aT", [12, P])
        Y = scratch("Y", [P, MH, DV + 1])
        yf = {n: scratch("y_" + n, [P, MH]) for n in ("den", "r", "ss", "v", "f")}
        Ysq = scratch("Ysq", [P, DV])

        xT = sb("xT", [P, KT, T])
        hH = sb("hH", [P, KT, T], F32R)
        hL = sb("hL", [P, KT, T], F32R)
        mix = sb("mix", [P, KT, T])
        sqb = sb("sqb", [P, KT, T])
        raw = sb("raw", [P, R, D])
        wh = sb("wh", [P, R, D], F32R)
        wl = sb("wl", [P, R, D], F32R)
        gp = sb("gp", [P, 2, T + 4])
        cv = sb("cv", [P, 2, T + 2])
        us = sb("us", [P, 2, T])
        fb = sb("fb", [P, 2, T])
        obuf = fb
        rstd = sb("rstd", [P, T])
        rstd2 = sb("rstd2", [P, T])
        PC = sb("PC", [P, 2, P])
        NC = sb("NC", [P, 2, P])
        cs = sb("cs", [P, 4, FT])
        csT = sb("csT", [P, P])
        peH = sb("peH", [P, 4, T], F32R)
        peL = sb("peL", [P, 4, T], F32R)
        wnH = sb("wnH", [P, 2, KT, 8], F32R)
        wnL = sb("wnL", [P, 2, KT, 8], F32R)
        ident = sb("ident", [P, P])
        ones = sb("ones", [P, P])
        Ut = sb("Ut", [P, P])
        Ub = sb("Ub", [P, P])
        MBlk = sb("MBlk", [P, P])
        cst = sb("cst", [P, 2])
        bcol = sb("bcol", [8, 4])
        sgb = us

        bank = [ctx.enter_context(nc.psum_tensor(f"bank{i}", [P, 512], F32)) for i in range(8)]

        raw_landed = [sem(f"raw_landed{i}") for i in range(R)]
        hi_ready, lo_ready, unit_used = sem("hi_ready"), sem("lo_ready"), sem("unit_used")
        bank_done = [sem(f"bank_done{i}") for i in range(4)]

        def gid(name, i=0):
            return GROUPS[name] + i

        def gbank(g):
            return bank[g % 4]

        READ = {}

        def read_by(name, signal, first=1, n=None):
            for i in range(n or GROUP_COUNT[name]):
                READ[gid(name, i)] = (signal, first + i)

        for name, signal in (("x", "x_in"), ("par", "par_in"), ("pe", "pe_f"), ("cache", "cache_read"), ("in0", "in_read0"),
                             ("narrow0", "narrow_step0"), ("tok", "tok_read"), ("o", "o_lo0"), ("in1", "in_read1"),
                             ("narrow1", "narrow_step1"), ("mtok", "mtok_read"), ("y", "ytok")):
            read_by(name, signal)
        read_by("swin", "in_read0", 13)
        for t in range(3):
            read_by(f"inter{t}", "Y", 4 * t + 1)
            read_by(f"mo{t}", "mo_f", 4 * t + 1)
        for l in range(2):
            for name, signal in (("cs", "csT"), ("ple", "ple_sb"), ("gate", "sigm")):
                read_by(f"{name}{l}", f"{signal}{l}")
            read_by(f"out{l}", "sq", 8 * NORMS[f"mixpost{l}"] + 1)
            read_by(f"down{l}", "sq", 8 * NORMS[f"ffnpost{l}"] + 1)
            for i in range(2 * FT):
                READ[gid(f"up{l}", i)] = (("us" if i % 2 else "gp") + str(l), i // 2 + 1)

        FULL, uses = {}, [0] * 4
        for l in range(2):
            for i in range(len(ATT_COLS) if l == 0 else len(REC_COLS)):
                FULL[gid(f"in{l}", i) if l or i < 12 else gid("swin", i - 12)] = (unit_used, UNITS[f"in{l}"] + i + 1)
            for i in range(8):
                FULL[gid(f"out{l}", i)] = (unit_used, UNITS[f"out{l}"] + i + 1)
                FULL[gid(f"down{l}", i)] = (unit_used, UNITS[f"down{l}"] + 4 * i + 4)
                FULL[gid(f"gate{l}", i)] = (unit_used, UNITS[f"gate{l}"] + i + 1)
            for i in range(2 * FT):
                FULL[gid(f"up{l}", i)] = (unit_used, UNITS[f"up{l}"] + i + 1)
            for i in (3, 7):
                FULL[gid(f"ple{l}", i)] = (unit_used, UNITS[f"ple{l}"] + i // 4 + 1)
        for i in range(8):
            FULL[gid("o", i)] = (sem("pv_done"), 6 * (i + 1))
        for gi in range(N_GROUPS):
            if gi not in FULL:
                uses[gi % 4] += 1
                FULL[gi] = (bank_done[gi % 4], uses[gi % 4])

        def bank_free(eng, g):
            if g >= 4:
                name, value = READ[g - 4]
                eng.wait_ge(sem(name), value)

        def bank_full(eng, g, it=0):
            signal, value = FULL[g]
            eng.wait_ge(signal, value + it)

        TASKS = attention_tasks()
        OUT_DMAS = []

        def score_width(i):
            fox, h, t = TASKS[i]
            return TOK[t][0] + P if fox and t < 2 else PAST + TS if fox else TOK[t][0] + P + 1 if t < 2 else P + TS + 1

        def attention_pe(pe):
            mmul = nc.tensor.matmul
            trans = nc.tensor.transpose
            pe.wait_ge(sem("const2"), 1)
            pe.wait_ge(sem("lf_ready"), 1)
            for t, (t0, n) in enumerate(TOK):
                m = trans(bank[5][0:n, t * 8:t * 8 + 8], lfz[:, 0, t0:t0 + n], ident[0:8, 0:8])
            m.then_inc(sem("lf_tr"), 1)
            pe.wait_ge(sem("lf_tok"), 1)
            L = [lftok[:, 0, :], lftok[:, 1, :], lftok[0:64, 2, :]]
            Cc = [clf[:, 0, :], clf[:, 1, :]]

            def run_sum(out, terms):
                for i, (a, b) in enumerate(terms):
                    m = mmul(out, a, b, start=i == 0, stop=i == len(terms) - 1)
                return m

            U, N1 = Ut[:], ones[:]
            run_sum(bank[6][:, 0:8], [(U, L[0])])
            run_sum(bank[6][:, 8:16], [(N1, L[0]), (U, L[1])])
            run_sum(bank[6][0:64, 16:24], [(N1[:, 0:64], Cc[0]), (N1[:, 0:64], Cc[1]), (Ut[0:64, 0:64], L[2])])
            run_sum(bank[7][0:8, 0:128], [(L[0], U)])
            run_sum(bank[7][0:8, 128:256], [(L[0], N1), (L[1], U)])
            run_sum(bank[5][0:8, 0:128], [(Cc[0], U)])
            run_sum(bank[5][0:8, 128:256], [(Cc[0], N1), (Cc[1], U)])
            run_sum(bank[5][0:8, 256:320], [(Cc[0], N1[:, 0:64]), (Cc[1], N1[:, 0:64]), (L[2], Ut[0:64, 0:64])]).then_inc(sem("F_sums"), 1)
            pe.wait_ge(sem("in_read0"), 18)
            for kind in range(3):
                for t, (t0, n) in enumerate(TOK):
                    gi = gid("tok", 3 * kind + t)
                    bank_free(pe, gi)
                    srcs = [kT[:, j, t0:t0 + n] for j in range(4)] if kind == 0 else \
                        [sqb[:, j, t0:t0 + n] for j in range(4)] if kind == 1 else [kplain[:, t0:t0 + n], sqb[:, 4, t0:t0 + n]]
                    for j, s in enumerate(srcs):
                        m = trans(gbank(gi)[0:n, j * P:(j + 1) * P], s, ident[:])
                    m.then_inc(bank_done[gi % 4], 1)
            pe.wait_ge(sem("F_rows"), 1)
            pe.wait_ge(sem("tok_read"), 9)

            def scores(i):
                fox, h, t = TASKS[i]
                t0, n = TOK[t]
                hf = 64 * (h % 2)
                if i >= 2:
                    pe.wait_ge(sem("s_moved"), i - 1)
                b = bank[4 + i % 2]
                q = mix[hf:hf + 64, (0 if fox else 4) + h // 2, t0:t0 + n]
                segs = []
                if fox and t < 2:
                    segs = [(kT[hf:hf + 64, h // 2, 0:t0 + n], 0, 0)]
                elif fox:
                    segs = [(kcT[hf:hf + 64, h // 2, :], 0, TP), (kT[hf:hf + 64, h // 2, TP:T], PAST, TP + PAST)]
                elif t < 2:
                    segs = [(kdup[hf:hf + 64, h // 4, 0:t0 + n], 0, None)]
                else:
                    segs = [(kcdup[hf:hf + 64, h // 4, :], 0, None), (kdup[hf:hf + 64, h // 4, TP:T], P, None)]
                for k, off, fr in segs:
                    w = k.shape[1]
                    m = mmul(b[0:n, off:off + w], q, k, start=True, stop=fr is None)
                    if fr is not None:
                        m = mmul(b[0:n, off:off + w], ident[0:8, h:h + 1].to_broadcast([8, n]), Frow[:, fr:fr + w], start=False, stop=True)
                m.then_inc(sem("s_done"), 1)

            def blocks(i):
                fox, h, t = TASKS[i]
                c = h * 64 if fox else (h // 4) * 64
                V = Vtok if fox else Stok[:, :, P:2 * P]
                if t < 2:
                    return [(P, V[:, b, c:c + 64]) for b in range(t + 1)]
                if fox:
                    return [(P, vcache[:, b, c:c + 64]) for b in range(2)] + [(64, V[0:64, 2, c:c + 64])]
                return [(P, vcs[:, c:c + 64]), (64, V[0:64, 2, c:c + 64])]

            def transposes(i):
                n = TOK[TASKS[i][2]][1]
                pe.wait_ge(sem("p_ready"), i + 1)
                if i >= 2:
                    pe.wait_ge(sem("pt_moved"), i - 1)
                for b, (rows, _) in enumerate(blocks(i)):
                    m = trans(bank[6 + i % 2][0:rows, b * P:b * P + n], S_sb[0:n, i % 2, b * P:b * P + rows], ident[0:n, 0:n])
                m.then_inc(sem("pt_done"), 1)

            def values(i):
                fox, h, t = TASKS[i]
                t0, n = TOK[t]
                gi = gid("o", i // 6)
                if i % 6 == 0:
                    bank_free(pe, gi)
                pe.wait_ge(sem("pt_moved"), i + 1)
                hf = 64 * (h % 2)
                bl = blocks(i)
                for b, (rows, v) in enumerate(bl):
                    m = mmul(gbank(gi)[hf:hf + 64, t0:t0 + n], v, PT[0:rows, i % 2, b * P:b * P + n], start=b == 0, stop=b == len(bl) - 1)
                m.then_inc(sem("pv_done"), 1)

            n_t = len(TASKS)
            for i in range(n_t + 2):
                if i < n_t:
                    scores(i)
                if 1 <= i <= n_t:
                    transposes(i - 1)
                if i >= 2:
                    values(i - 2)

        def mlstm_pe(pe):
            mmul = nc.tensor.matmul
            trans = nc.tensor.transpose
            pe.wait_ge(sem("mgates"), 1)
            for t, (t0, n) in enumerate(TOK):
                trans(bank[5][0:n, t * 16:t * 16 + 8], mz[:, 0, t0:t0 + n], ident[0:8, 0:8])
                m = trans(bank[5][0:n, t * 16 + 8:t * 16 + 16], mz[:, 1, t0:t0 + n], ident[0:8, 0:8])
            m.then_inc(sem("mgates_tr"), 1)
            pe.wait_ge(sem("mlf"), 1)
            lf = ml["lf"][:].rearrange("p t h -> p (t h)")
            mmul(bank[6][:, 0:12], Ub[:], lf, start=True, stop=True)
            mmul(bank[6][:, 16:28], ones[0:64, :], lf[0:64, :], start=True, stop=True)
            mmul(bank[7][:, 32:44], ones[64:128, :], lf[64:128, :], start=True, stop=True).then_inc(sem("msums"), 1)
            for kind in range(3):
                for t, (t0, n) in enumerate(TOK):
                    gi = gid("mtok", 3 * kind + t)
                    bank_free(pe, gi)
                    for j in range(4):
                        s = mix[:, 4 + j, t0:t0 + n] if kind == 0 else sqb[:, 4 * (kind - 1) + j, t0:t0 + n]
                        m = trans(gbank(gi)[0:n, j * P:(j + 1) * P], s, ident[:])
                    m.then_inc(bank_done[gi % 4], 1)
            pe.wait_ge(sem("ma"), 1)
            trans(bank[7][0:12, 0:P], ml["a"][:].rearrange("p t h -> p (t h)"), ident[:]).then_inc(sem("maT"), 1)
            pe.wait_ge(sem("maT_read"), 1)
            for t in range(3):
                b = bank[5 + t]
                for h in range(MH):
                    r = 4 * t + h
                    m = mmul(b[:, h * P:(h + 1) * P], ident[0:12, r:r + 1].to_broadcast([12, P]), aT[:], start=True, stop=True)
                m.then_inc(sem("mspread"), 1)
            for t, (t0, n) in enumerate(TOK):
                pe.wait_ge(sem("mD_raw"), t + 1)
                if t:
                    pe.wait_ge(sem("mw"), t)
                for h in range(MH):
                    m = mmul(bank[4][0:n, h * P:h * P + n], mix[:, h, t0:t0 + n], mix[:, 4 + h, t0:t0 + n], start=True, stop=True)
                m.then_inc(sem("mqk"), 1)
                for half in range(2 if t < 2 else 1):
                    r0 = 64 * half
                    s = 0 if t < 2 else 1
                    c = 2 * t + half
                    for h in range(MH):
                        gi = gid(f"inter{t}", h)
                        if half == 0:
                            bank_free(pe, gi)
                        if c == 0 or c == 4:
                            pe.wait_ge(sem("C_init"), 1)
                        else:
                            pe.wait_ge(sem("C_new"), 4 * c - 4 + h + 1)
                        m = mmul(gbank(gi)[r0:r0 + 64, 0:DV + 1], mix[:, h, t0 + r0:t0 + r0 + 64], C[:, s, h, :], start=True, stop=True)
                        if half == 1 or t == 2:
                            m.then_inc(bank_done[gi % 4], 1)
                        else:
                            m.then_inc(sem("inter_half"), 1)
                        k = 4 * c + h
                        pe.wait_ge(sem("Kg"), 4 * t + h + 1)
                        if k >= 2:
                            pe.wait_ge(sem("C_new"), k - 1)
                        if k < 2:
                            pe.wait_ge(sem("mD_raw"), 3)
                        mmul(bank[6 + k % 2][:, 0:DV + 1], KmT[r0:r0 + 64, t, h * P:(h + 1) * P], Vaug[r0:r0 + 64, t, h, :],
                             start=True, stop=True).then_inc(sem("C_add"), 1)
                pe.wait_ge(sem("mw"), t + 1)
                for h in range(MH):
                    m = trans(bank[4][0:n, h * P:h * P + n], Dm[0:n, t, h, 0:n], ident[0:n, 0:n])
                m.then_inc(sem("mwT"), 1)
                pe.wait_ge(sem("mwT_read"), t + 1)
                for h in range(MH):
                    k = 4 * t + h
                    if k >= 1:
                        pe.wait_ge(sem("intra_read"), k)
                    if k == 0:
                        pe.wait_ge(sem("mD_raw"), 1)
                    mmul(bank[5][0:n, 0:DV + 1], wT[0:n, t % 2, h * P:h * P + n], Vaug[0:n, t, h, :], start=True, stop=True).then_inc(sem("intra"), 1)
                for h in range(MH):
                    gi = gid(f"mo{t}", h)
                    bank_free(pe, gi)
                    pe.wait_ge(sem("Yn"), 4 * t + h + 1)
                    for v in range(2):
                        m = trans(gbank(gi)[:, v * P:v * P + n], Y[0:n, h, v * P:(v + 1) * P], ident[0:n, 0:n])
                    m.then_inc(bank_done[gi % 4], 1)

        def attention_act(act):
            A = nc.scalar.activation
            act.wait_ge(sem("lf_abs"), 1)
            A(lfz[:, 1, :], lfz[:, 1, :], ACT.Exp, scale=-1.0).then_inc(sem("lf_exp"), 1)
            act.wait_ge(sem("lf_exp"), 1)
            A(lfz[:, 1, :], lfz[:, 1, :], ACT.Ln, bias=cst[0:8, 1:2]).then_inc(sem("lf_ln"), 1)
            for i in range(9):
                kind, t = i // 3, i % 3
                gi = gid("tok", i)
                n = TOK[t][1]
                bank_full(act, gi)
                dst = (Ktok, Vtok, Stok)[kind]
                w = 512 if kind < 2 else 256
                A(dst[0:n, t, :], gbank(gi)[0:n, 0:w], ACT.Copy).then_inc(sem("tok_read"), 1)
            n_t = len(TASKS)

            def pt_copy(i):
                fox, h, t = TASKS[i]
                n = TOK[t][1]
                act.wait_ge(sem("pt_done"), i + 1)
                if i >= 2:
                    act.wait_ge(sem("pv_done"), i - 1)
                full = (t + 1) if t < 2 else (2 if fox else 1)
                last = None
                if n == P:
                    last = A(PT[:, i % 2, 0:full * P], bank[6 + i % 2][:, 0:full * P], ACT.Copy)
                else:
                    src = bank[6 + i % 2][:, 0:full * P].rearrange("p (b c) -> p b c", c=P)[:, :, 0:n]
                    dst = PT[:, i % 2, 0:full * P].rearrange("p (b c) -> p b c", c=P)[:, :, 0:n]
                    A(dst, src, ACT.Copy)
                    last = A(PT[0:64, i % 2, full * P:full * P + n], bank[6 + i % 2][0:64, full * P:full * P + n], ACT.Copy)
                last.then_inc(sem("pt_moved"), 1)

            def o_hi(j):
                gi = gid("o", j)
                bank_full(act, gi)
                A(OH[:, j, :], gbank(gi)[:, 0:T], ACT.Copy).then_inc(sem("o_hi0"), 1)

            for i in range(n_t + 1):
                if i < n_t:
                    fox, h, t = TASKS[i]
                    n = TOK[t][1]
                    w = score_width(i)
                    act.wait_ge(sem("s_max"), i + 1)
                    A(S_sb[0:n, i % 2, 0:w], S_sb[0:n, i % 2, 0:w], ACT.Exp, bias=amax[0:n, i % 2, :],
                      accum_out=aden[0:n, i % 2, :]).then_inc(sem("s_exp"), 1)
                if i >= 1:
                    pt_copy(i - 1)
                if i >= 8 and (i - 2) % 6 == 0:
                    o_hi((i - 8) // 6)
            o_hi(7)

        def mlstm_act(act):
            A = nc.scalar.activation
            act.wait_ge(sem("mlf_abs"), 1)
            A(mz[:, 2, :], mz[:, 2, :], ACT.Exp, scale=-1.0).then_inc(sem("mlf_exp"), 1)
            act.wait_ge(sem("mlf_exp"), 1)
            A(mz[:, 2, :], mz[:, 2, :], ACT.Ln, bias=cst[0:8, 1:2]).then_inc(sem("mlf_ln"), 1)
            for i in range(9):
                kind, t = i // 3, i % 3
                gi = gid("mtok", i)
                n = TOK[t][1]
                bank_full(act, gi)
                if kind == 0:
                    ins = A(KmT[0:n, t, :], gbank(gi)[0:n, :], ACT.Copy)
                else:
                    h0 = 2 * (kind - 1)
                    ins = A(Vaug[0:n, t, h0:h0 + 2, 0:DV], gbank(gi)[0:n, :].rearrange("p (h v) -> p h v", h=2), ACT.Copy)
                ins.then_inc(sem("mtok_read"), 1)
            act.wait_ge(sem("mexp_in"), 1)
            fl = {n: ml[n][:].rearrange("p t h -> p (t h)") for n in ml}
            for n in ("sdec", "em", "g"):
                A(fl[n], fl[n], ACT.Exp)
            A(scd[:].rearrange("p c h -> p (c h)"), scd[:].rearrange("p c h -> p (c h)"), ACT.Exp).then_inc(sem("mexp"), 1)
            for t in range(3):
                n = TOK[t][1]
                for h in range(MH):
                    ins = A(Dm[0:n, t, h, 0:n], Dm[0:n, t, h, 0:n], ACT.Exp, bias=ml["nmu"][0:n, t, h:h + 1])
                ins.then_inc(sem("mD"), 1)
            for t in range(3):
                n = TOK[t][1]
                act.wait_ge(sem("mwT"), t + 1)
                src = bank[4][0:n, :].rearrange("p (h c) -> p h c", h=MH)[:, :, 0:n]
                dst = wT[0:n, t % 2, :].rearrange("p (h c) -> p h c", h=MH)[:, :, 0:n]
                A(dst, src, ACT.Copy).then_inc(sem("mwT_read"), 1)
                for h in range(MH):
                    act.wait_ge(sem("intra"), 4 * t + h + 1)
                    if t and h == 0:
                        bank_full(act, gid(f"mo{t - 1}", 3))
                    A(Y[0:n, h, :], bank[5][0:n, 0:DV + 1], ACT.Copy).then_inc(sem("intra_read"), 1)
                for h in range(MH):
                    act.wait_ge(sem("Y"), 4 * t + h + 1)
                    if 4 * t + h:
                        act.wait_ge(sem("Yss"), 4 * t + h)
                    A(Ysq[0:n, :], Y[0:n, h, 0:DV], ACT.Square, accum_out=yf["ss"][0:n, h:h + 1]).then_inc(sem("Yss"), 1)
                act.wait_ge(sem("Yvar"), t + 1)
                A(yf["v"][0:n, :], yf["v"][0:n, :], ACT.Sqrt, bias=cst[0:n, 0:1]).then_inc(sem("Yroot"), 1)
                for h in range(MH):
                    k = 4 * t + h
                    act.wait_ge(sem("mo_f"), k + 1)
                    t0 = TOK[t][0]
                    A(OH[:, 2 * h:2 * h + 2, t0:t0 + n], obuf[:, k % 2, 0:2 * n].rearrange("p (v c) -> p v c", v=2), ACT.Copy).then_inc(sem("o_hi1"), 1)

        def attention_dve(dve):
            V = nc.vector
            dve.wait_ge(sem("lf_ln"), 1)
            dve.wait_ge(sem("narrow_step0"), 3)
            V.tensor_tensor(lfz[:, 0, :], lfz[:, 2, :], lfz[:, 1, :], ALU.subtract).then_inc(sem("lf_ready"), 1)
            dve.wait_ge(sem("lf_tr"), 1)
            V.tensor_copy(lftok[:, 0:2, :], bank[5][:, 0:16].rearrange("p (t h) -> p t h", t=2))
            V.tensor_copy(lftok[0:64, 2, :], bank[5][0:64, 16:24]).then_inc(sem("lf_tok"), 1)
            dve.wait_ge(sem("F_sums"), 1)
            V.tensor_copy(Ftok[:, 0:2, :], bank[6][:, 0:16].rearrange("p (t h) -> p t h", t=2))
            V.tensor_copy(Ftok[0:64, 2, :], bank[6][0:64, 16:24])
            V.tensor_scalar(Frow[:, 0:256], bank[7][0:8, 0:256], -1.0, None, ALU.mult)
            V.tensor_scalar(Frow[:, 256:576], bank[5][0:8, 0:320], -1.0, None, ALU.mult).then_inc(sem("F_rows"), 1)
            dve.wait_ge(sem("F_rows"), 1)
            dve.wait_ge(sem("const2"), 1)
            n_t = len(TASKS)
            st = sem("s_step")
            ns = [0]

            def link(ins):
                ns[0] += 1
                ins.then_inc(st, 1)
                dve.wait_ge(st, ns[0])

            def o_lo(j):
                gi = gid("o", j)
                dve.wait_ge(sem("o_hi0"), j + 1)
                V.tensor_tensor(OL[:, j, :], gbank(gi)[:, 0:T], OH[:, j, :].bitcast(F32), ALU.subtract).then_inc(sem("o_lo0"), 1)

            for i in range(n_t + 1):
                if i < n_t:
                    fox, h, t = TASKS[i]
                    n = TOK[t][1]
                    b = i % 2
                    w = score_width(i)
                    dve.wait_ge(sem("s_done"), i + 1)
                    if i >= 2:
                        dve.wait_ge(sem("pt_done"), i - 1)
                    src = bank[4 + b]
                    if fox:
                        m = MFox[0:n, 384 - w:384] if t < 2 else MFox[0:n, 0:w]
                        V.scalar_tensor_tensor(out=S_sb[0:n, b, 0:w], in0=src[0:n, 0:w], scalar=Ftok[0:n, t, h:h + 1], in1=m,
                                               op0=ALU.add, op1=ALU.add).then_inc(sem("s_moved"), 1)
                    else:
                        V.tensor_copy(S_sb[0:n, b, w - 1:w], sinkb[0:n, h:h + 1])
                        if t < 2:
                            V.tensor_tensor(S_sb[0:n, b, 0:w - 1], src[0:n, 0:w - 1], MSwa[0:n, 256 - (w - 1):256], ALU.add).then_inc(sem("s_moved"), 1)
                        else:
                            V.tensor_copy(S_sb[0:n, b, 0:w - 1], src[0:n, 0:w - 1]).then_inc(sem("s_moved"), 1)
                    dve.wait_ge(sem("s_moved"), i + 1)
                    V.tensor_reduce(amax[0:n, b, :], S_sb[0:n, b, 0:w], X, ALU.max, negate=True).then_inc(sem("s_max"), 1)
                if i >= 1:
                    k = i - 1
                    b = k % 2
                    n = TOK[TASKS[k][2]][1]
                    w = score_width(k)
                    dve.wait_ge(sem("s_exp"), k + 1)
                    link(V.reciprocal(ainv[0:n, b, :], aden[0:n, b, :]))
                    V.tensor_scalar(S_sb[0:n, b, 0:w], S_sb[0:n, b, 0:w], ainv[0:n, b, :], None, ALU.mult).then_inc(sem("p_ready"), 1)
                if i >= 8 and (i - 2) % 6 == 0:
                    o_lo((i - 8) // 6)
            o_lo(7)

        def mlstm_dve(dve):
            V = nc.vector
            st = sem("m_step")
            ns = [0]

            def link(ins):
                ns[0] += 1
                ins.then_inc(st, 1)
                dve.wait_ge(st, ns[0])
                return ins

            fl = {n: ml[n][:].rearrange("p t h -> p (t h)") for n in ml}
            dve.wait_ge(sem("mlf_ln"), 1)
            dve.wait_ge(sem("narrow_step1"), 3)
            V.tensor_tensor(mz[:, 1, :], mz[:, 1, :], mz[:, 2, :], ALU.subtract).then_inc(sem("mgates"), 1)
            link(V.memset(gt[:], 0.0))
            V.memset(C[:, 0], 0.0)
            V.memset(mprev[:, 0, :], 0.0)
            link(V.memset(Vaug[:, :, :, DV:DV + 1], 1.0))
            dve.wait_ge(sem("ld_state"), 48)
            dve.sem_inc(sem("C_init"), 1)
            dve.wait_ge(sem("mgates_tr"), 1)
            V.tensor_copy(gt[:, 0:2, :], bank[5][:, 0:32].rearrange("p (t c) -> p t c", t=2))
            link(V.tensor_copy(gt[0:64, 2, :], bank[5][0:64, 32:48]))
            V.tensor_copy(ml["lf"][:], gt[:, :, 12:16]).then_inc(sem("mlf"), 1)
            dve.wait_ge(sem("msums"), 1)
            V.tensor_copy(fl["bt"], bank[6][:, 0:12])
            V.tensor_copy(BL[:, 0, :], bank[6][:, 16:28])
            link(V.tensor_copy(BL[:, 1, :], bank[7][:, 32:44]))
            V.tensor_tensor(ml["a"][:], gt[:, :, 0:4], ml["bt"][:], ALU.subtract).then_inc(sem("ma"), 1)
            dve.wait_ge(sem("maT"), 1)
            V.tensor_copy(aT[:], bank[7][0:12, 0:P]).then_inc(sem("maT_read"), 1)
            for t in range(3):
                dve.wait_ge(sem("mspread"), t + 1)
                b = bank[5 + t][:, :].rearrange("p (h s) -> p h s", h=MH)
                V.tensor_reduce(MF[:, t, :, :], bank[5 + t][:, :].rearrange("p (h c s) -> p h c s", h=MH, c=2), X, ALU.max)
                for h in range(MH):
                    ins = V.tensor_tensor(Dm[:, t, h, :], b[:, h, :], MBlk[:], ALU.add)
                link(ins)
                dve.wait_ge(st, ns[0])
                V.tensor_reduce(ml["M"][:, t, :], Dm[:, t], X, ALU.max).then_inc(sem("mD_raw"), 1)
            dve.wait_ge(sem("mD_raw"), 3)
            for c in range(5):
                t, half = c // 2, c % 2
                link(V.tensor_tensor(muc[:, c, :], mprev[:, c, :], MF[:, t, :, half], ALU.max))
                dst = mprev[:, c + 1, :] if c < 3 else mprev[:, 5, :] if c == 3 else mz[:, 3, 0:4]
                if c < 4:
                    link(V.tensor_tensor(dst, muc[:, c, :], BL[:, half, 4 * t:4 * t + 4], ALU.add))
                else:
                    link(V.tensor_tensor(dst, muc[0:8, c, :], BL[0:8, half, 4 * t:4 * t + 4], ALU.add))
            for t in range(3):
                for half in range(2):
                    c = min(2 * t + half, 4)
                    r = slice(64 * half, 64 * half + 64)
                    V.tensor_copy(ml["mp"][r, t, :], mprev[r, c, :])
                    ins = V.tensor_copy(ml["muL"][r, t, :], muc[r, c, :])
            link(ins)
            link(V.tensor_tensor(fl["mu"], fl["mp"], fl["M"], ALU.max))
            V.tensor_scalar(fl["nmu"], fl["mu"], -1.0, None, ALU.mult)
            V.tensor_tensor(fl["sdec"], fl["mp"], fl["mu"], ALU.subtract)
            link(V.tensor_tensor(fl["t0"], fl["bt"], fl["mu"], ALU.add))
            V.tensor_scalar(fl["em"], fl["t0"], -1.0, None, ALU.mult)
            V.tensor_tensor(fl["g"], fl["a"], fl["muL"], ALU.subtract)
            V.tensor_tensor(scd[:], mprev[:, 0:5, :], muc[:], ALU.subtract).then_inc(sem("mexp_in"), 1)
            dve.wait_ge(sem("mexp"), 1)
            dve.wait_ge(sem("mtok_read"), 9)
            for t in range(3):
                n = TOK[t][1]
                for h in range(MH):
                    k = KmT[0:n, t, h * P:(h + 1) * P]
                    V.tensor_scalar(k, k, ml["g"][0:n, t, h:h + 1], None, ALU.mult).then_inc(sem("Kg"), 1)
            for t, (t0, n) in enumerate(TOK):
                dve.wait_ge(sem("mD"), t + 1)
                dve.wait_ge(sem("mqk"), t + 1)
                src = bank[4][0:n, :].rearrange("p (h c) -> p h c", h=MH)[:, :, 0:n]
                V.tensor_tensor(Dm[0:n, t, :, 0:n], src, Dm[0:n, t, :, 0:n], ALU.mult).then_inc(sem("mw"), 1)
                s = 0 if t < 2 else 1
                for half in range(2 if t < 2 else 1):
                    c = 2 * t + half
                    for h in range(MH):
                        k = 4 * c + h
                        dve.wait_ge(sem("C_add"), k + 1)
                        V.scalar_tensor_tensor(out=C[:, s, h, :], in0=C[:, s, h, :], scalar=scd[:, c, h:h + 1],
                                               in1=bank[6 + k % 2][:, 0:DV + 1], op0=ALU.mult, op1=ALU.add).then_inc(sem("C_new"), 1)
                for h in range(MH):
                    gi = gid(f"inter{t}", h)
                    bank_full(dve, gi)
                    dve.wait_ge(sem("intra_read"), 4 * t + h + 1)
                    V.scalar_tensor_tensor(out=Y[0:n, h, :], in0=gbank(gi)[0:n, 0:DV + 1], scalar=ml["sdec"][0:n, t, h:h + 1],
                                           in1=Y[0:n, h, :], op0=ALU.mult, op1=ALU.add).then_inc(sem("Y"), 1)
                dve.wait_ge(sem("Y"), 4 * t + 4)
                den = yf["den"][0:n, :]
                link(V.scalar_tensor_tensor(out=den, in0=Y[0:n, :, DV], scalar=-1.0, in1=Y[0:n, :, DV], op0=ALU.mult, op1=ALU.max))
                link(V.tensor_tensor(den, den, ml["em"][0:n, t, :], ALU.max))
                r = yf["r"][0:n, :]
                link(V.reciprocal(r, den))
                v = yf["v"][0:n, :]
                link(V.tensor_tensor(v, r, r, ALU.mult))
                dve.wait_ge(sem("Yss"), 4 * t + 4)
                link(V.tensor_tensor(v, v, yf["ss"][0:n, :], ALU.mult))
                V.tensor_scalar(v, v, 1.0 / DV, None, ALU.mult).then_inc(sem("Yvar"), 1)
                dve.wait_ge(sem("Yroot"), t + 1)
                f = yf["f"][0:n, :]
                link(V.reciprocal(f, v))
                link(V.tensor_tensor(f, f, r, ALU.mult))
                for h in range(MH):
                    V.tensor_scalar(Y[0:n, h, 0:DV], Y[0:n, h, 0:DV], yf["f"][0:n, h:h + 1], None, ALU.mult).then_inc(sem("Yn"), 1)
                if t == 0:
                    dve.wait_ge(sem("og"), 8)
                for h in range(MH):
                    k = 4 * t + h
                    gi = gid(f"mo{t}", h)
                    bank_full(dve, gi)
                    for vt in range(2):
                        j = 2 * h + vt
                        o = obuf[:, k % 2, vt * n:vt * n + n]
                        ins = V.scalar_tensor_tensor(out=o, in0=gbank(gi)[:, vt * P:vt * P + n], scalar=NC[:, 1, 96 + j:97 + j],
                                                     in1=sig[:, j, t0:t0 + n], op0=ALU.mult, op1=ALU.mult)
                    ins.then_inc(sem("mo_f"), 1)
                    dve.wait_ge(sem("o_hi1"), k + 1)
                    V.tensor_tensor(OL[:, 2 * h:2 * h + 2, t0:t0 + n], obuf[:, k % 2, 0:2 * n].rearrange("p (v c) -> p v c", v=2),
                                    OH[:, 2 * h:2 * h + 2, t0:t0 + n].bitcast(F32), ALU.subtract).then_inc(sem("o_lo1"), 1)

        block = ctx.enter_context(nc.Block())

        @block.sync
        def _(sp):
            def col_unit(w, c):
                return w[:, c:c + P].rearrange("(k p) c -> p k c", p=P)

            def load(u, src, shape=None):
                if u >= R:
                    sp.wait_ge(lo_ready, u - R + 1)
                dst = raw[:, u % R, :].rearrange("p (k c) -> p k c", k=src.shape[1])
                sp.dma_start(dst, src).then_inc(raw_landed[u % R], 16)

            for l in range(2):
                w_in, cols, w_out = (I["w_att_in"], ATT_COLS, I["w_att_out"]) if l == 0 else (I["w_rec_in"], REC_COLS, I["w_rec_out"])
                for i, c in enumerate(cols):
                    load(UNITS[f"in{l}"] + i, col_unit(w_in[0], c))
                for i in range(8):
                    load(UNITS[f"out{l}"] + i, col_unit(w_out[0], i * P))
                u0 = UNITS[f"up{l}"]
                with sp.Fori(0, FT // 2) as it:
                    for s in range(4):
                        u = u0 + s
                        sp.wait_ge(lo_ready, u - R + 1 + it * 4)
                        c = it * (2 * P) + (s // 2) * P + (s % 2) * FF
                        src = I["w_ffn_up"][l][:, bass.ds(c, P)].rearrange("(k p) c -> p k c", p=P)
                        dst = raw[:, u % R, :].rearrange("p (k c) -> p k c", k=KT)
                        sp.dma_start(dst, src).then_inc(raw_landed[u % R], 16)
                u0 = UNITS[f"down{l}"]
                with sp.Fori(0, KT) as it:
                    for s in range(4):
                        u = u0 + s
                        sp.wait_ge(lo_ready, u - R + 1 + it * 4)
                        src = I["w_ffn_down"][l][s * D:(s + 1) * D, bass.ds(it * P, P)].rearrange("(k p) c -> p k c", p=P)
                        dst = raw[:, u % R, :].rearrange("p (k c) -> p k c", k=KT)
                        sp.dma_start(dst, src).then_inc(raw_landed[u % R], 16)
                for i in range(2):
                    load(UNITS[f"ple{l}"] + i, I["w_ple"][l][:, i * 512:(i + 1) * 512].rearrange("(k p) c -> p k c", p=P))
                for i in range(8):
                    load(UNITS[f"gate{l}"] + i, col_unit(I["w_ple_gate"][l], i * P))

        @block.gpsimd
        def _(pool):
            g = nc.gpsimd
            ld_x, ld_par, ld_pe, ld_cache, ld_narrow = (sem(n) for n in ("ld_x", "ld_par", "ld_pe", "ld_cache", "ld_narrow"))
            pool.dma_start(xtok[:, 0:2, :], I["x_prompt"][0].rearrange("(t p) d -> p t d", p=P)).then_inc(ld_x, 16)
            pool.dma_start(xtok[0:TS, 2, :], I["x_sample"][0]).then_inc(ld_x, 16)
            ch = sem("const_step")
            n = [0]

            def link(ins):
                n[0] += 1
                ins.then_inc(ch, 1)
                pool.wait_ge(ch, n[0])

            link(g.memset(ident[:], 0.0))
            link(g.affine_select(out=ident[:], in_=ident[:], compare_op=ALU.not_equal, fill=1.0, base=0,
                                 pattern=[[-1, P]], channel_multiplier=1))
            g.memset(cst[:, 0:1], EPS)
            link(g.memset(cst[:, 1:2], 1.0))
            g.memset(ones[:], 1.0).then_inc(sem("const"), 1)
            for l in range(2):
                pool.dma_start(prow[0:96, l, :], I["ffn_conv_w"][l].rearrange("t (j c) -> (t j) c", c=P)).then_inc(ld_par, 16)
                pool.dma_start(prow[96:128, l, :], I["ffn_conv_b"][l].rearrange("(j c) -> j c", c=P)).then_inc(ld_par, 16)
                pool.dma_start(nrow[0:64, l, :], I["state_ffn_conv"][l, 0].rearrange("r (j c) -> (r j) c", c=P)).then_inc(ld_par, 16)
                for i, nm in enumerate(("ln_mix_pre", "ln_mix_post", "ln_ffn_pre", "ln_ffn_post")):
                    pool.dma_start(nrow[64 + 8 * i:72 + 8 * i, l, :], I[nm][l].rearrange("(j c) -> j c", c=P)).then_inc(ld_par, 16)
                pool.dma_start(nrow[96:104, l, :], I["rec_norm"][0].rearrange("(j c) -> j c", c=P)).then_inc(ld_par, 16)
            pool.dma_start(wnr[:, 0], I["w_att_in"][0][:, 1536:1544].rearrange("(k p) c -> p k c", p=P)).then_inc(ld_narrow, 16)
            pool.dma_start(wnr[:, 1], I["w_rec_in"][0][:, 2048:2056].rearrange("(k p) c -> p k c", p=P)).then_inc(ld_narrow, 16)
            for l in range(2):
                pool.dma_start(petok[:, l, 0:2, :], I["p_prompt"][l, 0].rearrange("(t p) d -> p t d", p=P)).then_inc(ld_pe, 16)
                pool.dma_start(petok[0:TS, l, 2, :], I["p_sample"][l, 0]).then_inc(ld_pe, 16)
            pool.dma_start(kcache[:], I["cache_fox_k"][0, 0].rearrange("(t p) h d -> p t (h d)", p=P)).then_inc(ld_cache, 16)
            pool.dma_start(vcache[:], I["cache_fox_v"][0, 0].rearrange("(t p) h d -> p t (h d)", p=P)).then_inc(ld_cache, 16)
            pool.dma_start(kcs[:], I["cache_swa_k"][0, 0].rearrange("p h d -> p (h d)")).then_inc(ld_cache, 16)
            pool.dma_start(vcs[:], I["cache_swa_v"][0, 0].rearrange("p h d -> p (h d)")).then_inc(ld_cache, 16)
            pool.dma_start(clf[:], I["cache_fox_logf"][0, 0].rearrange("(t p) h -> p t h", p=P)).then_inc(ld_cache, 16)
            pool.dma_start(sinkb[:], I["swa_sink"][0:1, :].to_broadcast([P, NH])).then_inc(ld_cache, 16)
            pool.dma_start(bcol[:, 0:1], I["fox_fb"].rearrange("a h -> h a"), allow_slow_non_contiguous=True).then_inc(ld_cache, 16)
            pool.dma_start(bcol[0:4, 1:2], I["rec_ig_b"].rearrange("a h -> h a"), allow_slow_non_contiguous=True).then_inc(ld_cache, 16)
            pool.dma_start(bcol[4:8, 1:2], I["rec_fg_b"].rearrange("a h -> h a"), allow_slow_non_contiguous=True).then_inc(ld_cache, 16)
            link(g.memset(Ut[:], 1.0))
            link(g.affine_select(out=Ut[:], in_=Ut[:], compare_op=ALU.is_ge, fill=0.0, base=0, pattern=[[1, P]], channel_multiplier=-1))
            link(g.tensor_copy(Ub[:], Ut[:]))
            link(g.memset(Ub[0:64, 64:128], 0.0))
            link(g.memset(MFox[:], 0.0))
            link(g.affine_select(out=MFox[:, 256:384], in_=MFox[:, 256:384], compare_op=ALU.is_ge, fill=NEG, base=0,
                                 pattern=[[-1, P]], channel_multiplier=1))
            link(g.tensor_copy(MBlk[:], MFox[:, 256:384]))
            link(g.memset(MBlk[64:128, 0:64], NEG))
            link(g.memset(MSwa[:], 0.0))
            link(g.memset(MSwa[64:128, 0:64], NEG))
            link(g.memset(MSwa[0:64, 192:256], NEG))
            g.memset(gp[:], 0.0).then_inc(sem("const2"), 1)

            st = sem("stored")
            n_st = [0]

            def store(dst, src, short_rows=False):
                pool.dma_start(dst, src, allow_slow_non_contiguous=short_rows).then_inc(st, 16)
                n_st[0] += 1

            pool.wait_ge(ld_cache, 16 * 9)
            store(O["s_swa_k"][0, 0, 0:64].rearrange("p h d -> p (h d)"), kcs[64:128, :])
            store(O["s_swa_v"][0, 0, 0:64].rearrange("p h d -> p (h d)"), vcs[64:128, :])
            for l in range(2):
                if l == 0:
                    pool.wait_ge(sem("lf_tok"), 1)
                    store(O["p_fox_logf"][0, 0].rearrange("(t p) h -> p t h", p=P), lftok[:, 0:2, :])
                    store(O["s_fox_logf"][0, 0], lftok[0:TS, 2, :])
                    pool.wait_ge(sem("tok_read"), 9)
                    for nm, tt in (("k", Ktok), ("v", Vtok)):
                        store(O[f"p_fox_{nm}"][0, 0].rearrange("(t p) h d -> p t (h d)", p=P), tt[:, 0:2, :])
                        store(O[f"s_fox_{nm}"][0, 0].rearrange("p h d -> p (h d)"), tt[0:TS, 2, :])
                    for i, nm in enumerate(("k", "v")):
                        store(O[f"p_swa_{nm}"][0, 0].rearrange("p h d -> p (h d)"), Stok[:, 1, i * P:(i + 1) * P])
                        store(O[f"s_swa_{nm}"][0, 0, 64:128].rearrange("p h d -> p (h d)"), Stok[0:TS, 2, i * P:(i + 1) * P])
                else:
                    signal, value = FULL[gid("gate0", 7)]
                    pool.wait_ge(signal, value)
                    pool.dma_start(C[:, 1, :, 0:DV], I["state_mlstm_c"][0, 0].rearrange("h k v -> k h v")).then_inc(sem("ld_state"), 16)
                    pool.dma_start(C[:, 1, :, DV:DV + 1], I["state_mlstm_n"][0, 0].rearrange("h (k a) -> k h a", a=1), allow_slow_non_contiguous=True).then_inc(sem("ld_state"), 16)
                    pool.dma_start(mprev[:, 4, :], I["state_mlstm_m"][0].to_broadcast([P, MH])).then_inc(sem("ld_state"), 16)
                    for b, pre in ((0, "p"), (1, "s")):
                        pool.wait_ge(sem("C_new"), 16 + 4 * b)
                        store(O[f"{pre}_ml_c"][0, 0].rearrange("h k v -> k h v"), C[:, b, :, 0:DV])
                        store(O[f"{pre}_ml_n"][0, 0].rearrange("h (k a) -> k h a", a=1), C[:, b, :, DV:DV + 1], True)
                    store(O["p_ml_m"][0], mprev[0:1, 5, :])
                    store(O["s_ml_m"][0], mz[0:1, 3, 0:4])
                def add_x(stage, l):
                    for j in range(KT):
                        pool.wait_ge(sem("post"), eights(f"{stage}{l}", j))
                        g.tensor_tensor(xT[:, j, :], xT[:, j, :], mix[:, j, :], ALU.add).then_inc(sem("x_post"), 1)

                add_x("mixpost", l)
                pool.wait_ge(st, 16 * n_st[0])
                pool.sem_inc(sem(f"scratch_out{l}"), 1)
                with pool.Fori(0, FT // 2) as it:
                    for s in range(2):
                        pool.wait_ge(sem(f"us{l}"), it * 2 + (s + 1))
                        pool.wait_ge(sem(f"gelu{l}"), it * 2 + (s + 1))
                        g.tensor_tensor(fb[:, s, 0:TP], cv[:, s, 0:TP], us[:, s, 0:TP], ALU.mult)
                        g.tensor_tensor(fb[:, s, TP:T], cv[:, s, TP + 2:T + 2], us[:, s, TP:T], ALU.mult)
                        tail = gp[:, s, 192:324].rearrange("p (b r) -> p b r", b=2)[:, :, 64:66]
                        dst = cs[:, :, bass.ds(it * 2 + s, 1)].rearrange("p (b r) j -> p b (r j)", b=2)
                        g.tensor_copy(dst, tail).then_inc(sem(f"f{l}"), 1)
                pool.wait_ge(sem(f"csT{l}"), 1)
                store(O["p_conv"][l, 0].rearrange("r (j c) -> (r j) c", c=P), csT[0:64, :])
                store(O["s_conv"][l, 0].rearrange("r (j c) -> (r j) c", c=P), csT[64:128, :])
                add_x("ffnpost", l)
                for j in range(KT):
                    pool.wait_ge(sem(f"sg{l}"), j + 1)
                    g.tensor_tensor(xT[:, j, :], xT[:, j, :], sgb[:, j % 2, :], ALU.add).then_inc(sem(f"x_out{l}"), 1)
                pool.wait_ge(st, 16 * n_st[0])
            for t in range(3):
                pool.wait_ge(sem("ytok"), 2 * (t + 1))
                n_t = TOK[t][1]
                dst = O["y_prompt"][0, t * P:t * P + P] if t < 2 else O["y_sample"][0]
                store(dst, xtok[0:n_t, t, :])
            pool.wait_ge(st, 16 * n_st[0])

        @block.tensor
        def _(pe):
            mmul = nc.tensor.matmul
            trans = nc.tensor.transpose

            def unit(u, out, rh, rl, first, last, k_wait=None, it=0):
                pe.wait_ge(lo_ready, u + 1 + it)
                for k in range(8):
                    if k_wait:
                        k_wait(k)
                    a, b = wh[:, u % R, k * P:(k + 1) * P], wl[:, u % R, k * P:(k + 1) * P]
                    mmul(out, a, rh[:, k, :], start=first and k == 0, stop=False)
                    mmul(out, a, rl[:, k, :], start=False, stop=False)
                    m = mmul(out, b, rh[:, k, :], start=False, stop=last and k == 7)
                m.then_inc(unit_used, 1)

            def stats(name, j, src):
                pe.wait_ge(sem("sq"), 8 * NORMS[name] + j + 1)
                m = mmul(bank[4][:, 0:T], ones[:], src[:, j, :], start=j == 0, stop=j == KT - 1)
                if j == KT - 1:
                    m.then_inc(sem("sq_sum"), 1)

            pe.wait_ge(sem("const"), 1)
            pe.wait_ge(sem("const_step"), 2)
            pe.wait_ge(sem("ld_x"), 32)
            for j in range(KT):
                gi = gid("x", j)
                bank_free(pe, gi)
                for t, (t0, n) in enumerate(TOK):
                    m = trans(gbank(gi)[:, t0:t0 + n], xtok[0:n, t, j * P:(j + 1) * P], ident[0:n, 0:n])
                m.then_inc(bank_done[gi % 4], 1)
            pe.wait_ge(sem("ld_par"), 16 * 16)
            for l in range(2):
                for i, (rows, n) in enumerate(((prow, P), (nrow, 104))):
                    gi = gid("par", 2 * l + i)
                    bank_free(pe, gi)
                    trans(gbank(gi)[:, 0:n], rows[0:n, l, :], ident[0:n, 0:n]).then_inc(bank_done[gi % 4], 1)
            pe.wait_ge(sem("ld_pe"), 64)
            for l in range(2):
                for k in range(2):
                    gi = gid("pe", 2 * l + k)
                    bank_free(pe, gi)
                    for t, (t0, n) in enumerate(TOK):
                        m = trans(gbank(gi)[:, t0:t0 + n], petok[0:n, l, t, k * P:(k + 1) * P], ident[0:n, 0:n])
                    m.then_inc(bank_done[gi % 4], 1)
            pe.wait_ge(sem("ld_cache"), 16 * 9)
            for j in range(4):
                gi = gid("cache", j)
                bank_free(pe, gi)
                for t in range(2):
                    m = trans(gbank(gi)[:, t * P:(t + 1) * P], kcache[:, t, j * P:(j + 1) * P], ident[:])
                m.then_inc(bank_done[gi % 4], 1)
            gi = gid("cache", 4)
            bank_free(pe, gi)
            trans(gbank(gi)[:, 0:P], kcs[:], ident[:]).then_inc(bank_done[gi % 4], 1)

            for l in range(2):
                n_in = len(ATT_COLS) if l == 0 else len(REC_COLS)

                def narrow():
                    gi = gid(f"narrow{l}")
                    bank_free(pe, gi)
                    pe.wait_ge(sem("narrow_split"), 1)
                    out = gbank(gi)[0:8, 0:T]
                    for k in range(KT):
                        mmul(out, wnH[:, l, k, :], hH[:, k, :], start=k == 0, stop=False)
                        mmul(out, wnH[:, l, k, :], hL[:, k, :], start=False, stop=False)
                        m = mmul(out, wnL[:, l, k, :], hH[:, k, :], start=False, stop=k == KT - 1)
                    m.then_inc(bank_done[gi % 4], 1)

                for i in range(n_in):
                    gi = gid(f"in{l}", i) if (l == 1 or i < 12) else gid("swin", i - 12)
                    if l == 0 and i == 12:
                        narrow()
                    bank_free(pe, gi)
                    unit(UNITS[f"in{l}"] + i, gbank(gi)[:, 0:T], hH, hL, True, True,
                         (lambda k: pe.wait_ge(sem("h_lo"), eights(f"mixpre{l}", k))) if i == 0 else None)
                    if i == 0:
                        for j in range(KT):
                            stats(f"mixpre{l}", j, sqb)
                if l == 1:
                    narrow()
                if l == 0:
                    attention_pe(pe)
                else:
                    mlstm_pe(pe)
                for i in range(8):
                    gi = gid(f"out{l}", i)
                    bank_free(pe, gi)
                    unit(UNITS[f"out{l}"] + i, gbank(gi)[:, 0:T], OH, OL, True, True,
                         (lambda k: pe.wait_ge(sem(f"o_lo{l}"), k + 1 if l == 0 else 12)) if i == 0 else None)
                    if i >= 1:
                        stats(f"mixpost{l}", i - 1, sqb)
                stats(f"mixpost{l}", 7, sqb)
                u0, g0 = UNITS[f"up{l}"], gid(f"up{l}")
                for s in range(4):
                    bank_free(pe, g0 + s)
                    unit(u0 + s, gbank(g0 + s)[:, 0:T], hH, hL, True, True,
                         (lambda k: pe.wait_ge(sem("h_lo"), eights(f"ffnpre{l}", k))) if s == 0 else None)
                    if s == 0:
                        for j in range(KT):
                            stats(f"ffnpre{l}", j, sqb)
                with pe.Fori(1, FT // 2) as it:
                    for s in range(4):
                        gi = g0 + s
                        pe.wait_ge(sem(("us" if s % 2 else "gp") + str(l)), it * 2 + (s // 2 - 1))
                        unit(u0 + s, gbank(gi)[:, 0:T], hH, hL, True, True, it=it * 4)
                gi = gid(f"cs{l}")
                bank_free(pe, gi)
                pe.wait_ge(sem(f"f_lo{l}"), FT)
                trans(gbank(gi)[:, 0:P], cs[:].rearrange("p a j -> p (a j)"), ident[:]).then_inc(bank_done[gi % 4], 1)
                u0, g0 = UNITS[f"down{l}"], gid(f"down{l}")
                for i in range(8):
                    gi = g0 + i
                    bank_free(pe, gi)
                    for q in range(4):
                        unit(u0 + 4 * i + q, gbank(gi)[:, 0:T], FH[:, 8 * q:8 * q + 8, :], FL[:, 8 * q:8 * q + 8, :], q == 0, q == 3)
                        if q == 0 and i >= 1:
                            stats(f"ffnpost{l}", i - 1, sqb)
                stats(f"ffnpost{l}", 7, sqb)
                for i in range(8):
                    gi = gid(f"ple{l}", i)
                    bank_free(pe, gi)
                    u = UNITS[f"ple{l}"] + i // 4
                    pe.wait_ge(lo_ready, u + 1)
                    out = gbank(gi)[:, 0:T]
                    for k in range(2):
                        c = k * 512 + (i % 4) * P
                        a, b = wh[:, u % R, c:c + P], wl[:, u % R, c:c + P]
                        mmul(out, a, peH[:, 2 * l + k, :], start=k == 0, stop=False)
                        mmul(out, a, peL[:, 2 * l + k, :], start=False, stop=False)
                        m = mmul(out, b, peH[:, 2 * l + k, :], start=False, stop=k == 1)
                    m.then_inc(unit_used if i % 4 == 3 else bank_done[gi % 4], 1)
                for i in range(8):
                    gi = gid(f"gate{l}", i)
                    bank_free(pe, gi)
                    unit(UNITS[f"gate{l}"] + i, gbank(gi)[:, 0:T], OH, OL, True, True,
                         (lambda k: pe.wait_ge(sem(f"xs_lo{l}"), k + 1)) if i == 0 else None)
            for t, (t0, n) in enumerate(TOK):
                for half in range(2):
                    gi = gid("y", 2 * t + half)
                    bank_free(pe, gi)
                    pe.wait_ge(sem("x_out1"), 8)
                    for j in range(4):
                        m = trans(gbank(gi)[0:n, j * P:(j + 1) * P], xT[:, 4 * half + j, t0:t0 + n], ident[:])
                    m.then_inc(bank_done[gi % 4], 1)



        @block.scalar
        def _(act):
            A = nc.scalar.activation

            def hi(u, it=0, mod=None):
                if mod is None:
                    if u >= N_UNITS:
                        return
                    act.wait_ge(raw_landed[u % R], 16 * (u // R + 1))
                    if u >= R:
                        act.wait_ge(unit_used, u - R + 1)
                else:
                    act.wait_ge(raw_landed[u % R], mod * 16 + 16 * (u // R + 1))
                    act.wait_ge(unit_used, mod * 4 + (u - R + 1))
                A(wh[:, u % R, :], raw[:, u % R, :], ACT.Copy).then_inc(hi_ready, 1)

            ach = sem("act_step")
            cnt = [0]

            def link(ins):
                cnt[0] += 1
                ins.then_inc(ach, 1)
                act.wait_ge(ach, cnt[0])

            def prenorm(stage, l, ready, col):
                for j in range(KT):
                    ready(j)
                    A(hH[:, j, :], xT[:, j, :], ACT.Copy, scale=NC[:, l, col + j:col + j + 1]).then_inc(sem("h_hi"), 1)
                    A(sqb[:, j, :], xT[:, j, :], ACT.Square).then_inc(sem("sq"), 1)

            def root(stage, l):
                act.wait_ge(sem("sq_sum"), NORMS[f"{stage}{l}"] + 1)
                A(fb[:, 0, :], bank[4][:, 0:T], ACT.Sqrt, scale=1.0 / D, bias=cst[:, 0:1]).then_inc(sem("root"), 1)

            for u in range(LEAD):
                hi(u)
            act.wait_ge(sem("par_in"), 4)
            act.wait_ge(sem("const"), 1)
            act.wait_ge(sem("ld_narrow"), 32)
            A(wnH[:].rearrange("p a b c -> p (a b c)"), wnr[:].rearrange("p a b c -> p (a b c)"), ACT.Copy).then_inc(sem("narrow_hi"), 1)
            act.wait_ge(sem("pe_f"), 4)
            A(peH[:].rearrange("p a t -> p (a t)"), pef[:].rearrange("p a t -> p (a t)"), ACT.Copy).then_inc(sem("pe_hi"), 1)
            for l in range(2):
                u_in, u_out = UNITS[f"in{l}"], UNITS[f"out{l}"]
                n_in = u_out - u_in
                prenorm("mixpre", l, (lambda j: act.wait_ge(sem("x_in"), j + 1)) if l == 0 else
                        (lambda j: act.wait_ge(sem("x_out0"), j + 1)), 64)
                hi(u_in + LEAD)
                root("mixpre", l)
                for i in range(1, n_in):
                    hi(u_in + i + LEAD)
                    if l == 1 and i >= 17:
                        j = i - 17
                        act.wait_ge(sem("in_read1"), 17 + j)
                        A(sig[:, j, :], sig[:, j, :], ACT.Sigmoid).then_inc(sem("og"), 1)
                if l == 1:
                    act.wait_ge(sem("in_read1"), 24)
                    A(sig[:, 7, :], sig[:, 7, :], ACT.Sigmoid).then_inc(sem("og"), 1)
                if l == 0:
                    attention_act(act)
                else:
                    mlstm_act(act)
                for i in range(8):
                    hi(u_out + i + LEAD)
                    gi = gid(f"out{l}", i)
                    bank_full(act, gi)
                    A(mix[:, i, :], gbank(gi)[:, 0:T], ACT.Copy).then_inc(sem(f"mix_{l}"), 1)
                    A(sqb[:, i, :], gbank(gi)[:, 0:T], ACT.Square).then_inc(sem("sq"), 1)
                root("mixpost", l)
                prenorm("ffnpre", l, lambda j: act.wait_ge(sem("x_post"), eights(f"mixpost{l}", j)), 80)
                root("ffnpre", l)
                act.wait_ge(sem(f"scratch_out{l}"), 1)
                u0 = UNITS[f"up{l}"]
                with act.Fori(0, FT // 2) as it:
                    for s in range(2):
                        hi(u0 + 2 * s + LEAD, mod=it)
                        act.wait_ge(sem(f"gp{l}"), it * 2 + (s + 1))
                        j = it * 2 + s
                        A(cv[:, s, :], gp[:, s, 2:T + 4], ACT.Identity, scale=PC[:, l, bass.ds(j + 64, 1)],
                          bias=PC[:, l, bass.ds(j + 96, 1)]).then_inc(sem(f"cv{l}"), 1)
                        hi(u0 + 2 * s + 1 + LEAD, mod=it)
                        act.wait_ge(sem(f"conv{l}"), it * 4 + (2 * s + 2))
                        A(cv[:, s, :], cv[:, s, :], ACT.Gelu_apprx_tanh).then_inc(sem(f"gelu{l}"), 1)
                        act.wait_ge(sem(f"f{l}"), it * 2 + (s + 1))
                        A(FH[:, bass.ds(j, 1), :].rearrange("p a t -> p (a t)"), fb[:, s, :], ACT.Copy).then_inc(sem(f"f_hi{l}"), 1)
                u0 = UNITS[f"down{l}"]
                for i in range(8):
                    for q in range(4):
                        hi(u0 + 4 * i + q + LEAD)
                    gi = gid(f"down{l}", i)
                    bank_full(act, gi)
                    A(mix[:, i, :], gbank(gi)[:, 0:T], ACT.Copy).then_inc(sem(f"mixf_{l}"), 1)
                    A(sqb[:, i, :], gbank(gi)[:, 0:T], ACT.Square).then_inc(sem("sq"), 1)
                root("ffnpost", l)
                for i in range(8):
                    if i % 4 == 3:
                        hi(UNITS[f"ple{l}"] + i // 4 + LEAD)
                    gi = gid(f"ple{l}", i)
                    bank_full(act, gi)
                    A(sqb[:, i, :], gbank(gi)[:, 0:T], ACT.Copy).then_inc(sem(f"ple_sb{l}"), 1)
                    act.wait_ge(sem("x_post"), eights(f"ffnpost{l}", i))
                    A(OH[:, i, :], xT[:, i, :], ACT.Copy).then_inc(sem(f"xs_hi{l}"), 1)
                for i in range(8):
                    hi(UNITS[f"gate{l}"] + i + LEAD)
                    gi = gid(f"gate{l}", i)
                    bank_full(act, gi)
                    if i >= 2:
                        act.wait_ge(sem(f"x_out{l}"), i - 1)
                    A(sgb[:, i % 2, :], gbank(gi)[:, 0:T], ACT.Sigmoid).then_inc(sem(f"sigm{l}"), 1)
            for i in range(6):
                t, half = i // 2, i % 2
                gi = gid("y", i)
                n = TOK[t][1]
                bank_full(act, gi)
                A(xtok[0:n, t, half * 512:(half + 1) * 512], gbank(gi)[0:n, :], ACT.Copy).then_inc(sem("ytok"), 1)




        @block.vector
        def _(dve):
            V = nc.vector

            def lo(u, mod=None):
                if mod is None:
                    if u >= N_UNITS:
                        return
                    dve.wait_ge(hi_ready, u + 1)
                else:
                    dve.wait_ge(hi_ready, mod * 4 + (u + 1))
                V.tensor_tensor(wl[:, u % R, :], raw[:, u % R, :], wh[:, u % R, :].bitcast(F32), ALU.subtract).then_inc(lo_ready, 1)

            def prenorm_lo(stage, l, col):
                for j in range(KT):
                    dve.wait_ge(sem("h_hi"), eights(f"{stage}{l}", j))
                    V.scalar_tensor_tensor(out=hL[:, j, :], in0=xT[:, j, :], scalar=NC[:, l, col + j:col + j + 1],
                                           in1=hH[:, j, :].bitcast(F32), op0=ALU.mult, op1=ALU.subtract).then_inc(sem("h_lo"), 1)

            def inverse(stage, l, dst):
                dve.wait_ge(sem("root"), NORMS[f"{stage}{l}"] + 1)
                V.reciprocal(dst[:], fb[:, 0, :]).then_inc(sem("rstd"), 1)
                dve.wait_ge(sem("rstd"), NORMS[f"{stage}{l}"] + 1)

            def postnorm(stage, l, col):
                inverse(stage, l, rstd2)
                for j in range(KT):
                    V.scalar_tensor_tensor(out=mix[:, j, :], in0=mix[:, j, :], scalar=NC[:, l, col + j:col + j + 1],
                                           in1=rstd2[:], op0=ALU.mult, op1=ALU.mult).then_inc(sem("post"), 1)

            for j in range(KT):
                gi = gid("x", j)
                bank_full(dve, gi)
                V.tensor_copy(xT[:, j, :], gbank(gi)[:, 0:T]).then_inc(sem("x_in"), 1)
            for l in range(2):
                for i, dst in enumerate((PC, NC)):
                    gi = gid("par", 2 * l + i)
                    n = (P, 104)[i]
                    bank_full(dve, gi)
                    V.tensor_copy(dst[:, l, 0:n], gbank(gi)[:, 0:n]).then_inc(sem("par_in"), 1)
            for i in range(4):
                gi = gid("pe", i)
                bank_full(dve, gi)
                V.tensor_copy(pef[:, i, :], gbank(gi)[:, 0:T]).then_inc(sem("pe_f"), 1)
            for u in range(LEAD):
                lo(u)
            dve.wait_ge(sem("narrow_hi"), 1)
            V.tensor_tensor(wnL[:].rearrange("p a b c -> p (a b c)"), wnr[:].rearrange("p a b c -> p (a b c)"),
                            wnH[:].rearrange("p a b c -> p (a b c)").bitcast(F32), ALU.subtract).then_inc(sem("narrow_split"), 1)
            dve.wait_ge(sem("pe_hi"), 1)
            V.tensor_tensor(peL[:].rearrange("p a t -> p (a t)"), pef[:].rearrange("p a t -> p (a t)"),
                            peH[:].rearrange("p a t -> p (a t)").bitcast(F32), ALU.subtract).then_inc(sem("pe_split"), 1)
            dve.wait_ge(sem("pe_split"), 1)
            dve.wait_ge(sem("narrow_split"), 1)
            for j in range(4):
                gi = gid("cache", j)
                bank_full(dve, gi)
                V.tensor_copy(kcT[:, j, :], gbank(gi)[:, 0:PAST]).then_inc(sem("cache_read"), 1)
            gi = gid("cache", 4)
            bank_full(dve, gi)
            for half in range(2):
                for g in range(2):
                    ins = V.tensor_copy(kcdup[64 * half:64 * half + 64, g, :], gbank(gi)[64 * g:64 * g + 64, 0:P])
            ins.then_inc(sem("cache_read"), 1)

            for l in range(2):
                u_in, u_out = UNITS[f"in{l}"], UNITS[f"out{l}"]
                n_in = u_out - u_in
                prenorm_lo("mixpre", l, 64)
                lo(u_in + LEAD)
                inverse("mixpre", l, rstd)

                def scaled(dst, gi, rows=slice(0, P), factor=None, src_rows=None, last=True):
                    sr = src_rows or rows
                    src = gbank(gi)[sr, 0:T]
                    if factor is None:
                        ins = V.tensor_tensor(dst, src, rstd[sr, :], ALU.mult)
                    else:
                        ins = V.scalar_tensor_tensor(out=dst, in0=src, scalar=factor, in1=rstd[sr, :], op0=ALU.mult, op1=ALU.mult)
                    if last:
                        ins.then_inc(sem(f"in_read{l}"), 1)
                    return ins

                def narrow(z):
                    gi = gid(f"narrow{l}")
                    bank_full(dve, gi)
                    s = sem(f"narrow_step{l}")
                    scaled(z[:, 0, :], gi, rows=slice(0, 8), last=False).then_inc(s, 1)
                    dve.wait_ge(s, 1)
                    V.tensor_scalar(z[:, 0, :], z[:, 0, :], bcol[:, l:l + 1], None, ALU.add).then_inc(s, 1)
                    dve.wait_ge(s, 2)
                    k = 1 if l == 0 else 2
                    V.scalar_tensor_tensor(out=z[:, k, :], in0=z[:, 0, :], scalar=-1.0, in1=z[:, 0, :], op0=ALU.mult, op1=ALU.max).then_inc(sem("lf_abs" if l == 0 else "mlf_abs"), 1)
                    V.tensor_scalar(z[:, 2 if l == 0 else 1, :], z[:, 0, :], 0.0, None, ALU.min).then_inc(s, 1)

                for i in range(n_in):
                    if i:
                        lo(u_in + i + LEAD)
                    if l == 0:
                        gi = gid("in0", i) if i < 12 else gid("swin", i - 12)
                        if i == 12:
                            narrow(lfz)
                        bank_full(dve, gi)
                        if i < 4:
                            scaled(mix[:, i, :], gi, factor=HD ** -0.5)
                        elif i < 8:
                            scaled(kT[:, i - 4, :], gi)
                        elif i < 12:
                            scaled(sqb[:, i - 8, :], gi)
                        elif i < 16:
                            scaled(mix[:, i - 8, :], gi, factor=HD ** -0.5)
                        elif i == 16:
                            for half in range(2):
                                for g in range(2):
                                    scaled(kdup[64 * half:64 * half + 64, g, :], gi, src_rows=slice(64 * g, 64 * g + 64), last=False)
                            scaled(kplain[:], gi)
                        else:
                            scaled(sqb[:, 4, :], gi)
                    else:
                        gi = gid("in1", i)
                        bank_full(dve, gi)
                        if i < 4:
                            scaled(mix[:, i, :], gi)
                        elif i < 8:
                            scaled(mix[:, i, :], gi, factor=DK ** -0.5)
                        elif i < 16:
                            scaled(sqb[:, i - 8, :], gi)
                        else:
                            scaled(sig[:, i - 16, :], gi)
                if l == 0:
                    attention_dve(dve)
                else:
                    narrow(mz)
                    mlstm_dve(dve)
                for i in range(8):
                    lo(u_out + i + LEAD)
                dve.wait_ge(sem(f"mix_{l}"), 8)
                postnorm("mixpost", l, 72)
                prenorm_lo("ffnpre", l, 80)
                inverse("ffnpre", l, rstd)
                dve.wait_ge(sem(f"scratch_out{l}"), 1)
                u0, g0 = UNITS[f"up{l}"], gid(f"up{l}")
                with dve.Fori(0, FT // 2) as it:
                    for s in range(2):
                        j = it * 2 + s
                        ga, gu = g0 + 2 * s, g0 + 2 * s + 1
                        hist = NC[:, l, 0:64].rearrange("p (r j) -> p r j", r=2)[:, :, bass.ds(j, 1)].rearrange("p r j -> p (r j)")
                        V.tensor_copy(gp[:, s, 258:260], hist)
                        bank_full(dve, ga, it * 4)
                        V.tensor_tensor(gp[:, s, 2:258], gbank(ga)[:, 0:TP], rstd[:, 0:TP], ALU.mult)
                        V.tensor_tensor(gp[:, s, 260:324], gbank(ga)[:, TP:T], rstd[:, TP:T], ALU.mult)\
                            .then_inc(sem(f"gp{l}"), 1)
                        lo(u0 + 2 * s + LEAD, mod=it)
                        dve.wait_ge(sem(f"cv{l}"), it * 2 + (s + 1))
                        for tap in (1, 0):
                            V.scalar_tensor_tensor(out=cv[:, s, :], in0=gp[:, s, tap:tap + T + 2], scalar=PC[:, l, bass.ds(j + 32 * tap, 1)],
                                                   in1=cv[:, s, :], op0=ALU.mult, op1=ALU.add).then_inc(sem(f"conv{l}"), 1)
                            if tap:
                                dve.wait_ge(sem(f"conv{l}"), it * 4 + (2 * s + 1))
                        bank_full(dve, gu, it * 4)
                        V.tensor_tensor(us[:, s, :], gbank(gu)[:, 0:T], rstd[:], ALU.mult).then_inc(sem(f"us{l}"), 1)
                        lo(u0 + 2 * s + 1 + LEAD, mod=it)
                        dve.wait_ge(sem(f"f_hi{l}"), it * 2 + (s + 1))
                        V.tensor_tensor(FL[:, bass.ds(j, 1), :].rearrange("p a t -> p (a t)"), fb[:, s, :],
                                        FH[:, bass.ds(j, 1), :].rearrange("p a t -> p (a t)").bitcast(F32), ALU.subtract).then_inc(sem(f"f_lo{l}"), 1)
                gi = gid(f"cs{l}")
                bank_full(dve, gi)
                V.tensor_copy(csT[:], gbank(gi)[:, 0:P]).then_inc(sem(f"csT{l}"), 1)
                for i in range(32):
                    lo(UNITS[f"down{l}"] + i + LEAD)
                dve.wait_ge(sem(f"mixf_{l}"), 8)
                postnorm("ffnpost", l, 88)
                for i in range(8):
                    if i % 4 == 3:
                        lo(UNITS[f"ple{l}"] + i // 4 + LEAD)
                    dve.wait_ge(sem(f"xs_hi{l}"), i + 1)
                    V.tensor_tensor(OL[:, i, :], xT[:, i, :], OH[:, i, :].bitcast(F32), ALU.subtract).then_inc(sem(f"xs_lo{l}"), 1)
                for i in range(8):
                    lo(UNITS[f"gate{l}"] + i + LEAD)
                    dve.wait_ge(sem(f"sigm{l}"), i + 1)
                    dve.wait_ge(sem(f"ple_sb{l}"), i + 1)
                    V.tensor_tensor(sgb[:, i % 2, :], sgb[:, i % 2, :], sqb[:, i, :], ALU.mult).then_inc(sem(f"sg{l}"), 1)






_OUTS = [
    ("y_prompt", (1, TP, D)), ("y_sample", (1, TS, D)),
    ("p_fox_k", (1, 1, TP, NH, HD)), ("p_fox_v", (1, 1, TP, NH, HD)), ("p_fox_logf", (1, 1, TP, NH)),
    ("p_swa_k", (1, 1, P, 2, HD)), ("p_swa_v", (1, 1, P, 2, HD)),
    ("p_ml_c", (1, 1, MH, DK, DV)), ("p_ml_n", (1, 1, MH, DK)), ("p_ml_m", (1, 1, MH)), ("p_conv", (2, 1, 2, FF)),
    ("s_fox_k", (1, 1, TS, NH, HD)), ("s_fox_v", (1, 1, TS, NH, HD)), ("s_fox_logf", (1, 1, TS, NH)),
    ("s_swa_k", (1, 1, P, 2, HD)), ("s_swa_v", (1, 1, P, 2, HD)),
    ("s_ml_c", (1, 1, MH, DK, DV)), ("s_ml_n", (1, 1, MH, DK)), ("s_ml_m", (1, 1, MH)), ("s_conv", (2, 1, 2, FF)),
]
_SQUEEZED = {"p_fox_k", "p_fox_v", "p_fox_logf"}


def kernel(**inputs):
    import numpy as np
    import concourse.bacc as bacc
    from concourse.bass_utils import run_bass_kernel_spmd as run

    nc = bacc.Bacc("TRN2", target_bir_lowering=False, num_devices=1)
    arrays, ins = {}, {}
    for name, a in inputs.items():
        a = np.ascontiguousarray(a)
        arrays[f"in_{name}"] = a
        ins[name] = nc.dram_tensor(f"in_{name}", a.shape, F32, kind="ExternalInput").ap()
    outs = {n: nc.dram_tensor(f"out_{n}", s, F32, kind="ExternalOutput").ap() for n, s in _OUTS}
    encoder_step(nc, ins, outs)
    r = run(nc, [arrays], core_ids=[0]).results[0]
    return tuple(r[f"out_{n}"] for n, _ in _OUTS)
```

```python
from contextlib import ExitStack

import concourse.bass as bass
from concourse import mybir

ACT = mybir.ActivationFunctionType
ALU = mybir.AluOpType
F32 = mybir.dt.float32
F32R = mybir.dt.float32r
X = mybir.AxisListType.X

P = 128
D = 1024
KT = D // P
TP, TS = 256, 64
T = TP + TS
CH = 64
FF = 4096
FT = FF // P
PAST = 256
HD = 64
NH = 8
MH, DK, DV = 4, 128, 256
EPS = 1e-6
NEG = -1e30
R = 4
TOK = [(0, 128), (128, 128), (256, 64)]

ATT_COLS = [P * j for j in range(12)] + [1544 + P * j for j in range(6)]
REC_COLS = [P * j for j in range(8)] + [2056 + P * j for j in range(8)] + [1024 + P * j for j in range(8)]
UNITS, at = {}, 0
for l, n_in in ((0, len(ATT_COLS)), (1, len(REC_COLS))):
    for name, n in ((f"in{l}", n_in), (f"out{l}", 8), (f"up{l}", 2 * FT), (f"down{l}", FT), (f"ple{l}", 2), (f"gate{l}", 8)):
        UNITS[name] = at
        at += n
N_UNITS = at

AHEAD = 3


def attention_tasks():
    return [(fox, h, t) for fox in (True, False) for h in range(NH) for t in range(3)]


TASKS = attention_tasks()
SKEW_T, SKEW_V = 3, 5
HALF_AT = [0, 2, 4, 6, 8, 10, 12, 14, 16, 18, 19, 20]
TOK_AT = [1, 3, 5, 21, 22, 23]


def attention_events():
    out = []
    for i in range(len(TASKS) + SKEW_V):
        if i < len(TASKS):
            out.append(("scores", i))
        for n, at in enumerate(HALF_AT):
            if at == i:
                out.append(("half", 12 + n // 2, n % 2))
        if 0 <= i - SKEW_T < len(TASKS):
            out.append(("turn", i - SKEW_T))
        if 0 <= i - SKEW_V:
            out.append(("values", i - SKEW_V))
        for n, at in enumerate(TOK_AT):
            if at == i:
                out.append(("tok", 3 + n))
    return out


def recurrent_events():
    out = [("unit", 0), ("stats",), ("unit", 1), ("unit", 2), ("unit", 3), ("narrow",), ("unit", 4), ("unit", 5), ("gates",),
           ("unit", 6), ("sums",), ("unit", 7), ("arow",), ("unit", 8), ("spread",), ("unit", 9)]
    out += [("ktok", t) for t in range(3)]
    out += [("unit", 10), ("unit", 11), ("qk", 0), ("unit", 12), ("wT", 0), ("qk", 1), ("unit", 13), ("wT", 1), ("qk", 2),
            ("unit", 14), ("wT", 2), ("unit", 15), ("unit", 16), ("unit", 17)]
    for h in range(MH):
        halves = [("half", 18 + 2 * h + n // 2, n % 2) for n in range(4)] if h < MH - 1 else []
        out += [("vtok", h, t) for t in range(3)]
        for piece in (("chunk", h, 0), ("half",), ("chunk", h, 1), ("intra", h, 0), ("chunk", h, 2), ("half",), ("chunk", h, 3),
                      ("intra", h, 1), ("chunk", h, 4), ("intra", h, 2), ("half",), ("half",), ("heads", h)):
            if piece == ("half",):
                out += [halves.pop(0)] if halves else []
            else:
                out.append(piece)
    return out


def group_order():
    o = [("par", 0), ("par", 1)] + [("x", j) for j in range(KT)] + [("in0", i) for i in range(4)]
    o += [("par", 2), ("par", 3)] + [("pe", i) for i in range(4)] + [("cache", i) for i in range(5)]
    o += [("in0", 4), ("in0", 5), ("narrow0", 0)] + [("in0", i) for i in range(6, 12)] + [("tok", t) for t in range(3)]
    for e in attention_events():
        if e[0] == "half" and e[2] == 0:
            o.append(("in0", e[1]))
        elif e[0] == "values" and e[1] % 6 == 0:
            o.append(("o", e[1] // 6))
        elif e[0] == "tok":
            o.append(e)
    for l in range(2):
        if l:
            for e in recurrent_events():
                if e[0] == "unit" or (e[0] == "half" and e[2] == 0):
                    o.append(("in1", e[1]))
                elif e[0] == "narrow":
                    o.append(("narrow1", 0))
                elif e[0] == "ktok":
                    o.append(("ktok", e[1]))
                elif e[0] in ("vtok", "intra"):
                    o.append((e[0], 3 * e[1] + e[2]))
                elif e[0] == "heads":
                    o += [("heads", 2 * e[1]), ("heads", 2 * e[1] + 1)]
        o += [(f"out{l}", i) for i in range(8)] + [(f"up{l}", i) for i in range(2 * FT)]
        o += [(f"down{l}", 0), (f"cs{l}", 0)] + [(f"down{l}", i) for i in range(1, 8)] + [(f"ple{l}", i) for i in range(8)]
        o += [(f"gate{l}", i) for i in range(8 if l == 0 else 7)]
    return o + [("y", 0), ("y", 1), ("y", 2), ("gate1", 7), ("y", 3), ("y", 4), ("y", 5)]


GROUPS = {key: n for n, key in enumerate(group_order())}
assert len(GROUPS) == len(group_order())

NORMS = {f"{stage}{l}": 4 * l + i for l in range(2) for i, stage in enumerate(("mixpre", "mixpost", "ffnpre", "ffnpost"))}


def eights(stage, j):
    return 8 * (NORMS[stage] // 2) + j + 1


def encoder_step(nc, I, O):
    ctx = ExitStack()
    with ctx:
        def sb(name, shape, dt=F32):
            return ctx.enter_context(nc.sbuf_tensor(name, shape, dt))

        made = {}

        def sem(name):
            if name not in made:
                made[name] = ctx.enter_context(nc.semaphore(name))

            return made[name]

        ARENA = 2 * FT * T * 4
        arena = sb("arena", [P, ARENA // 4])
        nc_at = nc.alloc_sbuf_tensor_at
        base = nc.sbuf_base - ARENA
        FH = nc_at("hidden_hi", [P, FT, T], F32R, offset=base)
        FL = nc_at("hidden_lo", [P, FT, T], F32R, offset=base + FT * T * 4)
        scr0 = base + 8 * T * 4
        scr1 = base + FT * T * 4 + 24 * T * 4
        OH, OL = FH[:, 0:8, :], FL[:, 24:32, :]
        cursor = [scr0]

        def scratch(name, shape, dt=F32):
            n = 4
            for s in shape[1:]:
                n *= s
            a = cursor[0]
            cursor[0] += (n + 31) // 32 * 32
            assert cursor[0] <= scr1, (name, cursor[0] - scr1)
            return nc_at(name, shape, dt, offset=a)

        xtok = scratch("xtok", [P, 3, D])
        petok = scratch("petok", [P, 2, 3, 256])
        prow = scratch("prow", [P, 2, P])
        nrow = scratch("nrow", [P, 2, P])
        pef = scratch("pef", [P, 4, T])
        wnr = scratch("wnr", [P, 2, KT, 8])
        kcache = scratch("kcache", [P, 2, 512])
        startup_end = cursor[0]
        cursor[0] = scr0
        kcT = scratch("kcT", [P, 4, PAST])
        kcdup = scratch("kcdup", [P, 2, P])
        Ktok = scratch("Ktok", [P, 3, 512])
        Vtok = scratch("Vtok", [P, 3, 512])
        Stok = scratch("Stok", [P, 3, 256])
        Frow = scratch("Frow", [NH, TP + PAST + TS])
        lfz = scratch("lfz", [NH, 3, T])
        PT = scratch("PT", [P, 4, 384])
        cursor[0] = max(cursor[0], startup_end)
        kT = scratch("kT", [P, 4, T])
        kdup = scratch("kdup", [P, 2, T])
        kplain = scratch("kplain", [P, T])
        MFox = scratch("MFox", [P, 384])
        MSwa = scratch("MSwa", [P, 256])
        vcache = scratch("vcache", [P, 2, 512])
        kcs = scratch("kcs", [P, P])
        vcs = scratch("vcs", [P, P])
        clf = scratch("clf", [P, 2, NH])
        sinkb = scratch("sinkb", [P, NH])
        FrowR = scratch("FrowR", [104, TP + PAST + TS], F32R)
        selR = scratch("selR", [104, NH], F32R)
        S_sb = scratch("S_sb", [P, 6, T + 2])
        lftok = scratch("lftok", [P, 3, NH])
        Ftok = scratch("Ftok", [P, 3, NH])
        amax = scratch("amax", [P, 6, 1])
        aden = scratch("aden", [P, 6, 1])
        ainv = scratch("ainv", [P, 6, 1])
        cursor[0] = scr0
        sig = scratch("sig", [P, 8, T])
        Vaug = scratch("Vaug", [P, 2, 3, DV + 1])
        KmT = scratch("Ktok1", [P, 3, 512])
        Dm = scratch("Dm", [P, 3, MH, P])
        wT = scratch("wT", [P, 3, 512])
        C = scratch("C", [P, 2, MH, DV + 1])
        mz = scratch("mz", [8, 4, T])
        gt = scratch("gates_tok", [P, 3, 16])
        ml = {n: scratch("ml_" + n, [P, 3, MH]) for n in
              ("bt", "a", "M", "mp", "muL", "mu", "nmu", "sdec", "em", "g", "t0", "lf")}
        MF = scratch("MF", [P, 3, MH, 2])
        BL = scratch("BL", [P, 2, 12])
        mprev = scratch("mprev", [P, 6, MH])
        muc = scratch("muc", [P, 5, MH])
        scd = scratch("scd", [P, 5, MH])
        aT = scratch("aT", [12, P])
        Y = scratch("Y", [P, 2, 3, DV + 1])
        yf = {n: scratch("y_" + n, [P, 2, 3]) for n in ("den", "r", "ss", "v", "w", "f")}
        Ysq = scratch("Ysq", [P, DV])

        xT = sb("xT", [P, KT, T])
        hH = sb("hH", [P, KT, T], F32R)
        hL = sb("hL", [P, KT, T], F32R)
        mix = sb("mix", [P, KT, T])
        sqb = sb("sqb", [P, KT, T])
        raw = sb("raw", [P, R, D])
        wh = sb("wh", [P, R, D], F32R)
        wl = sb("wl", [P, R, D], F32R)
        gp = sb("gp", [P, 2, T + 4])
        cv = sb("cv", [P, 2, T + 2])
        us = sb("us", [P, 2, T])
        fb = sb("fb", [P, 2, T])
        obuf = fb
        diag = cv[:].rearrange("p s t -> p (s t)")[:, 0:3 * P].rearrange("p (t c) -> p t c", t=3)
        rstd = sb("rstd", [P, T])
        rstd2 = sb("rstd2", [P, T])
        PC = sb("PC", [P, 2, P])
        NC = sb("NC", [P, 2, P])
        cs = sb("cs", [P, 4, FT])
        csT = sb("csT", [P, P])
        peH = sb("peH", [P, 4, T], F32R)
        peL = sb("peL", [P, 4, T], F32R)
        wnH = sb("wnH", [P, 2, KT, 8], F32R)
        wnL = sb("wnL", [P, 2, KT, 8], F32R)
        ident = sb("ident", [P, P])
        ones = sb("ones", [P, P])
        Ut = sb("Ut", [P, P])
        Ub = sb("Ub", [P, P])
        MBlk = sb("MBlk", [P, P])
        cst = sb("cst", [P, 5])
        mark = sb("mark", [1, 1])
        ms = sb("ms", [P, 3])
        rcol = sb("rcol", [P, 3])
        bcol = sb("bcol", [8, 4])
        sgb = us

        bank = [ctx.enter_context(nc.psum_tensor(f"bank{i}", [P, 512], F32)) for i in range(8)]

        raw_landed = [sem(f"raw_landed{i}") for i in range(R)]
        hi_ready, lo_ready, unit_used = sem("hi_ready"), sem("lo_ready"), sem("unit_used")
        bank_done = [sem(f"bank_done{i}") for i in range(4)]

        def gid(name, i=0):
            return GROUPS[name, i]

        def gbank(g):
            return bank[g % 4]

        READ = {}

        def read_by(name, signal, n, first=1):
            for i in range(n):
                READ[gid(name, i)] = (signal, first + i)

        for name, signal, n in (("x", "x_in", 8), ("par", "par_in", 4), ("pe", "pe_f", 4), ("cache", "cache_read", 5), ("in0", "in_read0", 18),
                                ("narrow0", "narrow_step0", 1), ("tok", "tok_read", 9), ("o", "o_lo0", 8), ("in1", "in_read1", 24),
                                ("narrow1", "narrow_step1", 1), ("ktok", "ktok_read", 3), ("vtok", "vtok_read", 12), ("intra", "Y", 12),
                                ("heads", "mo_f", 8)):
            read_by(name, signal, n)
        for i in range(6):
            READ[gid("y", i)] = ("ytok", i + 1)
        for l in range(2):
            for name, signal, n in (("cs", "csT", 1), ("ple", "ple_sb", 8), ("gate", "sigm", 8)):
                read_by(f"{name}{l}", f"{signal}{l}", n)
            read_by(f"out{l}", "sq", 8, 8 * NORMS[f"mixpost{l}"] + 1)
            read_by(f"down{l}", "sq", 8, 8 * NORMS[f"ffnpost{l}"] + 1)
            for i in range(2 * FT):
                READ[gid(f"up{l}", i)] = (("us" if i % 2 else "gp") + str(l), i // 2 + 1)

        FULL, uses = {}, [0] * 4
        for l in range(2):
            for i in range(len(ATT_COLS) if l == 0 else len(REC_COLS)):
                FULL[gid(f"in{l}", i)] = (unit_used, UNITS[f"in{l}"] + i + 1)
            for i in range(8):
                FULL[gid(f"out{l}", i)] = (unit_used, UNITS[f"out{l}"] + i + 1)
                FULL[gid(f"down{l}", i)] = (unit_used, UNITS[f"down{l}"] + 4 * i + 4)
                FULL[gid(f"gate{l}", i)] = (unit_used, UNITS[f"gate{l}"] + i + 1)
            for i in range(2 * FT):
                FULL[gid(f"up{l}", i)] = (unit_used, UNITS[f"up{l}"] + i + 1)
            for i in (3, 7):
                FULL[gid(f"ple{l}", i)] = (unit_used, UNITS[f"ple{l}"] + i // 4 + 1)
        for i in range(8):
            FULL[gid("o", i)] = (sem("pv_done"), 6 * (i + 1))
        for gi in range(len(GROUPS)):
            if gi not in FULL:
                uses[gi % 4] += 1
                FULL[gi] = (bank_done[gi % 4], uses[gi % 4])

        def bank_free(eng, g):
            if g >= 4:
                name, value = READ[g - 4]
                eng.wait_ge(sem(name), value)

        def bank_full(eng, g, it=0):
            signal, value = FULL[g]
            eng.wait_ge(signal, value + it)

        def copy_y(eng, i):
            half, t = i // 3, i % 3
            gi, n = gid("y", i), TOK[t][1]
            bank_full(eng, gi)
            dst, src = xtok[0:n, t, half * 512:(half + 1) * 512], gbank(gi)[0:n, :]
            if i in (3, 5):
                nc.vector.tensor_copy(dst, src).then_inc(sem("ytok_v"), 1)
            else:
                nc.scalar.activation(dst, src, ACT.Copy).then_inc(sem("ytok"), 1)

        def x_added(eng, stage, j):
            eng.wait_ge(sem("x_odd" if j % 2 else "x_even"), 4 * (NORMS[stage] // 2) + j // 2 + 1)

        def score_width(i):
            fox, h, t = TASKS[i]
            return TOK[t][0] + P if fox and t < 2 else PAST + TS if fox else TOK[t][0] + P + 1 if t < 2 else P + TS + 1

        block = ctx.enter_context(nc.Block())

        @block.sync
        def _(sp):
            sp.dma_start(xtok[:, 0, :], I["x_prompt"][0, 0:P]).then_inc(sem("ld_x"), 16)
            sp.dma_start(xtok[:, 1, :], I["x_prompt"][0, P:TP]).then_inc(sem("ld_x"), 16)
            sp.dma_start(xtok[0:TS, 2, :], I["x_sample"][0]).then_inc(sem("ld_x"), 16)

            def col_unit(w, c):
                return w[:, c:c + P].rearrange("(k p) c -> p k c", p=P)

            def load(u, src):
                if u >= R:
                    sp.wait_ge(lo_ready, u - R + 1)
                dst = raw[:, u % R, :].rearrange("p (k c) -> p k c", k=src.shape[1])
                sp.dma_start(dst, src).then_inc(raw_landed[u % R], 16)

            for l in range(2):
                w_in, cols, w_out = (I["w_att_in"], ATT_COLS, I["w_att_out"]) if l == 0 else (I["w_rec_in"], REC_COLS, I["w_rec_out"])
                for i, c in enumerate(cols):
                    load(UNITS[f"in{l}"] + i, col_unit(w_in[0], c))
                for i in range(8):
                    load(UNITS[f"out{l}"] + i, col_unit(w_out[0], i * P))
                u0 = UNITS[f"up{l}"]
                with sp.Fori(0, FT // 2) as it:
                    for s in range(4):
                        u = u0 + s
                        sp.wait_ge(lo_ready, it * 4 + (u - R + 1))
                        c = it * (2 * P) + (s // 2) * P + (s % 2) * FF
                        src = I["w_ffn_up"][l][:, bass.ds(c, P)].rearrange("(k p) c -> p k c", p=P)
                        dst = raw[:, u % R, :].rearrange("p (k c) -> p k c", k=KT)
                        sp.dma_start(dst, src).then_inc(raw_landed[u % R], 16)
                u0 = UNITS[f"down{l}"]
                with sp.Fori(0, KT) as it:
                    for s in range(4):
                        u = u0 + s
                        sp.wait_ge(lo_ready, it * 4 + (u - R + 1))
                        src = I["w_ffn_down"][l][s * D:(s + 1) * D, bass.ds(it * P, P)].rearrange("(k p) c -> p k c", p=P)
                        dst = raw[:, u % R, :].rearrange("p (k c) -> p k c", k=KT)
                        sp.dma_start(dst, src).then_inc(raw_landed[u % R], 16)
                for i in range(2):
                    load(UNITS[f"ple{l}"] + i, I["w_ple"][l][:, i * 512:(i + 1) * 512].rearrange("(k p) c -> p k c", p=P))
                for i in range(8):
                    load(UNITS[f"gate{l}"] + i, col_unit(I["w_ple_gate"][l], i * P))

            def store_y(t, half):
                n = TOK[t][1]
                dst = O["y_prompt"][0, t * P:t * P + P] if t < 2 else O["y_sample"][0]
                c = slice(half * 512, (half + 1) * 512)
                sp.dma_start(dst[:, c], xtok[0:n, t, c]).then_inc(sem("y_stored"), 16)

            for t in range(3):
                sp.wait_ge(sem("ytok"), t + 1)
                store_y(t, 0)
            for t, signal, value in ((0, "ytok_v", 1), (1, "ytok", 4), (2, "ytok_v", 2)):
                sp.wait_ge(sem(signal), value)
                store_y(t, 1)
            sp.wait_ge(sem("y_stored"), 16 * 6)

        @block.gpsimd
        def _(pool):
            g = nc.gpsimd
            ch = sem("const_step")
            n = [0]

            def link(ins):
                n[0] += 1
                ins.then_inc(ch, 1)
                pool.wait_ge(ch, n[0])

            link(g.memset(ident[:], 0.0))
            link(g.affine_select(out=ident[:], in_=ident[:], compare_op=ALU.not_equal, fill=1.0, base=0,
                                 pattern=[[-1, P]], channel_multiplier=1))
            g.memset(mark[:], 0.0)
            g.memset(cst[:, 2:5], -0.5)
            link(g.memset(cst[:, 1:2], 1.0))
            g.memset(ones[:], 1.0).then_inc(sem("const"), 1)
            par, ld_pe, ld_cache = sem("ld_par1"), sem("ld_pe"), sem("ld_cache")
            pool.dma_start(prow[0:96, 1, :], I["ffn_conv_w"][1].rearrange("t (j c) -> (t j) c", c=P)).then_inc(par, 16)
            pool.dma_start(prow[96:128, 1, :], I["ffn_conv_b"][1].rearrange("(j c) -> j c", c=P)).then_inc(par, 16)
            pool.dma_start(nrow[0:64, 1, :], I["state_ffn_conv"][1, 0].rearrange("r (j c) -> (r j) c", c=P)).then_inc(par, 16)
            for i, nm in enumerate(("ln_mix_pre", "ln_mix_post", "ln_ffn_pre", "ln_ffn_post")):
                pool.dma_start(nrow[64 + 8 * i:72 + 8 * i, 1, :], I[nm][1].rearrange("(j c) -> j c", c=P)).then_inc(par, 16)
            pool.dma_start(nrow[96:104, 1, :], I["rec_norm"][0].rearrange("(j c) -> j c", c=P)).then_inc(par, 16)
            for l in range(2):
                pool.dma_start(petok[:, l, 0:2, :], I["p_prompt"][l, 0].rearrange("(t p) d -> p t d", p=P)).then_inc(ld_pe, 16)
                pool.dma_start(petok[0:TS, l, 2, :], I["p_sample"][l, 0]).then_inc(ld_pe, 16)
            pool.dma_start(kcache[:], I["cache_fox_k"][0, 0].rearrange("(t p) h d -> p t (h d)", p=P)).then_inc(ld_cache, 16)
            pool.dma_start(vcache[:], I["cache_fox_v"][0, 0].rearrange("(t p) h d -> p t (h d)", p=P)).then_inc(ld_cache, 16)
            pool.dma_start(kcs[:], I["cache_swa_k"][0, 0].rearrange("p h d -> p (h d)")).then_inc(ld_cache, 16)
            pool.dma_start(vcs[:], I["cache_swa_v"][0, 0].rearrange("p h d -> p (h d)")).then_inc(ld_cache, 16)
            pool.dma_start(clf[:], I["cache_fox_logf"][0, 0].rearrange("(t p) h -> p t h", p=P)).then_inc(ld_cache, 16)
            pool.dma_start(sinkb[:], I["swa_sink"][0:1, :].to_broadcast([P, NH])).then_inc(ld_cache, 16)
            pool.dma_start(bcol[:, 0:1], I["fox_fb"].rearrange("a h -> h a"), allow_slow_non_contiguous=True).then_inc(ld_cache, 16)
            pool.dma_start(bcol[0:4, 1:2], I["rec_ig_b"].rearrange("a h -> h a"), allow_slow_non_contiguous=True).then_inc(ld_cache, 16)
            pool.dma_start(bcol[4:8, 1:2], I["rec_fg_b"].rearrange("a h -> h a"), allow_slow_non_contiguous=True).then_inc(ld_cache, 16)
            link(g.memset(Ut[:], 1.0))
            link(g.affine_select(out=Ut[:], in_=Ut[:], compare_op=ALU.is_ge, fill=0.0, base=0, pattern=[[1, P]], channel_multiplier=-1))
            link(g.tensor_copy(Ub[:], Ut[:]))
            link(g.memset(Ub[0:64, 64:128], 0.0))
            link(g.memset(MFox[:], 0.0))
            link(g.affine_select(out=MFox[:, 256:384], in_=MFox[:, 256:384], compare_op=ALU.is_ge, fill=NEG, base=0,
                                 pattern=[[-1, P]], channel_multiplier=1))
            link(g.tensor_copy(MBlk[:], MFox[:, 256:384]))
            link(g.memset(MBlk[64:128, 0:64], NEG))
            link(g.memset(MSwa[:], 0.0))
            link(g.memset(MSwa[64:128, 0:64], NEG))
            link(g.memset(MSwa[0:64, 192:256], NEG))
            link(g.memset(FrowR[:].bitcast(F32), 0.0))
            link(g.memset(selR[:].bitcast(F32), 0.0))
            g.memset(gp[:], 0.0).then_inc(sem("const2"), 1)

            st = sem("stored")
            n_st = [0]

            def store(dst, src, short_rows=False):
                pool.dma_start(dst, src, allow_slow_non_contiguous=short_rows).then_inc(st, 16)
                n_st[0] += 1

            def inverse_rms(stage):
                pool.wait_ge(sem("ms"), NORMS[stage] + 1)
                g.tensor_tensor(rcol[:], ms[:], cst[:, 2:5], ALU.pow).then_inc(sem("rcol"), 1)

            def post_odd(stage):
                inverse_rms(stage)
                pool.wait_ge(sem("rstd"), NORMS[stage] + 1)
                for j in range(1, KT, 2):
                    k = 4 * (NORMS[stage] // 2) + j // 2 + 1
                    g.tensor_tensor(mix[:, j, :], mix[:, j, :], rstd2[:], ALU.mult).then_inc(sem("post_odd"), 1)
                    pool.wait_ge(sem("post_odd"), k)
                    g.tensor_tensor(xT[:, j, :], xT[:, j, :], mix[:, j, :], ALU.add).then_inc(sem("x_odd"), 1)

            inverse_rms("mixpre0")
            for l in range(2):
                if l == 0:
                    pool.wait_ge(ld_cache, 16 * 9)
                    store(O["s_swa_k"][0, 0, 0:64].rearrange("p h d -> p (h d)"), kcs[64:128, :])
                    store(O["s_swa_v"][0, 0, 0:64].rearrange("p h d -> p (h d)"), vcs[64:128, :])
                    pool.wait_ge(sem("lf_tok"), 1)
                    store(O["p_fox_logf"][0, 0].rearrange("(t p) h -> p t h", p=P), lftok[:, 0:2, :])
                    store(O["s_fox_logf"][0, 0], lftok[0:TS, 2, :])
                    for i in range(len(TASKS)):
                        n_q, w, b = TOK[TASKS[i][2]][1], score_width(i), i % 6
                        pool.wait_ge(sem("a_inv"), i + 1)
                        g.tensor_scalar(S_sb[0:n_q, b, 0:w], S_sb[0:n_q, b, 0:w], ainv[0:n_q, b, :], None, ALU.mult).then_inc(sem("p_ready"), 1)
                    pool.wait_ge(sem("tok_read"), 9)
                    for nm, tt in (("k", Ktok), ("v", Vtok)):
                        store(O[f"p_fox_{nm}"][0, 0].rearrange("(t p) h d -> p t (h d)", p=P), tt[:, 0:2, :])
                        store(O[f"s_fox_{nm}"][0, 0].rearrange("p h d -> p (h d)"), tt[0:TS, 2, :])
                    for i, nm in enumerate(("k", "v")):
                        store(O[f"p_swa_{nm}"][0, 0].rearrange("p h d -> p (h d)"), Stok[:, 1, i * P:(i + 1) * P])
                        store(O[f"s_swa_{nm}"][0, 0, 64:128].rearrange("p h d -> p (h d)"), Stok[0:TS, 2, i * P:(i + 1) * P])
                else:
                    signal, value = FULL[gid("gate0", 7)]
                    pool.wait_ge(signal, value)
                    pool.dma_start(C[:, 1, :, 0:DV], I["state_mlstm_c"][0, 0].rearrange("h k v -> k h v")).then_inc(sem("ld_state"), 16)
                    pool.dma_start(C[:, 1, :, DV:DV + 1], I["state_mlstm_n"][0, 0].rearrange("h (k a) -> k h a", a=1),
                                   allow_slow_non_contiguous=True).then_inc(sem("ld_state"), 16)
                    pool.dma_start(mprev[:, 4, :], I["state_mlstm_m"][0].to_broadcast([P, MH])).then_inc(sem("ld_state"), 16)
                    inverse_rms("mixpre1")
                    for h in range(MH):
                        pool.wait_ge(sem("Yvar"), h + 1)
                        g.tensor_tensor(yf["w"][:, h % 2, :], yf["v"][:, h % 2, :], cst[:, 2:5], ALU.pow).then_inc(sem("Yroot"), 1)
                    pool.wait_ge(sem("C_new"), 20)
                    for b, pre in ((0, "p"), (1, "s")):
                        store(O[f"{pre}_ml_c"][0, 0].rearrange("h k v -> k h v"), C[:, b, :, 0:DV])
                        store(O[f"{pre}_ml_n"][0, 0].rearrange("h (k a) -> k h a", a=1), C[:, b, :, DV:DV + 1], True)
                    store(O["p_ml_m"][0], mprev[0:1, 5, :])
                    store(O["s_ml_m"][0], mz[0:1, 3, 0:4])
                post_odd(f"mixpost{l}")
                inverse_rms(f"ffnpre{l}")
                pool.wait_ge(st, 16 * n_st[0])
                pool.sem_inc(sem(f"scratch_out{l}"), 1)
                with pool.Fori(0, FT // 2) as it:
                    for s in range(2):
                        pool.wait_ge(sem(f"gelu{l}"), it * 2 + (s + 1))
                        pool.wait_ge(sem(f"us{l}"), it * 2 + (s + 1))
                        g.tensor_tensor(fb[:, s, 0:TP], cv[:, s, 0:TP], us[:, s, 0:TP], ALU.mult)
                        g.tensor_tensor(fb[:, s, TP:T], cv[:, s, TP + 2:T + 2], us[:, s, TP:T], ALU.mult)
                        tail = gp[:, s, 192:324].rearrange("p (b r) -> p b r", b=2)[:, :, 64:66]
                        dst = cs[:, :, bass.ds(it * 2 + s, 1)].rearrange("p (b r) j -> p b (r j)", b=2)
                        g.tensor_copy(dst, tail).then_inc(sem(f"f{l}"), 1)
                pool.wait_ge(sem(f"csT{l}"), 1)
                store(O["p_conv"][l, 0].rearrange("r (j c) -> (r j) c", c=P), csT[0:64, :])
                store(O["s_conv"][l, 0].rearrange("r (j c) -> (r j) c", c=P), csT[64:128, :])
                post_odd(f"ffnpost{l}")
                pool.wait_ge(st, 16 * n_st[0])

        @block.tensor
        def _(pe):
            mmul = nc.tensor.matmul
            trans = nc.tensor.transpose

            def block3(u, k, out, rh, rl, first, last):
                a, b = wh[:, u % R, k * P:(k + 1) * P], wl[:, u % R, k * P:(k + 1) * P]
                mmul(out, a, rh[:, k, :], start=first and k == 0, stop=False)
                mmul(out, a, rl[:, k, :], start=False, stop=False)
                m = mmul(out, b, rh[:, k, :], start=False, stop=last and k == 7)
                if k == 7:
                    m.then_inc(unit_used, 1)

            def unit(u, out, rh, rl, first=True, last=True, hook=None, it=0, ks=range(8)):
                if 0 in ks:
                    pe.wait_ge(lo_ready, it + (u + 1))
                for k in ks:
                    if hook:
                        hook(k)
                    block3(u, k, out, rh, rl, first, last)

            def ahead(us, gs, rh, rl, k_wait, stage=None):
                for gi in gs:
                    bank_free(pe, gi)
                pe.wait_ge(lo_ready, us[-1] + 1)
                for k in range(8):
                    k_wait(k)
                    for u, gi in zip(us, gs):
                        block3(u, k, gbank(gi)[:, 0:T], rh, rl, True, True)
                    if stage:
                        stats(stage, k)

            def stats(stage, j):
                pe.wait_ge(sem("sq"), 8 * NORMS[stage] + j + 1)
                for t, c in enumerate((0, P, T - P)):
                    m = mmul(bank[4][:, t:t + 1], sqb[:, j, c:c + P], ones[:, 0:1], start=j == 0 and t == 0, stop=j == KT - 1,
                             skip_group_check=True)
                if j == KT - 1:
                    m.then_inc(sem("sq_sum"), 1)

            def spread_rms(stage):
                pe.wait_ge(sem("diag"), NORMS[stage] + 1)
                mmul(bank[5][:, 0:P], ones[:], diag[:, 0, :], start=True, stop=True)
                mmul(bank[5][:, P:2 * P], ones[:], diag[:, 1, :], start=True, stop=True)
                mmul(bank[5][:, TP:T], ones[:], diag[:, 2, 64:128], start=True, stop=True).then_inc(sem("rms_rows"), 1)

            def rms_at(stage, at):
                return lambda k: spread_rms(stage) if k == at else None

            def turn_rows(gi, n_rows, src, col):
                for t, (t0, n) in enumerate(TOK):
                    m = trans(gbank(gi)[:, t0:t0 + n], src(t, n)[:, col * P:(col + 1) * P], ident[0:n, 0:n])
                m.then_inc(bank_done[gi % 4], 1)

            pe.wait_ge(sem("const"), 1)
            pe.wait_ge(sem("const_step"), 3)

            def parameters(l):
                pe.wait_ge(sem(f"ld_par{l}"), 16 * (7 + l))
                for i, (rows, n) in enumerate(((prow, P), (nrow, 96 + 8 * l))):
                    gi = gid("par", 2 * l + i)
                    bank_free(pe, gi)
                    trans(gbank(gi)[:, 0:n], rows[0:n, l, :], ident[0:n, 0:n]).then_inc(bank_done[gi % 4], 1)

            parameters(0)
            pe.wait_ge(sem("ld_x"), 48)
            for j in range(KT):
                gi = gid("x", j)
                bank_free(pe, gi)
                turn_rows(gi, T, lambda t, n: xtok[0:n, t, :], j)

            def narrow(l):
                gi = gid(f"narrow{l}", 0)
                bank_free(pe, gi)
                pe.wait_ge(sem("narrow_split"), 1)
                out = gbank(gi)[0:8, 0:T]
                for k in range(KT):
                    mmul(out, wnH[:, l, k, :], hH[:, k, :], start=k == 0, stop=False)
                    mmul(out, wnH[:, l, k, :], hL[:, k, :], start=False, stop=False)
                    m = mmul(out, wnL[:, l, k, :], hH[:, k, :], start=False, stop=k == KT - 1)
                m.then_inc(bank_done[gi % 4], 1)

            def in_unit(l, i, hook=None, ks=range(8)):
                gi = gid(f"in{l}", i)
                if 0 in ks:
                    bank_free(pe, gi)
                unit(UNITS[f"in{l}"] + i, gbank(gi)[:, 0:T], hH, hL, hook=hook, ks=ks)

            def input_attention():
                ahead([UNITS["in0"] + i for i in range(AHEAD)], [gid("in0", i) for i in range(AHEAD)], hH, hL,
                      lambda k: pe.wait_ge(sem("h_lo"), eights("mixpre0", k)), "mixpre0")
                in_unit(0, 3, rms_at("mixpre0", 3))
                parameters(1)
                pe.wait_ge(sem("ld_pe"), 64)
                for i in range(4):
                    gi = gid("pe", i)
                    bank_free(pe, gi)
                    turn_rows(gi, T, lambda t, n: petok[0:n, i // 2, t, :], i % 2)
                pe.wait_ge(sem("ld_cache"), 16 * 9)
                for j in range(5):
                    gi = gid("cache", j)
                    bank_free(pe, gi)
                    for t in range(2 if j < 4 else 1):
                        m = trans(gbank(gi)[:, t * P:(t + 1) * P], kcache[:, t, j * P:(j + 1) * P] if j < 4 else kcs[:], ident[:])
                    m.then_inc(bank_done[gi % 4], 1)
                for i in range(4, 12):
                    in_unit(0, i)
                    if i == 5:
                        narrow(0)
                    elif i == 7:
                        turn_forget()
                    elif i == 9:
                        sum_forget()
                for t in range(3):
                    turn_tok(t)
                pe.wait_ge(sem("F_rows"), 1)
                for e in attention_events():
                    if e[0] == "scores":
                        scores(e[1])
                    elif e[0] == "half":
                        in_unit(0, e[1], ks=range(4 * e[2], 4 * e[2] + 4))
                    elif e[0] == "tok":
                        turn_tok(e[1])
                    elif e[0] == "turn":
                        turn(e[1])
                    else:
                        values(e[1])

            def turn_forget():
                pe.wait_ge(sem("lf_ready"), 1)
                for t, (t0, n) in enumerate(TOK):
                    m = trans(bank[5][0:n, t * 8:t * 8 + 8], lfz[:, 0, t0:t0 + n], ident[0:8, 0:8])
                m.then_inc(sem("lf_tr"), 1)

            def sum_forget():
                pe.wait_ge(sem("const2"), 1)
                pe.wait_ge(sem("lf_tok"), 1)
                L = [lftok[:, 0, :], lftok[:, 1, :], lftok[0:64, 2, :]]
                Cc = [clf[:, 0, :], clf[:, 1, :]]
                U, N1 = Ut[:], ones[:]

                def run_sum(out, terms):
                    for i, (a, b) in enumerate(terms):
                        m = mmul(out, a, b, start=i == 0, stop=i == len(terms) - 1)
                    return m

                run_sum(bank[6][:, 0:8], [(U, L[0])])
                run_sum(bank[6][:, 8:16], [(N1, L[0]), (U, L[1])])
                run_sum(bank[6][0:64, 16:24], [(N1[:, 0:64], Cc[0]), (N1[:, 0:64], Cc[1]), (Ut[0:64, 0:64], L[2])])
                run_sum(bank[7][0:8, 0:128], [(L[0], U)])
                run_sum(bank[7][0:8, 128:256], [(L[0], N1), (L[1], U)])
                run_sum(bank[5][0:8, 0:128], [(Cc[0], U)])
                run_sum(bank[5][0:8, 128:256], [(Cc[0], N1), (Cc[1], U)])
                run_sum(bank[5][0:8, 256:320], [(Cc[0], N1[:, 0:64]), (Cc[1], N1[:, 0:64]), (L[2], Ut[0:64, 0:64])]).then_inc(sem("F_sums"), 1)

            def turn_tok(i):
                kind, t = i // 3, i % 3
                t0, n = TOK[t]
                gi = gid("tok", i)
                bank_free(pe, gi)
                pe.wait_ge(sem("in_read0"), 12 if kind < 2 else 18)
                srcs = [(sqb, kT)[kind][:, j, t0:t0 + n] for j in range(4)] if kind < 2 else [kplain[:, t0:t0 + n], sqb[:, 4, t0:t0 + n]]
                for j, s in enumerate(srcs):
                    m = trans(gbank(gi)[0:n, j * P:(j + 1) * P], s, ident[:])
                m.then_inc(bank_done[gi % 4], 1)

            def scores(i):
                fox, h, t = TASKS[i]
                t0, n = TOK[t]
                hf = 64 * (h % 2)
                if not fox:
                    pe.wait_ge(sem("in_read0"), 18)
                if i >= 2:
                    pe.wait_ge(sem("s_moved"), i - 1)
                b = bank[4 + i % 2]
                q = mix[hf:hf + 64, (0 if fox else 4) + h // 2, t0:t0 + n]
                if fox and t < 2:
                    segs = [(kT[hf:hf + 64, h // 2, 0:t0 + n], 0, 0)]
                elif fox:
                    segs = [(kcT[hf:hf + 64, h // 2, :], 0, TP), (kT[hf:hf + 64, h // 2, TP:T], PAST, TP + PAST)]
                elif t < 2:
                    segs = [(kdup[hf:hf + 64, h // 4, 0:t0 + n], 0, None)]
                else:
                    segs = [(kcdup[hf:hf + 64, h // 4, :], 0, None), (kdup[hf:hf + 64, h // 4, TP:T], P, None)]
                for k, off, fr in segs:
                    w = k.shape[1]
                    m = mmul(b[0:n, off:off + w], q, k, start=True, stop=fr is None)
                    if fr is not None:
                        m = mmul(b[0:n, off:off + w], selR[hf:hf + 40, h:h + 1].to_broadcast([40, n]), FrowR[hf:hf + 40, fr:fr + w], start=False, stop=True)
                m.then_inc(sem("s_done"), 1)

            def blocks(i):
                fox, h, t = TASKS[i]
                c = h * 64 if fox else (h // 4) * 64
                V = Vtok if fox else Stok[:, :, P:2 * P]
                if t < 2:
                    return [(P, V[:, b, c:c + 64]) for b in range(t + 1)]
                if fox:
                    return [(P, vcache[:, b, c:c + 64]) for b in range(2)] + [(64, V[0:64, 2, c:c + 64])]
                return [(P, vcs[:, c:c + 64]), (64, V[0:64, 2, c:c + 64])]

            def turn(i):
                n = TOK[TASKS[i][2]][1]
                pe.wait_ge(sem("p_ready"), i + 1)
                if i >= 2:
                    pe.wait_ge(sem("pt_moved"), i - 1)
                for b, (rows, _) in enumerate(blocks(i)):
                    m = trans(bank[6 + i % 2][0:rows, b * P:b * P + n], S_sb[0:n, i % 6, b * P:b * P + rows], ident[0:n, 0:n])
                m.then_inc(sem("pt_done"), 1)

            def values(i):
                fox, h, t = TASKS[i]
                t0, n = TOK[t]
                gi = gid("o", i // 6)
                if i % 6 == 0:
                    bank_free(pe, gi)
                if i == 0:
                    pe.wait_ge(sem("tok_read"), 3)
                if i == 24:
                    pe.wait_ge(sem("tok_read"), 9)
                pe.wait_ge(sem("pt_moved"), i + 1)
                hf = 64 * (h % 2)
                bl = blocks(i)
                for b, (rows, v) in enumerate(bl):
                    m = mmul(gbank(gi)[hf:hf + 64, t0:t0 + n], v, PT[0:rows, i % 4, b * P:b * P + n], start=b == 0, stop=b == len(bl) - 1)
                m.then_inc(sem("pv_done"), 1)

            def input_recurrent():
                for e in recurrent_events():
                    name, a = e[0], e[1:]
                    if name == "unit":
                        in_unit(1, a[0], (lambda k: pe.wait_ge(sem("h_lo"), eights("mixpre1", k))) if a[0] == 0 else
                                rms_at("mixpre1", 3) if a[0] == 1 else None)
                    elif name == "half":
                        in_unit(1, a[0], ks=range(4 * a[1], 4 * a[1] + 4))
                    elif name == "stats":
                        for j in range(KT):
                            stats("mixpre1", j)
                    elif name == "narrow":
                        narrow(1)
                    elif name == "gates":
                        pe.wait_ge(sem("mgates"), 1)
                        for t, (t0, n) in enumerate(TOK):
                            trans(bank[5][0:n, t * 16:t * 16 + 8], mz[:, 0, t0:t0 + n], ident[0:8, 0:8])
                            m = trans(bank[5][0:n, t * 16 + 8:t * 16 + 16], mz[:, 1, t0:t0 + n], ident[0:8, 0:8])
                        m.then_inc(sem("mgates_tr"), 1)
                    elif name == "sums":
                        pe.wait_ge(sem("mlf"), 1)
                        lf = ml["lf"][:].rearrange("p t h -> p (t h)")
                        mmul(bank[6][:, 0:12], Ub[:], lf, start=True, stop=True)
                        mmul(bank[6][:, 16:28], ones[0:64, :], lf[0:64, :], start=True, stop=True)
                        mmul(bank[7][:, 32:44], ones[64:128, :], lf[64:128, :], start=True, stop=True).then_inc(sem("msums"), 1)
                    elif name == "arow":
                        pe.wait_ge(sem("ma"), 1)
                        trans(bank[7][0:12, 0:P], ml["a"][:].rearrange("p t h -> p (t h)"), ident[:]).then_inc(sem("maT"), 1)
                    elif name == "spread":
                        pe.wait_ge(sem("maT_read"), 1)
                        for t in range(3):
                            for h in range(MH):
                                r = 4 * t + h
                                m = mmul(bank[5 + t][:, h * P:(h + 1) * P], ident[0:12, r:r + 1].to_broadcast([12, P]), aT[:], start=True, stop=True)
                            m.then_inc(sem("mspread"), 1)
                    elif name == "ktok":
                        t0, n = TOK[a[0]]
                        gi = gid("ktok", a[0])
                        bank_free(pe, gi)
                        pe.wait_ge(sem("in_read1"), 8)
                        for j in range(4):
                            m = trans(gbank(gi)[0:n, j * P:(j + 1) * P], mix[:, 4 + j, t0:t0 + n], ident[:])
                        m.then_inc(bank_done[gi % 4], 1)
                    elif name == "qk":
                        t = a[0]
                        t0, n = TOK[t]
                        pe.wait_ge(sem("in_read1"), 8)
                        if t:
                            pe.wait_ge(sem("mw"), t)
                        for h in range(MH):
                            m = mmul(bank[4][0:n, h * P:h * P + n], mix[:, h, t0:t0 + n], mix[:, 4 + h, t0:t0 + n], start=True, stop=True)
                        m.then_inc(sem("mqk"), 1)
                    elif name == "wT":
                        t = a[0]
                        n = TOK[t][1]
                        pe.wait_ge(sem("mw"), t + 1)
                        if t:
                            pe.wait_ge(sem("mwT_read"), t)
                        for h in range(MH):
                            m = trans(bank[5][0:n, h * P:h * P + n], Dm[0:n, t, h, 0:n], ident[0:n, 0:n])
                        m.then_inc(sem("mwT"), 1)
                    elif name == "vtok":
                        h, t = a
                        t0, n = TOK[t]
                        gi = gid("vtok", 3 * h + t)
                        bank_free(pe, gi)
                        pe.wait_ge(sem("in_read1"), 18 + 2 * h)
                        for v in range(2):
                            m = trans(gbank(gi)[0:n, v * P:(v + 1) * P], sqb[:, 2 * h + v, t0:t0 + n], ident[:])
                        m.then_inc(bank_done[gi % 4], 1)
                    elif name == "chunk":
                        h, c = a
                        t, r0, s, k = c // 2, 64 * (c % 2), c // 4, 5 * a[0] + a[1]
                        t0 = TOK[t][0] + r0
                        if k == 0:
                            pe.wait_ge(sem("C_init"), 1)
                            pe.wait_ge(sem("Kg"), 12)
                        else:
                            pe.wait_ge(sem("C_new"), k)
                            pe.wait_ge(sem("inter_read"), k)
                        mmul(bank[6][r0:r0 + 64, 0:DV + 1], mix[:, h, t0:t0 + 64], C[:, s, h, :], start=True, stop=True).then_inc(sem("inter_done"), 1)
                        if c == 0:
                            pe.wait_ge(sem("vtok_read"), 3 * h + 3)
                        mmul(bank[7][:, 0:DV + 1], KmT[r0:r0 + 64, t, h * P:(h + 1) * P], Vaug[r0:r0 + 64, h % 2, t, :],
                             start=True, stop=True).then_inc(sem("C_add"), 1)
                    elif name == "intra":
                        h, t = a
                        n = TOK[t][1]
                        gi = gid("intra", 3 * h + t)
                        bank_free(pe, gi)
                        pe.wait_ge(sem("mwT_read"), 3)
                        mmul(gbank(gi)[0:n, 0:DV + 1], wT[0:n, t, h * P:h * P + n], Vaug[0:n, h % 2, t, :], start=True, stop=True)\
                            .then_inc(bank_done[gi % 4], 1)
                    elif name == "heads":
                        h = a[0]
                        pe.wait_ge(sem("Yn"), 3 * h + 3)
                        for v in range(2):
                            gi = gid("heads", 2 * h + v)
                            bank_free(pe, gi)
                            turn_rows(gi, T, lambda t, n: Y[0:n, h % 2, t, 0:DV], v)

            for l in range(2):
                if l == 0:
                    input_attention()
                else:
                    input_recurrent()
                for i in range(8):
                    gi = gid(f"out{l}", i)
                    bank_free(pe, gi)
                    unit(UNITS[f"out{l}"] + i, gbank(gi)[:, 0:T], OH, OL,
                         hook=(lambda k: pe.wait_ge(sem(f"o_lo{l}"), k + 1)) if i == 0 else None)
                    if i >= 1:
                        stats(f"mixpost{l}", i - 1)
                stats(f"mixpost{l}", 7)
                spread_rms(f"mixpost{l}")
                u0, g0 = UNITS[f"up{l}"], gid(f"up{l}", 0)
                ahead(range(u0, u0 + AHEAD), range(g0, g0 + AHEAD), hH, hL,
                      lambda k: pe.wait_ge(sem("h_lo"), eights(f"ffnpre{l}", k)), f"ffnpre{l}")
                bank_free(pe, g0 + 3)
                unit(u0 + 3, gbank(g0 + 3)[:, 0:T], hH, hL, hook=rms_at(f"ffnpre{l}", 3))
                with pe.Fori(1, FT // 2) as it:
                    for s in range(4):
                        gi = g0 + s
                        pe.wait_ge(sem(("us" if s % 2 else "gp") + str(l)), it * 2 + (s // 2 - 1))
                        unit(u0 + s, gbank(gi)[:, 0:T], hH, hL, it=it * 4)
                u0 = UNITS[f"down{l}"]
                for i in range(8):
                    gi = gid(f"down{l}", i)
                    bank_free(pe, gi)
                    for q in range(4):
                        unit(u0 + 4 * i + q, gbank(gi)[:, 0:T], FH[:, 8 * q:8 * q + 8, :], FL[:, 8 * q:8 * q + 8, :], q == 0, q == 3,
                             hook=(lambda k: pe.wait_ge(sem(f"f_lo{l}"), 8 * q + k + 1)) if i == 0 else None)
                        if q == 1 and i >= 1:
                            stats(f"ffnpost{l}", i - 1)
                    if i == 0:
                        gi = gid(f"cs{l}", 0)
                        bank_free(pe, gi)
                        trans(gbank(gi)[:, 0:P], cs[:].rearrange("p a j -> p (a j)"), ident[:]).then_inc(bank_done[gi % 4], 1)
                stats(f"ffnpost{l}", 7)
                for i in range(8):
                    if i == 3:
                        spread_rms(f"ffnpost{l}")
                    gi = gid(f"ple{l}", i)
                    bank_free(pe, gi)
                    u = UNITS[f"ple{l}"] + i // 4
                    pe.wait_ge(lo_ready, u + 1)
                    out = gbank(gi)[:, 0:T]
                    for k in range(2):
                        c = k * 512 + (i % 4) * P
                        a, b = wh[:, u % R, c:c + P], wl[:, u % R, c:c + P]
                        mmul(out, a, peH[:, 2 * l + k, :], start=k == 0, stop=False)
                        mmul(out, a, peL[:, 2 * l + k, :], start=False, stop=False)
                        m = mmul(out, b, peH[:, 2 * l + k, :], start=False, stop=k == 1)
                    m.then_inc(unit_used if i % 4 == 3 else bank_done[gi % 4], 1)
                u0 = UNITS[f"gate{l}"]
                ahead(range(u0, u0 + AHEAD), [gid(f"gate{l}", i) for i in range(AHEAD)], OH, OL,
                      lambda k: pe.wait_ge(sem(f"xs_lo{l}"), k + 1))

                def turn_y(half):
                    for t, (t0, n) in enumerate(TOK):
                        gi = gid("y", 3 * half + t)
                        bank_free(pe, gi)
                        pe.wait_ge(sem("x_out1"), 4 * half + 4)
                        for j in range(4):
                            m = trans(gbank(gi)[0:n, j * P:(j + 1) * P], xT[:, 4 * half + j, t0:t0 + n], ident[:])
                        m.then_inc(bank_done[gi % 4], 1)

                for i in range(AHEAD, 8):
                    if l == 1 and i == 7:
                        turn_y(0)
                    gi = gid(f"gate{l}", i)
                    bank_free(pe, gi)
                    unit(u0 + i, gbank(gi)[:, 0:T], OH, OL)
                if l == 1:
                    turn_y(1)

        @block.scalar
        def _(act):
            A = nc.scalar.activation
            par = sem("ld_par0")
            for i, nm in enumerate(("ln_mix_pre", "ln_mix_post", "ln_ffn_pre", "ln_ffn_post")):
                act.dma_start(nrow[64 + 8 * i:72 + 8 * i, 0, :], I[nm][0].rearrange("(j c) -> j c", c=P)).then_inc(par, 16)
            act.dma_start(nrow[0:64, 0, :], I["state_ffn_conv"][0, 0].rearrange("r (j c) -> (r j) c", c=P)).then_inc(par, 16)
            act.dma_start(prow[0:96, 0, :], I["ffn_conv_w"][0].rearrange("t (j c) -> (t j) c", c=P)).then_inc(par, 16)
            act.dma_start(prow[96:128, 0, :], I["ffn_conv_b"][0].rearrange("(j c) -> j c", c=P)).then_inc(par, 16)
            act.dma_start(wnr[:, 0], I["w_att_in"][0][:, 1536:1544].rearrange("(k p) c -> p k c", p=P)).then_inc(sem("ld_narrow"), 16)
            act.dma_start(wnr[:, 1], I["w_rec_in"][0][:, 2048:2056].rearrange("(k p) c -> p k c", p=P)).then_inc(sem("ld_narrow"), 16)

            def hi(u, it=None):
                if it is None:
                    if u >= N_UNITS:
                        return
                    act.wait_ge(raw_landed[u % R], 16 * (u // R + 1))
                    if u >= R:
                        act.wait_ge(unit_used, u - R + 1)
                else:
                    act.wait_ge(raw_landed[u % R], it * 16 + 16 * (u // R + 1))
                    act.wait_ge(unit_used, it * 4 + (u - R + 1))
                A(wh[:, u % R, :], raw[:, u % R, :], ACT.Copy).then_inc(hi_ready, 1)

            def prenorm(l, j, col):
                A(hH[:, j, :], xT[:, j, :], ACT.Copy, scale=NC[:, l, col + j:col + j + 1]).then_inc(sem("h_hi"), 1)
                A(sqb[:, j, :], xT[:, j, :], ACT.Square).then_inc(sem("sq"), 1)

            def tok_copy(i):
                kind, t = i // 3, i % 3
                gi = gid("tok", i)
                n = TOK[t][1]
                bank_full(act, gi)
                dst = (Vtok, Ktok, Stok)[kind]
                w = 512 if kind < 2 else 256
                A(dst[0:n, t, :], gbank(gi)[0:n, 0:w], ACT.Copy).then_inc(sem("tok_read"), 1)

            def weights(i):
                n, w, b = TOK[TASKS[i][2]][1], score_width(i), i % 6
                act.wait_ge(sem("s_max"), i + 1)
                A(S_sb[0:n, b, 0:w], S_sb[0:n, b, 0:w], ACT.Exp, bias=amax[0:n, b, :], accum_out=aden[0:n, b, :]).then_inc(sem("s_exp"), 1)

            def pt_copy(i):
                fox, h, t = TASKS[i]
                n = TOK[t][1]
                act.wait_ge(sem("pt_done"), i + 1)
                if i >= 4:
                    act.wait_ge(sem("pv_done"), i - 3)
                full = (t + 1) if t < 2 else (2 if fox else 1)
                if n == P:
                    last = A(PT[:, i % 4, 0:full * P], bank[6 + i % 2][:, 0:full * P], ACT.Copy)
                else:
                    src = bank[6 + i % 2][:, 0:full * P].rearrange("p (b c) -> p b c", c=P)[:, :, 0:n]
                    dst = PT[:, i % 4, 0:full * P].rearrange("p (b c) -> p b c", c=P)[:, :, 0:n]
                    A(dst, src, ACT.Copy)
                    last = A(PT[0:64, i % 4, full * P:full * P + n], bank[6 + i % 2][0:64, full * P:full * P + n], ACT.Copy)
                last.then_inc(sem("pt_moved"), 1)

            def o_hi(j):
                gi = gid("o", j)
                bank_full(act, gi)
                A(OH[:, j, :], gbank(gi)[:, 0:T], ACT.Copy).then_inc(sem("o_hi0"), 1)

            def input_attention():
                for j in range(KT):
                    act.wait_ge(sem("x_in"), j + 1)
                    if j == 0:
                        act.wait_ge(sem("par_in"), 2)
                    prenorm(0, j, 64)
                act.wait_ge(sem("ld_narrow"), 32)
                A(wnH[:].rearrange("p a b c -> p (a b c)"), wnr[:].rearrange("p a b c -> p (a b c)"), ACT.Copy).then_inc(sem("narrow_hi"), 1)
                act.wait_ge(sem("const2"), 1)
                for r0 in range(0, P, 32):
                    ins = A(selR[r0:r0 + 8, :], ident[0:8, 0:8], ACT.Copy)
                ins.then_inc(sem("sel"), 1)
                for i in range(4):
                    hi(i + R)
                act.wait_ge(sem("pe_f"), 4)
                A(peH[:].rearrange("p a t -> p (a t)"), pef[:].rearrange("p a t -> p (a t)"), ACT.Copy).then_inc(sem("pe_hi"), 1)
                for i in range(4, 12):
                    hi(i + R)
                    if i == 6:
                        act.wait_ge(sem("lf_abs"), 1)
                        A(lfz[:, 1, :], lfz[:, 1, :], ACT.Exp, scale=-1.0).then_inc(sem("lf_exp"), 1)
                        act.wait_ge(sem("lf_exp"), 1)
                        A(lfz[:, 1, :], lfz[:, 1, :], ACT.Ln, bias=cst[0:8, 1:2]).then_inc(sem("lf_ln"), 1)
                act.wait_ge(sem("Frow"), 1)
                A(FrowR[0:8, :], Frow[:], ACT.Copy)
                A(FrowR[64:72, :], Frow[:], ACT.Copy).then_inc(sem("Frow_hi"), 1)
                for t in range(3):
                    tok_copy(t)
                for e in attention_events():
                    if e[0] == "scores":
                        weights(e[1])
                    elif e[0] == "half":
                        if e[2]:
                            hi(e[1] + R)
                    elif e[0] == "tok":
                        tok_copy(e[1])
                    elif e[0] == "turn":
                        pt_copy(e[1])
                    elif e[1] % 6 == 0 and e[1]:
                        o_hi(e[1] // 6 - 1)
                o_hi(7)

            def input_recurrent():
                u0 = UNITS["in1"]

                def out_gate(j):
                    act.wait_ge(sem("in_read1"), 9 + j)
                    A(sig[:, j, :], sig[:, j, :], ACT.Sigmoid).then_inc(sem("og"), 1)

                for e in recurrent_events():
                    name, a = e[0], e[1:]
                    if name == "unit":
                        hi(u0 + a[0] + R)
                        if a[0] == 5:
                            act.wait_ge(sem("mlf_abs"), 1)
                            A(mz[:, 2, :], mz[:, 2, :], ACT.Exp, scale=-1.0).then_inc(sem("mlf_exp"), 1)
                            act.wait_ge(sem("mlf_exp"), 1)
                            A(mz[:, 2, :], mz[:, 2, :], ACT.Ln, bias=cst[0:8, 1:2]).then_inc(sem("mlf_ln"), 1)
                        if a[0] == 15:
                            for j in range(7):
                                out_gate(j)
                        if a[0] == 16:
                            out_gate(7)
                    elif name == "half":
                        if a[1]:
                            hi(u0 + a[0] + R)
                    elif name == "ktok":
                        gi = gid("ktok", a[0])
                        n = TOK[a[0]][1]
                        bank_full(act, gi)
                        A(KmT[0:n, a[0], :], gbank(gi)[0:n, :], ACT.Copy).then_inc(sem("ktok_read"), 1)
                        if a[0] == 2:
                            act.wait_ge(sem("mexp_in"), 1)
                            for nm in ("sdec", "em", "g"):
                                x = ml[nm][:].rearrange("p t h -> p (t h)")
                                A(x, x, ACT.Exp)
                            A(scd[:].rearrange("p c h -> p (c h)"), scd[:].rearrange("p c h -> p (c h)"), ACT.Exp).then_inc(sem("mexp"), 1)
                            for t in range(3):
                                n = TOK[t][1]
                                for h in range(MH):
                                    ins = A(Dm[0:n, t, h, 0:n], Dm[0:n, t, h, 0:n], ACT.Exp, bias=ml["nmu"][0:n, t, h:h + 1])
                                ins.then_inc(sem("mD"), 1)
                    elif name == "wT":
                        t = a[0]
                        n = TOK[t][1]
                        act.wait_ge(sem("mwT"), t + 1)
                        src = bank[5][0:n, :].rearrange("p (h c) -> p h c", h=MH)[:, :, 0:n]
                        dst = wT[0:n, t, :].rearrange("p (h c) -> p h c", h=MH)[:, :, 0:n]
                        A(dst, src, ACT.Copy).then_inc(sem("mwT_read"), 1)
                    elif name == "vtok":
                        h, t = a
                        n = TOK[t][1]
                        gi = gid("vtok", 3 * h + t)
                        bank_full(act, gi)
                        if 3 * h + t == 0:
                            act.wait_ge(sem("C_init"), 1)
                        A(Vaug[0:n, h % 2, t, 0:DV], gbank(gi)[0:n, 0:DV], ACT.Copy).then_inc(sem("vtok_read"), 1)
                    elif name == "chunk":
                        h, c = a
                        t, r = c // 2, slice(64 * (c % 2), 64 * (c % 2) + 64)
                        act.wait_ge(sem("inter_done"), 5 * h + c + 1)
                        A(Y[r, h % 2, t, :], bank[6][r, 0:DV + 1], ACT.Copy, scale=ml["sdec"][r, t, h:h + 1]).then_inc(sem("inter_read"), 1)
                    elif name == "intra":
                        h, t = a
                        n = TOK[t][1]
                        k = 3 * h + t
                        act.wait_ge(sem("Y"), k + 1)
                        if k:
                            act.wait_ge(sem("Yss"), k)
                        A(Ysq[0:n, :], Y[0:n, h % 2, t, 0:DV], ACT.Square, accum_out=yf["ss"][0:n, h % 2, t:t + 1]).then_inc(sem("Yss"), 1)
                    elif name == "heads":
                        for v in range(2):
                            j = 2 * a[0] + v
                            act.wait_ge(sem("mo_f"), j + 1)
                            A(OH[:, j, :], obuf[:, v, :], ACT.Copy).then_inc(sem("o_hi1"), 1)

            for u in range(R):
                hi(u)
            for l in range(2):
                if l == 0:
                    input_attention()
                else:
                    input_recurrent()
                for i in range(8):
                    gi = gid(f"out{l}", i)
                    bank_full(act, gi)
                    A(mix[:, i, :], gbank(gi)[:, 0:T], ACT.Copy, scale=NC[:, l, 72 + i:73 + i]).then_inc(sem(f"mix_{l}"), 1)
                    A(sqb[:, i, :], gbank(gi)[:, 0:T], ACT.Square).then_inc(sem("sq"), 1)
                    hi(UNITS[f"out{l}"] + i + R)
                for j in range(KT):
                    x_added(act, f"mixpost{l}", j)
                    prenorm(l, j, 80)
                act.wait_ge(sem(f"scratch_out{l}"), 1)
                u0 = UNITS[f"up{l}"]
                with act.Fori(0, FT // 2) as it:
                    A(mark[:], mark[:], ACT.Gelu_apprx_tanh)
                    for s in range(2):
                        hi(u0 + 2 * s + R, it)
                        act.wait_ge(sem(f"gp{l}"), it * 2 + (s + 1))
                        j = it * 2 + s
                        A(cv[:, s, :], gp[:, s, 2:T + 4], ACT.Identity, scale=PC[:, l, bass.ds(j + 64, 1)],
                          bias=PC[:, l, bass.ds(j + 96, 1)]).then_inc(sem(f"cv{l}"), 1)
                        act.wait_ge(sem(f"conv{l}"), it * 4 + (2 * s + 2))
                        A(cv[:, s, :], cv[:, s, :], ACT.Gelu_apprx_tanh).then_inc(sem(f"gelu{l}"), 1)
                        hi(u0 + 2 * s + 1 + R, it)
                        act.wait_ge(sem(f"f{l}"), it * 2 + (s + 1))
                        A(FH[:, bass.ds(j, 1), :].rearrange("p a t -> p (a t)"), fb[:, s, :], ACT.Copy).then_inc(sem(f"f_hi{l}"), 1)
                u0 = UNITS[f"down{l}"]
                for i in range(8):
                    for q in range(4):
                        if q == 3:
                            gi = gid(f"down{l}", i)
                            bank_full(act, gi)
                            A(mix[:, i, :], gbank(gi)[:, 0:T], ACT.Copy, scale=NC[:, l, 88 + i:89 + i]).then_inc(sem(f"mixf_{l}"), 1)
                            A(sqb[:, i, :], gbank(gi)[:, 0:T], ACT.Square).then_inc(sem("sq"), 1)
                        hi(u0 + 4 * i + q + R)

                def ple_copy(i):
                    gi = gid(f"ple{l}", i)
                    bank_full(act, gi)
                    A(sqb[:, i, :], gbank(gi)[:, 0:T], ACT.Copy).then_inc(sem(f"ple_sb{l}"), 1)

                def x_hi(i):
                    x_added(act, f"ffnpost{l}", i)
                    A(OH[:, i, :], xT[:, i, :], ACT.Copy).then_inc(sem(f"xs_hi{l}"), 1)

                for i in range(4):
                    ple_copy(i)
                hi(UNITS[f"ple{l}"] + R)
                ple_copy(4)
                ple_copy(5)
                x_hi(0)
                ple_copy(6)
                x_hi(1)
                ple_copy(7)
                hi(UNITS[f"ple{l}"] + 1 + R)
                for i in range(2, 8):
                    x_hi(i)
                for i in range(8):
                    gi = gid(f"gate{l}", i)
                    bank_full(act, gi)
                    if i >= 2:
                        act.wait_ge(sem(f"x_out{l}"), i - 1)
                    A(sgb[:, i % 2, :], gbank(gi)[:, 0:T], ACT.Sigmoid).then_inc(sem(f"sigm{l}"), 1)
                    hi(UNITS[f"gate{l}"] + i + R)
                    if l == 0 and i:
                        act.wait_ge(sem("x_out0"), i)
                        prenorm(1, i - 1, 64)
                    if l == 1 and i == 6:
                        for t in range(3):
                            copy_y(act, t)
                if l == 0:
                    act.wait_ge(sem("x_out0"), 8)
                    prenorm(1, 7, 64)
            copy_y(act, 4)

        @block.vector
        def _(dve):
            V = nc.vector

            def lo(u, it=None):
                if it is None:
                    if u >= N_UNITS:
                        return
                    dve.wait_ge(hi_ready, u + 1)
                else:
                    dve.wait_ge(hi_ready, it * 4 + (u + 1))
                V.tensor_tensor(wl[:, u % R, :], raw[:, u % R, :], wh[:, u % R, :].bitcast(F32), ALU.subtract).then_inc(lo_ready, 1)

            def prenorm_lo(stage, l, j, col):
                dve.wait_ge(sem("h_hi"), eights(stage, j))
                V.scalar_tensor_tensor(out=hL[:, j, :], in0=xT[:, j, :], scalar=NC[:, l, col + j:col + j + 1],
                                       in1=hH[:, j, :].bitcast(F32), op0=ALU.mult, op1=ALU.subtract).then_inc(sem("h_lo"), 1)

            def mean_square(stage):
                dve.wait_ge(sem("sq_sum"), NORMS[stage] + 1)
                V.tensor_scalar(ms[:], bank[4][:, 0:3], 1.0 / D, EPS, ALU.mult, ALU.add).then_inc(sem("ms"), 1)

            def rms_diagonal(stage):
                dve.wait_ge(sem("rcol"), NORMS[stage] + 1)
                for t in range(3):
                    ins = V.tensor_scalar(diag[:, t, :], ident[:], rcol[:, t:t + 1], None, ALU.mult)
                ins.then_inc(sem("diag"), 1)

            def rms_rows(stage, dst):
                dve.wait_ge(sem("rms_rows"), NORMS[stage] + 1)
                V.tensor_copy(dst[:], bank[5][:, 0:T]).then_inc(sem("rstd"), 1)
                dve.wait_ge(sem("rstd"), NORMS[stage] + 1)

            def postnorm(stage, low):
                mean_square(stage)
                rms_diagonal(stage)
                rms_rows(stage, rstd2)
                k0 = 4 * (NORMS[stage] // 2)
                for j in range(0, KT, 2):
                    V.tensor_tensor(mix[:, j, :], mix[:, j, :], rstd2[:], ALU.mult).then_inc(sem("post_even"), 1)
                    dve.wait_ge(sem("post_even"), k0 + j // 2 + 1)
                    V.tensor_tensor(xT[:, j, :], xT[:, j, :], mix[:, j, :], ALU.add).then_inc(sem("x_even"), 1)
                    if j:
                        low(j - 2)
                        low(j - 1)
                dve.wait_ge(sem("x_odd"), k0 + 4)
                low(6)
                low(7)

            def scaled(l, i, dst, rows=slice(0, P), factor=None, src_rows=None, last=True, name=None):
                sr = src_rows or rows
                src = gbank(gid(name or f"in{l}", i))[sr, 0:T]
                if factor is None:
                    ins = V.tensor_tensor(dst, src, rstd[sr, :], ALU.mult)
                else:
                    ins = V.scalar_tensor_tensor(out=dst, in0=src, scalar=factor, in1=rstd[sr, :], op0=ALU.mult, op1=ALU.mult)
                if last:
                    ins.then_inc(sem(f"in_read{l}"), 1)
                return ins

            def narrow(l, z):
                bank_full(dve, gid(f"narrow{l}", 0))
                s = sem(f"narrow_step{l}")
                scaled(l, 0, z[:, 0, :], rows=slice(0, 8), last=False, name=f"narrow{l}").then_inc(s, 1)
                dve.wait_ge(s, 1)
                V.tensor_scalar(z[:, 0, :], z[:, 0, :], bcol[:, l:l + 1], None, ALU.add).then_inc(s, 1)
                dve.wait_ge(s, 2)
                k = 1 if l == 0 else 2
                V.scalar_tensor_tensor(out=z[:, k, :], in0=z[:, 0, :], scalar=-1.0, in1=z[:, 0, :], op0=ALU.mult, op1=ALU.max)\
                    .then_inc(sem("lf_abs" if l == 0 else "mlf_abs"), 1)
                V.tensor_scalar(z[:, 2 if l == 0 else 1, :], z[:, 0, :], 0.0, None, ALU.min).then_inc(s, 1)

            def in0_read(i):
                bank_full(dve, gid("in0", i))
                if i < 4:
                    scaled(0, i, mix[:, i, :], factor=HD ** -0.5)
                elif i < 8:
                    scaled(0, i, kT[:, i - 4, :])
                elif i < 12:
                    scaled(0, i, sqb[:, i - 8, :])
                elif i < 16:
                    scaled(0, i, mix[:, i - 8, :], factor=HD ** -0.5)
                elif i == 16:
                    for half in range(2):
                        for g in range(2):
                            scaled(0, i, kdup[64 * half:64 * half + 64, g, :], src_rows=slice(64 * g, 64 * g + 64), last=False)
                    scaled(0, i, kplain[:])
                else:
                    scaled(0, i, sqb[:, 4, :])

            def scores_moved(i):
                fox, h, t = TASKS[i]
                n, b, w = TOK[t][1], i % 6, score_width(i)
                dve.wait_ge(sem("s_done"), i + 1)
                if i >= 6:
                    dve.wait_ge(sem("pt_done"), i - 5)
                src = bank[4 + i % 2]
                if fox:
                    m = MFox[0:n, 384 - w:384] if t < 2 else MFox[0:n, 0:w]
                    V.scalar_tensor_tensor(out=S_sb[0:n, b, 0:w], in0=src[0:n, 0:w], scalar=Ftok[0:n, t, h:h + 1], in1=m,
                                           op0=ALU.add, op1=ALU.add).then_inc(sem("s_moved"), 1)
                else:
                    V.tensor_copy(S_sb[0:n, b, w - 1:w], sinkb[0:n, h:h + 1])
                    if t < 2:
                        V.tensor_tensor(S_sb[0:n, b, 0:w - 1], src[0:n, 0:w - 1], MSwa[0:n, 256 - (w - 1):256], ALU.add).then_inc(sem("s_moved"), 1)
                    else:
                        V.tensor_copy(S_sb[0:n, b, 0:w - 1], src[0:n, 0:w - 1]).then_inc(sem("s_moved"), 1)
                dve.wait_ge(sem("s_moved"), i + 1)
                V.tensor_reduce(amax[0:n, b, :], S_sb[0:n, b, 0:w], X, ALU.max, negate=True).then_inc(sem("s_max"), 1)

            def inverse_sum(i):
                n, b = TOK[TASKS[i][2]][1], i % 6
                dve.wait_ge(sem("s_exp"), i + 1)
                V.reciprocal(ainv[0:n, b, :], aden[0:n, b, :]).then_inc(sem("a_inv"), 1)

            def o_lo(j):
                dve.wait_ge(sem("o_hi0"), j + 1)
                V.tensor_tensor(OL[:, j, :], gbank(gid("o", j))[:, 0:T], OH[:, j, :].bitcast(F32), ALU.subtract).then_inc(sem("o_lo0"), 1)

            def input_attention():
                for u in range(R):
                    lo(u)
                for i, dst in enumerate((PC, NC)):
                    bank_full(dve, gid("par", i))
                    n = (P, 96)[i]
                    V.tensor_copy(dst[:, 0, 0:n], gbank(gid("par", i))[:, 0:n]).then_inc(sem("par_in"), 1)
                for j in range(KT):
                    gi = gid("x", j)
                    bank_full(dve, gi)
                    V.tensor_copy(xT[:, j, :], gbank(gi)[:, 0:T]).then_inc(sem("x_in"), 1)
                    if j:
                        prenorm_lo("mixpre0", 0, j - 1, 64)
                prenorm_lo("mixpre0", 0, 7, 64)
                dve.wait_ge(sem("narrow_hi"), 1)
                V.tensor_tensor(wnL[:].rearrange("p a b c -> p (a b c)"), wnr[:].rearrange("p a b c -> p (a b c)"),
                                wnH[:].rearrange("p a b c -> p (a b c)").bitcast(F32), ALU.subtract).then_inc(sem("narrow_split"), 1)
                mean_square("mixpre0")
                lo(4)
                rms_diagonal("mixpre0")
                lo(5)
                rms_rows("mixpre0", rstd)
                in0_read(0)
                in0_read(1)
                in0_read(2)
                lo(6)
                in0_read(3)
                lo(7)
                for i, dst in enumerate((PC, NC)):
                    bank_full(dve, gid("par", 2 + i))
                    n = (P, 104)[i]
                    V.tensor_copy(dst[:, 1, 0:n], gbank(gid("par", 2 + i))[:, 0:n]).then_inc(sem("par_in"), 1)
                for i in range(4):
                    bank_full(dve, gid("pe", i))
                    V.tensor_copy(pef[:, i, :], gbank(gid("pe", i))[:, 0:T]).then_inc(sem("pe_f"), 1)
                for j in range(4):
                    bank_full(dve, gid("cache", j))
                    V.tensor_copy(kcT[:, j, :], gbank(gid("cache", j))[:, 0:PAST]).then_inc(sem("cache_read"), 1)
                gi = gid("cache", 4)
                bank_full(dve, gi)
                for half in range(2):
                    for g in range(2):
                        ins = V.tensor_copy(kcdup[64 * half:64 * half + 64, g, :], gbank(gi)[64 * g:64 * g + 64, 0:P])
                ins.then_inc(sem("cache_read"), 1)
                dve.wait_ge(sem("pe_hi"), 1)
                V.tensor_tensor(peL[:].rearrange("p a t -> p (a t)"), pef[:].rearrange("p a t -> p (a t)"),
                                peH[:].rearrange("p a t -> p (a t)").bitcast(F32), ALU.subtract).then_inc(sem("pe_split"), 1)
                dve.wait_ge(sem("pe_split"), 1)
                for i in range(4, 12):
                    in0_read(i)
                    lo(i + R)
                    if i == 5:
                        narrow(0, lfz)
                    elif i == 6:
                        dve.wait_ge(sem("lf_ln"), 1)
                        dve.wait_ge(sem("narrow_step0"), 3)
                        V.tensor_tensor(lfz[:, 0, :], lfz[:, 2, :], lfz[:, 1, :], ALU.subtract).then_inc(sem("lf_ready"), 1)
                    elif i == 7:
                        dve.wait_ge(sem("lf_tr"), 1)
                        V.tensor_copy(lftok[:, 0:2, :], bank[5][:, 0:16].rearrange("p (t h) -> p t h", t=2))
                        V.tensor_copy(lftok[0:64, 2, :], bank[5][0:64, 16:24]).then_inc(sem("lf_tok"), 1)
                    elif i == 9:
                        dve.wait_ge(sem("F_sums"), 1)
                        V.tensor_copy(Ftok[:, 0:2, :], bank[6][:, 0:16].rearrange("p (t h) -> p t h", t=2))
                        V.tensor_copy(Ftok[0:64, 2, :], bank[6][0:64, 16:24])
                        V.tensor_scalar(Frow[:, 0:256], bank[7][0:8, 0:256], -1.0, None, ALU.mult)
                        V.tensor_scalar(Frow[:, 256:576], bank[5][0:8, 0:320], -1.0, None, ALU.mult).then_inc(sem("Frow"), 1)
                dve.wait_ge(sem("Frow_hi"), 1)
                dve.wait_ge(sem("sel"), 1)
                V.tensor_tensor(FrowR[32:40, :], Frow[:], FrowR[0:8, :].bitcast(F32), ALU.subtract)
                V.tensor_tensor(FrowR[96:104, :], Frow[:], FrowR[64:72, :].bitcast(F32), ALU.subtract).then_inc(sem("F_rows"), 1)
                for e in attention_events():
                    if e[0] == "scores":
                        scores_moved(e[1])
                        if e[1]:
                            inverse_sum(e[1] - 1)
                    elif e[0] == "half":
                        if e[2]:
                            in0_read(e[1])
                            lo(e[1] + R)
                    elif e[0] == "turn" and e[1] == len(TASKS) - SKEW_T:
                        inverse_sum(len(TASKS) - 1)
                    elif e[0] == "values" and e[1] % 6 == 0 and e[1]:
                        o_lo(e[1] // 6 - 1)
                o_lo(7)

            def input_recurrent():
                st = sem("m_step")
                ns = [0]

                def link(ins):
                    ns[0] += 1
                    ins.then_inc(st, 1)
                    dve.wait_ge(st, ns[0])

                fl = {nm: ml[nm][:].rearrange("p t h -> p (t h)") for nm in ml}
                u0 = UNITS["in1"]

                def in1_read(i):
                    bank_full(dve, gid("in1", i))
                    if i < 4:
                        scaled(1, i, mix[:, i, :])
                    elif i < 8:
                        scaled(1, i, mix[:, i, :], factor=DK ** -0.5)
                    elif i < 16:
                        scaled(1, i, sig[:, i - 8, :])
                    else:
                        scaled(1, i, sqb[:, i - 16, :])

                def maxima():
                    for t in range(3):
                        dve.wait_ge(sem("mspread"), t + 1)
                        b = bank[5 + t][:, :].rearrange("p (h s) -> p h s", h=MH)
                        V.tensor_reduce(MF[:, t, :, :], bank[5 + t][:, :].rearrange("p (h c s) -> p h c s", h=MH, c=2), X, ALU.max)
                        for h in range(MH):
                            ins = V.tensor_tensor(Dm[:, t, h, :], b[:, h, :], MBlk[:], ALU.add)
                        link(ins)
                        V.tensor_reduce(ml["M"][:, t, :], Dm[:, t], X, ALU.max).then_inc(sem("mD_raw"), 1)
                    dve.wait_ge(sem("mD_raw"), 3)
                    for c in range(5):
                        t, half = c // 2, c % 2
                        link(V.tensor_tensor(muc[:, c, :], mprev[:, c, :], MF[:, t, :, half], ALU.max))
                        if c < 4:
                            dst = mprev[:, c + 1, :] if c < 3 else mprev[:, 5, :]
                            link(V.tensor_tensor(dst, muc[:, c, :], BL[:, half, 4 * t:4 * t + 4], ALU.add))
                        else:
                            link(V.tensor_tensor(mz[:, 3, 0:4], muc[0:8, c, :], BL[0:8, half, 4 * t:4 * t + 4], ALU.add))
                    for t in range(3):
                        for half in range(2):
                            c = min(2 * t + half, 4)
                            r = slice(64 * half, 64 * half + 64)
                            V.tensor_copy(ml["mp"][r, t, :], mprev[r, c, :])
                            ins = V.tensor_copy(ml["muL"][r, t, :], muc[r, c, :])
                    link(ins)
                    link(V.tensor_tensor(fl["mu"], fl["mp"], fl["M"], ALU.max))
                    V.tensor_scalar(fl["nmu"], fl["mu"], -1.0, None, ALU.mult)
                    V.tensor_tensor(fl["sdec"], fl["mp"], fl["mu"], ALU.subtract)
                    link(V.tensor_tensor(fl["t0"], fl["bt"], fl["mu"], ALU.add))
                    V.tensor_scalar(fl["em"], fl["t0"], -1.0, None, ALU.mult)
                    V.tensor_tensor(fl["g"], fl["a"], fl["muL"], ALU.subtract)
                    V.tensor_tensor(scd[:], mprev[:, 0:5, :], muc[:], ALU.subtract).then_inc(sem("mexp_in"), 1)

                def head_norm(h):
                    b = h % 2
                    y = Y[:, b]
                    den, r, v, f = (yf[nm][:, b, :] for nm in ("den", "r", "v", "f"))
                    link(V.scalar_tensor_tensor(out=den, in0=y[:, :, DV], scalar=-1.0, in1=y[:, :, DV], op0=ALU.mult, op1=ALU.max))
                    link(V.tensor_tensor(den, den, ml["em"][:, :, h], ALU.max))
                    link(V.reciprocal(r, den))
                    link(V.tensor_tensor(v, r, r, ALU.mult))
                    dve.wait_ge(sem("Yss"), 3 * h + 3)
                    link(V.tensor_tensor(v, v, yf["ss"][:, b, :], ALU.mult))
                    V.tensor_scalar(v, v, 1.0 / DV, EPS, ALU.mult, ALU.add).then_inc(sem("Yvar"), 1)
                    dve.wait_ge(sem("Yroot"), h + 1)
                    link(V.tensor_tensor(f, yf["w"][:, b, :], r, ALU.mult))
                    for t in range(3):
                        n = TOK[t][1]
                        V.tensor_scalar(Y[0:n, b, t, 0:DV], Y[0:n, b, t, 0:DV], f[0:n, t:t + 1], None, ALU.mult).then_inc(sem("Yn"), 1)

                for e in recurrent_events():
                    name, a = e[0], e[1:]
                    if name == "unit":
                        i = a[0]
                        if i == 1:
                            rms_rows("mixpre1", rstd)
                            in1_read(0)
                        elif i == 0:
                            lo(u0 + R)
                        if i:
                            in1_read(i)
                            lo(u0 + i + R)
                        if i == 5:
                            dve.wait_ge(sem("mlf_ln"), 1)
                            dve.wait_ge(sem("narrow_step1"), 3)
                            V.tensor_tensor(mz[:, 1, :], mz[:, 1, :], mz[:, 2, :], ALU.subtract).then_inc(sem("mgates"), 1)
                    elif name == "stats":
                        mean_square("mixpre1")
                        rms_diagonal("mixpre1")
                    elif name == "narrow":
                        narrow(1, mz)
                        V.memset(gt[:], 0.0)
                        V.memset(C[:, 0], 0.0)
                        V.memset(mprev[:, 0, :], 0.0)
                        V.memset(Y[:], 1.0)
                        V.memset(yf["ss"][:], 1.0)
                        link(V.memset(Vaug[:, :, :, DV:DV + 1], 1.0))
                        dve.wait_ge(sem("ld_state"), 48)
                        dve.sem_inc(sem("C_init"), 1)
                    elif name == "half":
                        if a[1]:
                            in1_read(a[0])
                            lo(u0 + a[0] + R)
                    elif name == "gates":
                        dve.wait_ge(sem("mgates_tr"), 1)
                        V.tensor_copy(gt[:, 0:2, :], bank[5][:, 0:32].rearrange("p (t c) -> p t c", t=2))
                        link(V.tensor_copy(gt[0:64, 2, :], bank[5][0:64, 32:48]))
                        V.tensor_copy(ml["lf"][:], gt[:, :, 12:16]).then_inc(sem("mlf"), 1)
                    elif name == "sums":
                        dve.wait_ge(sem("msums"), 1)
                        V.tensor_copy(fl["bt"], bank[6][:, 0:12])
                        V.tensor_copy(BL[:, 0, :], bank[6][:, 16:28])
                        link(V.tensor_copy(BL[:, 1, :], bank[7][:, 32:44]))
                        V.tensor_tensor(ml["a"][:], gt[:, :, 0:4], ml["bt"][:], ALU.subtract).then_inc(sem("ma"), 1)
                    elif name == "arow":
                        dve.wait_ge(sem("maT"), 1)
                        V.tensor_copy(aT[:], bank[7][0:12, 0:P]).then_inc(sem("maT_read"), 1)
                    elif name == "spread":
                        maxima()
                    elif name == "qk":
                        t = a[0]
                        n = TOK[t][1]
                        if t == 0:
                            dve.wait_ge(sem("mexp"), 1)
                            dve.wait_ge(sem("ktok_read"), 3)
                            for tt in range(3):
                                nn = TOK[tt][1]
                                for h in range(MH):
                                    k = KmT[0:nn, tt, h * P:(h + 1) * P]
                                    V.tensor_scalar(k, k, ml["g"][0:nn, tt, h:h + 1], None, ALU.mult).then_inc(sem("Kg"), 1)
                        dve.wait_ge(sem("mD"), t + 1)
                        dve.wait_ge(sem("mqk"), t + 1)
                        src = bank[4][0:n, :].rearrange("p (h c) -> p h c", h=MH)[:, :, 0:n]
                        V.tensor_tensor(Dm[0:n, t, :, 0:n], src, Dm[0:n, t, :, 0:n], ALU.mult).then_inc(sem("mw"), 1)
                    elif name == "chunk":
                        h, c = a
                        dve.wait_ge(sem("C_add"), 5 * h + c + 1)
                        s = c // 4
                        V.scalar_tensor_tensor(out=C[:, s, h, :], in0=C[:, s, h, :], scalar=scd[:, c, h:h + 1],
                                               in1=bank[7][:, 0:DV + 1], op0=ALU.mult, op1=ALU.add).then_inc(sem("C_new"), 1)
                    elif name == "intra":
                        h, t = a
                        n = TOK[t][1]
                        gi = gid("intra", 3 * h + t)
                        bank_full(dve, gi)
                        dve.wait_ge(sem("inter_read"), 5 * h + min(2 * t + 2, 5))
                        V.tensor_tensor(Y[0:n, h % 2, t, :], gbank(gi)[0:n, 0:DV + 1], Y[0:n, h % 2, t, :], ALU.add).then_inc(sem("Y"), 1)
                        if t == 2:
                            dve.wait_ge(sem("Y"), 3 * h + 3)
                            head_norm(h)
                    elif name == "heads":
                        h = a[0]
                        if h == 0:
                            dve.wait_ge(sem("og"), 8)
                        for v in range(2):
                            j = 2 * h + v
                            gi = gid("heads", j)
                            bank_full(dve, gi)
                            V.scalar_tensor_tensor(out=obuf[:, v, :], in0=gbank(gi)[:, 0:T], scalar=NC[:, 1, 96 + j:97 + j],
                                                   in1=sig[:, j, :], op0=ALU.mult, op1=ALU.mult).then_inc(sem("mo_f"), 1)
                        for v in range(2):
                            j = 2 * h + v
                            dve.wait_ge(sem("o_hi1"), j + 1)
                            V.tensor_tensor(OL[:, j, :], obuf[:, v, :], OH[:, j, :].bitcast(F32), ALU.subtract).then_inc(sem("o_lo1"), 1)

            for l in range(2):
                if l == 0:
                    input_attention()
                else:
                    input_recurrent()
                for i in range(8):
                    lo(UNITS[f"out{l}"] + i + R)
                dve.wait_ge(sem(f"mix_{l}"), 8)
                postnorm(f"mixpost{l}", lambda j: prenorm_lo(f"ffnpre{l}", l, j, 80))
                mean_square(f"ffnpre{l}")
                rms_diagonal(f"ffnpre{l}")
                rms_rows(f"ffnpre{l}", rstd)
                dve.wait_ge(sem(f"scratch_out{l}"), 1)
                u0, g0 = UNITS[f"up{l}"], gid(f"up{l}", 0)
                with dve.Fori(0, FT // 2) as it:
                    for s in range(2):
                        j = it * 2 + s
                        ga, gu = g0 + 2 * s, g0 + 2 * s + 1
                        hist = NC[:, l, 0:64].rearrange("p (r j) -> p r j", r=2)[:, :, bass.ds(j, 1)].rearrange("p r j -> p (r j)")
                        V.tensor_copy(gp[:, s, 258:260], hist)
                        bank_full(dve, ga, it * 4)
                        V.tensor_tensor(gp[:, s, 2:258], gbank(ga)[:, 0:TP], rstd[:, 0:TP], ALU.mult)
                        V.tensor_tensor(gp[:, s, 260:324], gbank(ga)[:, TP:T], rstd[:, TP:T], ALU.mult).then_inc(sem(f"gp{l}"), 1)
                        lo(u0 + 2 * s + R, it)
                        dve.wait_ge(sem(f"cv{l}"), it * 2 + (s + 1))
                        for tap in (1, 0):
                            V.scalar_tensor_tensor(out=cv[:, s, :], in0=gp[:, s, tap:tap + T + 2], scalar=PC[:, l, bass.ds(j + 32 * tap, 1)],
                                                   in1=cv[:, s, :], op0=ALU.mult, op1=ALU.add).then_inc(sem(f"conv{l}"), 1)
                            if tap:
                                dve.wait_ge(sem(f"conv{l}"), it * 4 + (2 * s + 1))
                        bank_full(dve, gu, it * 4)
                        V.tensor_tensor(us[:, s, :], gbank(gu)[:, 0:T], rstd[:], ALU.mult).then_inc(sem(f"us{l}"), 1)
                        lo(u0 + 2 * s + 1 + R, it)
                        dve.wait_ge(sem(f"f_hi{l}"), it * 2 + (s + 1))
                        V.tensor_tensor(FL[:, bass.ds(j, 1), :].rearrange("p a t -> p (a t)"), fb[:, s, :],
                                        FH[:, bass.ds(j, 1), :].rearrange("p a t -> p (a t)").bitcast(F32), ALU.subtract).then_inc(sem(f"f_lo{l}"), 1)
                for i in range(32):
                    lo(UNITS[f"down{l}"] + i + R)
                    if i == 4:
                        bank_full(dve, gid(f"cs{l}", 0))
                        V.tensor_copy(csT[:], gbank(gid(f"cs{l}", 0))[:, 0:P]).then_inc(sem(f"csT{l}"), 1)
                dve.wait_ge(sem(f"mixf_{l}"), 8)

                def x_lo(j):
                    dve.wait_ge(sem(f"xs_hi{l}"), j + 1)
                    V.tensor_tensor(OL[:, j, :], xT[:, j, :], OH[:, j, :].bitcast(F32), ALU.subtract).then_inc(sem(f"xs_lo{l}"), 1)
                    if j < 2:
                        lo(UNITS[f"ple{l}"] + j + R)

                postnorm(f"ffnpost{l}", x_lo)
                for i in range(8):
                    dve.wait_ge(sem(f"sigm{l}"), i + 1)
                    dve.wait_ge(sem(f"ple_sb{l}"), i + 1)
                    V.tensor_tensor(sgb[:, i % 2, :], sgb[:, i % 2, :], sqb[:, i, :], ALU.mult).then_inc(sem(f"sg{l}"), 1)
                    dve.wait_ge(sem(f"sg{l}"), i + 1)
                    V.tensor_tensor(xT[:, i, :], xT[:, i, :], sgb[:, i % 2, :], ALU.add).then_inc(sem(f"x_out{l}"), 1)
                    lo(UNITS[f"gate{l}"] + i + R)
                    if l == 0 and i:
                        prenorm_lo("mixpre1", 1, i - 1, 64)
                if l == 0:
                    prenorm_lo("mixpre1", 1, 7, 64)
            copy_y(dve, 3)
            copy_y(dve, 5)


_OUTS = [
    ("y_prompt", (1, TP, D)), ("y_sample", (1, TS, D)),
    ("p_fox_k", (1, 1, TP, NH, HD)), ("p_fox_v", (1, 1, TP, NH, HD)), ("p_fox_logf", (1, 1, TP, NH)),
    ("p_swa_k", (1, 1, P, 2, HD)), ("p_swa_v", (1, 1, P, 2, HD)),
    ("p_ml_c", (1, 1, MH, DK, DV)), ("p_ml_n", (1, 1, MH, DK)), ("p_ml_m", (1, 1, MH)), ("p_conv", (2, 1, 2, FF)),
    ("s_fox_k", (1, 1, TS, NH, HD)), ("s_fox_v", (1, 1, TS, NH, HD)), ("s_fox_logf", (1, 1, TS, NH)),
    ("s_swa_k", (1, 1, P, 2, HD)), ("s_swa_v", (1, 1, P, 2, HD)),
    ("s_ml_c", (1, 1, MH, DK, DV)), ("s_ml_n", (1, 1, MH, DK)), ("s_ml_m", (1, 1, MH)), ("s_conv", (2, 1, 2, FF)),
]
_SQUEEZED = {"p_fox_k", "p_fox_v", "p_fox_logf"}


def kernel(**inputs):
    import numpy as np
    import concourse.bacc as bacc
    from concourse.bass_utils import run_bass_kernel_spmd as run

    nc = bacc.Bacc("TRN2", target_bir_lowering=False, num_devices=1)
    arrays, ins = {}, {}
    for name, a in inputs.items():
        a = np.ascontiguousarray(a)
        arrays[f"in_{name}"] = a
        ins[name] = nc.dram_tensor(f"in_{name}", a.shape, F32, kind="ExternalInput").ap()
    outs = {n: nc.dram_tensor(f"out_{n}", s, F32, kind="ExternalOutput").ap() for n, s in _OUTS}
    encoder_step(nc, ins, outs)
    r = run(nc, [arrays], core_ids=[0]).results[0]
    return tuple(r[f"out_{n}"] for n, _ in _OUTS)
```

```python
from contextlib import ExitStack

import concourse.bass as bass
from concourse import mybir

ACT = mybir.ActivationFunctionType
ALU = mybir.AluOpType
F32 = mybir.dt.float32
F32R = mybir.dt.float32r
X = mybir.AxisListType.X

P = 128
D = 1024
KT = D // P
TP, TS = 256, 64
T = TP + TS
CH = 64
FF = 4096
FT = FF // P
PAST = 256
HD = 64
NH = 8
MH, DK, DV = 4, 128, 256
EPS = 1e-6
NEG = -1e30
R = 4
TOK = [(0, 128), (128, 128), (256, 64)]

ATT_COLS = [P * j for j in range(12)] + [1544 + P * j for j in range(6)]
REC_COLS = ([P * j for j in range(8)] + [2056 + P * j for j in range(6)] + [1024 + P * j for j in range(8)]
            + [2056 + P * j for j in (6, 7)])
CHUNKS = [0, 4, 1, 2, 3]
ROWS = [2, 0, 1]
UNITS, at = {}, 0
for l, n_in in ((0, len(ATT_COLS)), (1, len(REC_COLS))):
    for name, n in ((f"in{l}", n_in), (f"out{l}", 8), (f"up{l}", 2 * FT), (f"down{l}", FT), (f"ple{l}", 2), (f"gate{l}", 8)):
        UNITS[name] = at
        at += n
N_UNITS = at

AHEAD = 3


def attention_tasks():
    return [(fox, h, t) for fox in (True, False) for h in range(NH) for t in range(3)]


TASKS = attention_tasks()
SKEW_T, SKEW_V = 3, 5
HALF_AT = [0, 2, 4, 6, 8, 10, 12, 14, 16, 18, 19, 20]
TOK_AT = [1, 2, 3, 21, 22, 23]


def attention_events():
    out = []
    for i in range(len(TASKS) + SKEW_V):
        if i < len(TASKS):
            out.append(("scores", i))
        if i > SKEW_V and (i - SKEW_V) % 6 == 0:
            out.append(("o_read", (i - SKEW_V) // 6 - 1))
        for n, at in enumerate(HALF_AT):
            if at == i:
                out.append(("half", 12 + n // 2, n % 2))
        if 0 <= i - SKEW_T < len(TASKS):
            out.append(("turn", i - SKEW_T))
        if 0 <= i - SKEW_V:
            out.append(("values", i - SKEW_V))
        for n, at in enumerate(TOK_AT):
            if at == i:
                out.append(("tok", 3 + n))
    return out


def recurrent_events():
    out = [("unit", 0), ("stats",), ("unit", 1), ("unit", 2), ("unit", 3), ("narrow",), ("unit", 4), ("unit", 5), ("unit", 6), ("gates",),
           ("unit", 7), ("sums",), ("unit", 8), ("arow",), ("unit", 9), ("spread", 0), ("spread", 1), ("unit", 10), ("spread", 2)]
    out += [("ktok", t) for t in range(3)] + [("maxima",)]
    out += [("unit", 11), ("unit", 12), ("unit", 13), ("qk", 0), ("unit", 14), ("wT", 0), ("qk", 1), ("unit", 15), ("wT", 1), ("qk", 2), ("wT", 2)]
    for h in range(MH):
        half = [("half", 16 + 2 * h + n // 2, n % 2) for n in range(4)]
        out += [("vtok", h, t) for t in range(3)]
        out += [("add", h, 0), ("inter", h, 0), ("add", h, 1), ("inter", h, 1), half[0], ("add", h, 2), ("inter", h, 2), ("intra", h, 0)]
        out += ([("heads", h - 1)] if h else []) + [half[1], ("add", h, 3), ("inter", h, 3), ("intra", h, 1), half[2], ("add", h, 4),
                                                    ("inter", h, 4), half[3], ("intra", h, 2)]
    return out + [("heads", MH - 1)]


TURNS_AT = {4: [("par", 2), ("par", 3)], 5: [("pe", 0), ("pe", 1)], 6: [("narrow0", 0)], 7: [("pe", 2), ("pe", 3)],
            8: [("cache", 0), ("cache", 1)], 9: [("cache", 2), ("cache", 3)], 11: [("cache", 4)]}


def group_order():
    o = [("x", j) for j in range(4)] + [("par", 1)] + [("x", j) for j in range(4, KT)] + [("par", 0)] + [("in0", i) for i in range(4)]
    for i in range(4, 12):
        o += TURNS_AT.get(i, []) + [("in0", i)]
    o += [("tok", t) for t in range(3)]
    for e in attention_events():
        if e[0] == "half" and e[2] == 0:
            o.append(("in0", e[1]))
        elif e[0] == "values" and e[1] % 6 == 0:
            o.append(("o", e[1] // 6))
        elif e[0] == "tok":
            o.append(e)
    for l in range(2):
        if l:
            for e in recurrent_events():
                if e[0] == "unit" or (e[0] == "half" and e[2] == 0):
                    o.append(("in1", e[1]))
                elif e[0] == "narrow":
                    o.append(("narrow1", 0))
                elif e[0] == "ktok":
                    o.append(("ktok", e[1]))
                elif e[0] in ("vtok", "intra"):
                    o.append((e[0], 3 * e[1] + e[2]))
                elif e[0] == "heads":
                    o += [("heads", 2 * e[1]), ("heads", 2 * e[1] + 1)]
        o += [(f"out{l}", i) for i in range(8)] + [(f"up{l}", i) for i in range(2 * FT)]
        o += [(f"down{l}", 0), (f"cs{l}", 0)] + [(f"down{l}", i) for i in range(1, 8)] + [(f"ple{l}", i) for i in range(8)]
        o += [(f"gate{l}", i) for i in range(8 if l == 0 else 7)]
    return o + [("y", 0), ("y", 1), ("y", 2), ("gate1", 7), ("y", 3), ("y", 4), ("y", 5)]


GROUPS = {key: n for n, key in enumerate(group_order())}
assert len(GROUPS) == len(group_order())

NORMS = {f"{stage}{l}": 4 * l + i for l in range(2) for i, stage in enumerate(("mixpre", "mixpost", "ffnpre", "ffnpost"))}


def eights(stage, j):
    return 8 * (NORMS[stage] // 2) + j + 1


def encoder_step(nc, I, O):
    ctx = ExitStack()
    with ctx:
        def sb(name, shape, dt=F32):
            return ctx.enter_context(nc.sbuf_tensor(name, shape, dt))

        made = {}

        def sem(name):
            if name not in made:
                made[name] = ctx.enter_context(nc.semaphore(name))

            return made[name]

        ARENA = 2 * FT * T * 4
        arena = sb("arena", [P, ARENA // 4])
        nc_at = nc.alloc_sbuf_tensor_at
        base = nc.sbuf_base - ARENA
        FH = nc_at("hidden_hi", [P, FT, T], F32R, offset=base)
        FL = nc_at("hidden_lo", [P, FT, T], F32R, offset=base + FT * T * 4)
        scr0 = base + 8 * T * 4
        scr1 = base + FT * T * 4 + 24 * T * 4
        OH, OL = FH[:, 0:8, :], FL[:, 24:32, :]
        cursor = [scr0]

        def scratch(name, shape, dt=F32):
            n = 4
            for s in shape[1:]:
                n *= s
            a = cursor[0]
            cursor[0] += (n + 31) // 32 * 32
            assert cursor[0] <= scr1, (name, cursor[0] - scr1)
            return nc_at(name, shape, dt, offset=a)

        xtok = scratch("xtok", [P, 3, D])
        petok = scratch("petok", [P, 2, 3, 256])
        prow = scratch("prow", [P, 2, P])
        nrow = scratch("nrow", [P, 2, P])
        pef = scratch("pef", [P, 4, T])
        wnr = scratch("wnr", [P, 2, KT, 8])
        kcache = scratch("kcache", [P, 2, 512])
        startup_end = cursor[0]
        cursor[0] = scr0
        Frow = scratch("Frow", [NH, TP + PAST + TS])
        lfz = scratch("lfz", [NH, 3, T])
        kcT = scratch("kcT", [P, 4, PAST])
        kcdup = scratch("kcdup", [P, 2, P])
        assert cursor[0] <= scr0 + 3 * D * 4
        Ktok = scratch("Ktok", [P, 3, 512])
        Vtok = scratch("Vtok", [P, 3, 512])
        Stok = scratch("Stok", [P, 3, 256])
        PT = scratch("PT", [P, 4, 384])
        cursor[0] = max(cursor[0], startup_end)
        kT = scratch("kT", [P, 4, T])
        kdup = scratch("kdup", [P, 2, T])
        kplain = scratch("kplain", [P, T])
        MFox = scratch("MFox", [P, 384])
        MSwa = scratch("MSwa", [P, 256])
        vcache = scratch("vcache", [P, 2, 512])
        kcs = scratch("kcs", [P, P])
        vcs = scratch("vcs", [P, P])
        clf = scratch("clf", [P, 2, NH])
        sinkb = scratch("sinkb", [P, NH])
        FrowR = scratch("FrowR", [104, TP + PAST + TS], F32R)
        selR = scratch("selR", [104, NH], F32R)
        S_sb = scratch("S_sb", [P, 6, T + 2])
        lftok = scratch("lftok", [P, 3, NH])
        Ftok = scratch("Ftok", [P, 3, NH])
        amax = scratch("amax", [P, 6, 1])
        aden = scratch("aden", [P, 6, 1])
        ainv = scratch("ainv", [P, 6, 1])
        cursor[0] = scr0
        sig = scratch("sig", [P, 8, T])
        Vaug = scratch("Vaug", [P, 2, 3, DV + 1])
        KmT = scratch("Ktok1", [P, 3, 512])
        Dm = scratch("Dm", [P, 3, MH, P])
        wT = scratch("wT", [P, 3, 512])
        C = scratch("C", [P, 2, MH, DV + 1])
        mz = scratch("mz", [8, 4, T])
        gt = scratch("gates_tok", [P, 3, 16])
        ml = {n: scratch("ml_" + n, [P, 3, MH]) for n in
              ("bt", "a", "M", "mp", "muL", "mu", "nmu", "sdec", "em", "g", "t0", "lf")}
        MF = scratch("MF", [P, 3, MH, 2])
        BL = scratch("BL", [P, 2, 12])
        mprev = scratch("mprev", [P, 6, MH])
        muc = scratch("muc", [P, 5, MH])
        scd = scratch("scd", [P, 5, MH])
        aT = scratch("aT", [12, P])
        Y = scratch("Y", [P, 2, 3, DV + 1])
        yf = {n: scratch("y_" + n, [P, 2, 3]) for n in ("den", "r", "ss", "v", "w", "f")}
        Ysq = scratch("Ysq", [P, DV])

        xT = sb("xT", [P, KT, T])
        hH = sb("hH", [P, KT, T], F32R)
        hL = sb("hL", [P, KT, T], F32R)
        mix = sb("mix", [P, KT, T])
        sqb = sb("sqb", [P, KT, T])
        raw = sb("raw", [P, R, D])
        wh = sb("wh", [P, R, D], F32R)
        wl = sb("wl", [P, R, D], F32R)
        gp = sb("gp", [P, 2, T + 4])
        cv = sb("cv", [P, 2, T + 2])
        us = sb("us", [P, 2, T])
        fb = sb("fb", [P, 2, T])
        obuf = fb
        diag = cv[:].rearrange("p s t -> p (s t)")[:, 0:3 * P].rearrange("p (t c) -> p t c", t=3)
        rstd = sb("rstd", [P, T])
        rstd2 = sb("rstd2", [P, T])
        PC = sb("PC", [P, 2, P])
        NC = sb("NC", [P, 2, P])
        cs = sb("cs", [P, 4, FT])
        csT = sb("csT", [P, P])
        peH = sb("peH", [P, 4, T], F32R)
        peL = sb("peL", [P, 4, T], F32R)
        wnH = sb("wnH", [P, 2, KT, 8], F32R)
        wnL = sb("wnL", [P, 2, KT, 8], F32R)
        ident = sb("ident", [P, P])
        ones = sb("ones", [P, P])
        Ut = sb("Ut", [P, P])
        Ub = sb("Ub", [P, P])
        MBlk = sb("MBlk", [P, P])
        cst = sb("cst", [P, 5])
        mark = sb("mark", [1, 1])
        ms = sb("ms", [P, 3])
        rcol = sb("rcol", [P, 3])
        bcol = sb("bcol", [8, 4])
        sgb = us

        bank = [ctx.enter_context(nc.psum_tensor(f"bank{i}", [P, 512], F32)) for i in range(8)]

        raw_landed = [sem(f"raw_landed{i}") for i in range(R)]
        hi_ready, lo_ready, unit_used = sem("hi_ready"), sem("lo_ready"), sem("unit_used")
        bank_done = [sem(f"bank_done{i}") for i in range(4)]

        def gid(name, i=0):
            return GROUPS[name, i]

        def gbank(g):
            return bank[g % 4]

        READ = {}

        def read_by(name, signal, n, first=1):
            for i in range(n):
                READ[gid(name, i)] = (signal, first + i)

        for n, i in enumerate((1, 0, 2, 3)):
            READ[gid("par", i)] = ("par_in", n + 1)
        for name, signal, n in (("x", "x_in", 8), ("pe", "pe_f", 4), ("cache", "cache_read", 5), ("in0", "in_read0", 18),
                                ("narrow0", "narrow_step0", 1), ("tok", "tok_read", 9), ("o", "o_lo0", 8), ("in1", "in_read1", 24),
                                ("narrow1", "narrow_step1", 1), ("ktok", "ktok_read", 3), ("vtok", "vtok_read", 12), ("intra", "Y", 12),
                                ("heads", "mo_f", 8)):
            read_by(name, signal, n)
        for i in range(6):
            READ[gid("y", i)] = ("ytok", i + 1)
        for l in range(2):
            for name, signal, n in (("cs", "csT", 1), ("ple", "ple_sb", 8), ("gate", "sigm", 8)):
                read_by(f"{name}{l}", f"{signal}{l}", n)
            read_by(f"out{l}", f"mix_{l}", 8)
            read_by(f"down{l}", f"mixf_{l}", 8)
            for i in range(2 * FT):
                READ[gid(f"up{l}", i)] = (("us" if i % 2 else "gp") + str(l), i // 2 + 1)

        FULL, uses = {}, [0] * 4
        for l in range(2):
            for i in range(len(ATT_COLS) if l == 0 else len(REC_COLS)):
                FULL[gid(f"in{l}", i)] = (unit_used, UNITS[f"in{l}"] + i + 1)
            for i in range(8):
                FULL[gid(f"out{l}", i)] = (unit_used, UNITS[f"out{l}"] + i + 1)
                FULL[gid(f"down{l}", i)] = (unit_used, UNITS[f"down{l}"] + 4 * i + 4)
                FULL[gid(f"gate{l}", i)] = (unit_used, UNITS[f"gate{l}"] + i + 1)
            for i in range(2 * FT):
                FULL[gid(f"up{l}", i)] = (unit_used, UNITS[f"up{l}"] + i + 1)
            for i in (3, 7):
                FULL[gid(f"ple{l}", i)] = (unit_used, UNITS[f"ple{l}"] + i // 4 + 1)
        for i in range(8):
            FULL[gid("o", i)] = (sem("pv_done"), 6 * (i + 1))
        for gi in range(len(GROUPS)):
            if gi not in FULL:
                uses[gi % 4] += 1
                FULL[gi] = (bank_done[gi % 4], uses[gi % 4])

        def bank_free(eng, g):
            if g >= 4:
                name, value = READ[g - 4]
                eng.wait_ge(sem(name), value)

        def bank_full(eng, g, it=0):
            signal, value = FULL[g]
            eng.wait_ge(signal, value + it)

        def copy_y(eng, i):
            half, t = i // 3, i % 3
            gi, n = gid("y", i), TOK[t][1]
            bank_full(eng, gi)
            dst, src = xtok[0:n, t, half * 512:(half + 1) * 512], gbank(gi)[0:n, :]
            if i in (3, 5):
                nc.vector.tensor_copy(dst, src).then_inc(sem("ytok_v"), 1)
            else:
                nc.scalar.activation(dst, src, ACT.Copy).then_inc(sem("ytok"), 1)

        def x_added(eng, stage, j):
            eng.wait_ge(sem("x_odd" if j % 2 else "x_even"), 4 * (NORMS[stage] // 2) + j // 2 + 1)

        def add_squares(eng, ops, stage):
            for j in range(1, KT - 1):
                k = (KT - 2) * NORMS[stage] + j
                eng.wait_ge(sem("sq"), 8 * NORMS[stage] + j + 1)
                if j > 1:
                    eng.wait_ge(sem("sq_added"), k - 1)
                ops.tensor_tensor(sqb[:, 0, :], sqb[:, 0, :], sqb[:, j, :], ALU.add).then_inc(sem("sq_added"), 1)

        def score_width(i):
            fox, h, t = TASKS[i]
            return TOK[t][0] + P if fox and t < 2 else PAST + TS if fox else TOK[t][0] + P + 1 if t < 2 else P + TS + 1

        block = ctx.enter_context(nc.Block())

        @block.sync
        def _(sp):
            sp.dma_start(xtok[:, 0, :], I["x_prompt"][0, 0:P]).then_inc(sem("ld_x"), 16)
            sp.dma_start(xtok[:, 1, :], I["x_prompt"][0, P:TP]).then_inc(sem("ld_x"), 16)
            sp.dma_start(xtok[0:TS, 2, :], I["x_sample"][0]).then_inc(sem("ld_x"), 16)

            def col_unit(w, c):
                return w[:, c:c + P].rearrange("(k p) c -> p k c", p=P)

            def load(u, src):
                if u >= R:
                    sp.wait_ge(lo_ready, u - R + 1)
                dst = raw[:, u % R, :].rearrange("p (k c) -> p k c", k=src.shape[1])
                sp.dma_start(dst, src).then_inc(raw_landed[u % R], 16)

            for l in range(2):
                w_in, cols, w_out = (I["w_att_in"], ATT_COLS, I["w_att_out"]) if l == 0 else (I["w_rec_in"], REC_COLS, I["w_rec_out"])
                for i, c in enumerate(cols):
                    load(UNITS[f"in{l}"] + i, col_unit(w_in[0], c))
                for i in range(8):
                    load(UNITS[f"out{l}"] + i, col_unit(w_out[0], i * P))
                u0 = UNITS[f"up{l}"]
                with sp.Fori(0, FT // 2) as it:
                    for s in range(4):
                        u = u0 + s
                        sp.wait_ge(lo_ready, it * 4 + (u - R + 1))
                        c = it * (2 * P) + (s // 2) * P + (s % 2) * FF
                        src = I["w_ffn_up"][l][:, bass.ds(c, P)].rearrange("(k p) c -> p k c", p=P)
                        dst = raw[:, u % R, :].rearrange("p (k c) -> p k c", k=KT)
                        sp.dma_start(dst, src).then_inc(raw_landed[u % R], 16)
                u0 = UNITS[f"down{l}"]
                with sp.Fori(0, KT) as it:
                    for s in range(4):
                        u = u0 + s
                        sp.wait_ge(lo_ready, it * 4 + (u - R + 1))
                        src = I["w_ffn_down"][l][s * D:(s + 1) * D, bass.ds(it * P, P)].rearrange("(k p) c -> p k c", p=P)
                        dst = raw[:, u % R, :].rearrange("p (k c) -> p k c", k=KT)
                        sp.dma_start(dst, src).then_inc(raw_landed[u % R], 16)
                for i in range(2):
                    load(UNITS[f"ple{l}"] + i, I["w_ple"][l][:, i * 512:(i + 1) * 512].rearrange("(k p) c -> p k c", p=P))
                for i in range(8):
                    load(UNITS[f"gate{l}"] + i, col_unit(I["w_ple_gate"][l], i * P))

            def store_y(t, half):
                n = TOK[t][1]
                dst = O["y_prompt"][0, t * P:t * P + P] if t < 2 else O["y_sample"][0]
                c = slice(half * 512, (half + 1) * 512)
                sp.dma_start(dst[:, c], xtok[0:n, t, c]).then_inc(sem("y_stored"), 16)

            for t in range(3):
                sp.wait_ge(sem("ytok"), t + 1)
                store_y(t, 0)
            for t, signal, value in ((0, "ytok_v", 1), (1, "ytok", 4), (2, "ytok_v", 2)):
                sp.wait_ge(sem(signal), value)
                store_y(t, 1)
            sp.wait_ge(sem("y_stored"), 16 * 6)

        @block.gpsimd
        def _(pool):
            g = nc.gpsimd
            ch = sem("const_step")
            n = [0]

            def link(ins):
                n[0] += 1
                ins.then_inc(ch, 1)
                pool.wait_ge(ch, n[0])

            link(g.memset(ident[:], 0.0))
            link(g.affine_select(out=ident[:], in_=ident[:], compare_op=ALU.not_equal, fill=1.0, base=0,
                                 pattern=[[-1, P]], channel_multiplier=1))
            g.memset(mark[:], 0.0)
            g.memset(cst[:, 2:5], -0.5)
            link(g.memset(cst[:, 1:2], 1.0))
            g.memset(ones[:], 1.0).then_inc(sem("const"), 1)
            par, ld_pe, ld_cache = sem("ld_par1"), sem("ld_pe"), sem("ld_cache")
            pool.dma_start(prow[0:96, 1, :], I["ffn_conv_w"][1].rearrange("t (j c) -> (t j) c", c=P)).then_inc(par, 16)
            pool.dma_start(prow[96:128, 1, :], I["ffn_conv_b"][1].rearrange("(j c) -> j c", c=P)).then_inc(par, 16)
            pool.dma_start(nrow[0:64, 1, :], I["state_ffn_conv"][1, 0].rearrange("r (j c) -> (r j) c", c=P)).then_inc(par, 16)
            for i, nm in enumerate(("ln_mix_pre", "ln_mix_post", "ln_ffn_pre", "ln_ffn_post")):
                pool.dma_start(nrow[64 + 8 * i:72 + 8 * i, 1, :], I[nm][1].rearrange("(j c) -> j c", c=P)).then_inc(par, 16)
            pool.dma_start(nrow[96:104, 1, :], I["rec_norm"][0].rearrange("(j c) -> j c", c=P)).then_inc(par, 16)
            for l in range(2):
                pool.dma_start(petok[:, l, 0:2, :], I["p_prompt"][l, 0].rearrange("(t p) d -> p t d", p=P)).then_inc(ld_pe, 16)
                pool.dma_start(petok[0:TS, l, 2, :], I["p_sample"][l, 0]).then_inc(ld_pe, 16)
            pool.dma_start(bcol[:, 0:1], I["fox_fb"].rearrange("a h -> h a"), allow_slow_non_contiguous=True).then_inc(sem("ld_bias"), 16)
            pool.dma_start(bcol[0:4, 1:2], I["rec_ig_b"].rearrange("a h -> h a"), allow_slow_non_contiguous=True).then_inc(sem("ld_bias"), 16)
            pool.dma_start(bcol[4:8, 1:2], I["rec_fg_b"].rearrange("a h -> h a"), allow_slow_non_contiguous=True).then_inc(sem("ld_bias"), 16)
            pool.dma_start(kcache[:], I["cache_fox_k"][0, 0].rearrange("(t p) h d -> p t (h d)", p=P)).then_inc(ld_cache, 16)
            pool.dma_start(vcache[:], I["cache_fox_v"][0, 0].rearrange("(t p) h d -> p t (h d)", p=P)).then_inc(ld_cache, 16)
            pool.dma_start(kcs[:], I["cache_swa_k"][0, 0].rearrange("p h d -> p (h d)")).then_inc(ld_cache, 16)
            pool.dma_start(vcs[:], I["cache_swa_v"][0, 0].rearrange("p h d -> p (h d)")).then_inc(ld_cache, 16)
            pool.dma_start(clf[:], I["cache_fox_logf"][0, 0].rearrange("(t p) h -> p t h", p=P)).then_inc(ld_cache, 16)
            pool.dma_start(sinkb[:], I["swa_sink"][0:1, :].to_broadcast([P, NH])).then_inc(ld_cache, 16)
            link(g.memset(Ut[:], 1.0))
            link(g.affine_select(out=Ut[:], in_=Ut[:], compare_op=ALU.is_ge, fill=0.0, base=0, pattern=[[1, P]], channel_multiplier=-1))
            link(g.tensor_copy(Ub[:], Ut[:]))
            link(g.memset(Ub[0:64, 64:128], 0.0))
            link(g.memset(MFox[:], 0.0))
            link(g.affine_select(out=MFox[:, 256:384], in_=MFox[:, 256:384], compare_op=ALU.is_ge, fill=NEG, base=0,
                                 pattern=[[-1, P]], channel_multiplier=1))
            link(g.tensor_copy(MBlk[:], MFox[:, 256:384]))
            link(g.memset(MBlk[64:128, 0:64], NEG))
            link(g.memset(MSwa[:], 0.0))
            link(g.memset(MSwa[64:128, 0:64], NEG))
            link(g.memset(MSwa[0:64, 192:256], NEG))
            link(g.memset(FrowR[:].bitcast(F32), 0.0))
            link(g.memset(selR[:].bitcast(F32), 0.0))
            g.memset(gp[:], 0.0).then_inc(sem("const2"), 1)

            st = sem("stored")
            n_st = [0]

            def store(dst, src, short_rows=False):
                pool.dma_start(dst, src, allow_slow_non_contiguous=short_rows).then_inc(st, 16)
                n_st[0] += 1

            def inverse_rms(stage):
                pool.wait_ge(sem("ms"), NORMS[stage] + 1)
                g.tensor_tensor(rcol[:], ms[:], cst[:, 2:5], ALU.pow).then_inc(sem("rcol"), 1)

            def post_odd(stage):
                inverse_rms(stage)
                pool.wait_ge(sem("rms_copied"), NORMS[stage] // 2 + 1)
                for j in range(1, KT, 2):
                    k = 4 * (NORMS[stage] // 2) + j // 2 + 1
                    g.tensor_tensor(mix[:, j, :], mix[:, j, :], rstd2[:], ALU.mult).then_inc(sem("post_odd"), 1)
                    pool.wait_ge(sem("post_odd"), k)
                    g.tensor_tensor(xT[:, j, :], xT[:, j, :], mix[:, j, :], ALU.add).then_inc(sem("x_odd"), 1)

            inverse_rms("mixpre0")
            for l in range(2):
                if l == 0:
                    pool.wait_ge(ld_cache, 16 * 6)
                    store(O["s_swa_k"][0, 0, 0:64].rearrange("p h d -> p (h d)"), kcs[64:128, :])
                    store(O["s_swa_v"][0, 0, 0:64].rearrange("p h d -> p (h d)"), vcs[64:128, :])
                    pool.wait_ge(sem("lf_tok"), 1)
                    store(O["p_fox_logf"][0, 0].rearrange("(t p) h -> p t h", p=P), lftok[:, 0:2, :])
                    store(O["s_fox_logf"][0, 0], lftok[0:TS, 2, :])
                    for i in range(len(TASKS)):
                        n_q, w, b = TOK[TASKS[i][2]][1], score_width(i), i % 6
                        pool.wait_ge(sem("a_inv"), i + 1)
                        g.tensor_scalar(S_sb[0:n_q, b, 0:w], S_sb[0:n_q, b, 0:w], ainv[0:n_q, b, :], None, ALU.mult).then_inc(sem("p_ready"), 1)
                    pool.wait_ge(sem("tok_read"), 9)
                    for nm, tt in (("k", Ktok), ("v", Vtok)):
                        store(O[f"p_fox_{nm}"][0, 0].rearrange("(t p) h d -> p t (h d)", p=P), tt[:, 0:2, :])
                        store(O[f"s_fox_{nm}"][0, 0].rearrange("p h d -> p (h d)"), tt[0:TS, 2, :])
                    for i, nm in enumerate(("k", "v")):
                        store(O[f"p_swa_{nm}"][0, 0].rearrange("p h d -> p (h d)"), Stok[:, 1, i * P:(i + 1) * P])
                        store(O[f"s_swa_{nm}"][0, 0, 64:128].rearrange("p h d -> p (h d)"), Stok[0:TS, 2, i * P:(i + 1) * P])
                else:
                    add_squares(pool, g, "mixpre1")
                    inverse_rms("mixpre1")
                    signal, value = FULL[gid("gate0", 7)]
                    pool.wait_ge(signal, value)
                    pool.dma_start(C[:, 1, :, 0:DV], I["state_mlstm_c"][0, 0].rearrange("h k v -> k h v")).then_inc(sem("ld_state"), 16)
                    pool.dma_start(C[:, 1, :, DV:DV + 1], I["state_mlstm_n"][0, 0].rearrange("h (k a) -> k h a", a=1),
                                   allow_slow_non_contiguous=True).then_inc(sem("ld_state"), 16)
                    pool.dma_start(mprev[:, 4, :], I["state_mlstm_m"][0].to_broadcast([P, MH])).then_inc(sem("ld_state"), 16)
                    for h in range(MH):
                        pool.wait_ge(sem("Yvar"), h + 1)
                        g.tensor_tensor(yf["w"][:, h % 2, :], yf["v"][:, h % 2, :], cst[:, 2:5], ALU.pow).then_inc(sem("Yroot"), 1)
                    pool.wait_ge(sem("C_new"), 20)
                    for b, pre in ((0, "p"), (1, "s")):
                        store(O[f"{pre}_ml_c"][0, 0].rearrange("h k v -> k h v"), C[:, b, :, 0:DV])
                        store(O[f"{pre}_ml_n"][0, 0].rearrange("h (k a) -> k h a", a=1), C[:, b, :, DV:DV + 1], True)
                    store(O["p_ml_m"][0], mprev[0:1, 5, :])
                    store(O["s_ml_m"][0], mz[0:1, 3, 0:4])
                add_squares(pool, g, f"mixpost{l}")
                post_odd(f"mixpost{l}")
                pool.wait_ge(st, 16 * n_st[0])
                pool.sem_inc(sem(f"scratch_out{l}"), 1)
                add_squares(pool, g, f"ffnpre{l}")
                inverse_rms(f"ffnpre{l}")
                with pool.Fori(0, FT // 2) as it:
                    for s in range(2):
                        pool.wait_ge(sem(f"gelu{l}"), it * 2 + (s + 1))
                        pool.wait_ge(sem(f"us{l}"), it * 2 + (s + 1))
                        g.tensor_tensor(fb[:, s, 0:TP], cv[:, s, 0:TP], us[:, s, 0:TP], ALU.mult)
                        g.tensor_tensor(fb[:, s, TP:T], cv[:, s, TP + 2:T + 2], us[:, s, TP:T], ALU.mult)
                        tail = gp[:, s, 192:324].rearrange("p (b r) -> p b r", b=2)[:, :, 64:66]
                        dst = cs[:, :, bass.ds(it * 2 + s, 1)].rearrange("p (b r) j -> p b (r j)", b=2)
                        g.tensor_copy(dst, tail).then_inc(sem(f"f{l}"), 1)
                pool.wait_ge(sem(f"csT{l}"), 1)
                store(O["p_conv"][l, 0].rearrange("r (j c) -> (r j) c", c=P), csT[0:64, :])
                store(O["s_conv"][l, 0].rearrange("r (j c) -> (r j) c", c=P), csT[64:128, :])
                add_squares(pool, g, f"ffnpost{l}")
                post_odd(f"ffnpost{l}")
                pool.wait_ge(st, 16 * n_st[0])

        @block.tensor
        def _(pe):
            mmul = nc.tensor.matmul
            trans = nc.tensor.transpose

            def block3(u, k, out, rh, rl, first, last):
                a, b = wh[:, u % R, k * P:(k + 1) * P], wl[:, u % R, k * P:(k + 1) * P]
                mmul(out, a, rh[:, k, :], start=first and k == 0, stop=False)
                mmul(out, a, rl[:, k, :], start=False, stop=False)
                m = mmul(out, b, rh[:, k, :], start=False, stop=last and k == 7)
                if k == 7:
                    m.then_inc(unit_used, 1)

            def unit(u, out, rh, rl, first=True, last=True, hook=None, it=0, ks=range(8)):
                if 0 in ks:
                    pe.wait_ge(lo_ready, it + (u + 1))
                for k in ks:
                    if hook:
                        hook(k)
                    block3(u, k, out, rh, rl, first, last)

            def ahead(us, gs, rh, rl, k_wait):
                for k in range(8):
                    k_wait(k)
                    for u, gi in zip(us, gs):
                        if k == 0:
                            bank_free(pe, gi)
                            pe.wait_ge(lo_ready, u + 1)
                        block3(u, k, gbank(gi)[:, 0:T], rh, rl, True, True)

            def stats(stage):
                for j in (0, KT - 1):
                    if j:
                        pe.wait_ge(sem("sq"), 8 * NORMS[stage] + KT)
                    else:
                        pe.wait_ge(sem("sq_added"), (KT - 2) * (NORMS[stage] + 1))
                    for t, c in enumerate((0, P, T - P)):
                        m = mmul(bank[4][:, t:t + 1], sqb[:, j, c:c + P], ones[:, 0:1], start=j == 0 and t == 0, stop=j > 0,
                                 skip_group_check=True)
                m.then_inc(sem("sq_sum"), 1)

            def spread_rms(stage, b=5, signal="rms_rows"):
                for t, (t0, n) in enumerate(TOK):
                    pe.wait_ge(sem("diag"), 3 * NORMS[stage] + t + 1)
                    m = mmul(bank[b][:, t0:t0 + n], ones[:], diag[:, t, P - n:P], start=True, stop=True)
                m.then_inc(sem(signal), 1)

            def spread_post(stage):
                spread_rms(stage)
                spread_rms(stage, 7, "rms_again")

            def rms_at(stage, at):
                return lambda k: spread_rms(stage) if k == at else None

            def turn_rows(gi, n_rows, src, col):
                for t, (t0, n) in enumerate(TOK):
                    m = trans(gbank(gi)[:, t0:t0 + n], src(t, n)[:, col * P:(col + 1) * P], ident[0:n, 0:n])
                m.then_inc(bank_done[gi % 4], 1)

            pe.wait_ge(sem("const"), 1)
            pe.wait_ge(sem("const_step"), 3)

            def parameters(i):
                l, rows = i // 2, (prow, nrow)[i % 2]
                n = (P, 96 + 8 * l)[i % 2]
                gi = gid("par", i)
                bank_free(pe, gi)
                trans(gbank(gi)[:, 0:n], rows[0:n, l, :], ident[0:n, 0:n]).then_inc(bank_done[gi % 4], 1)

            pe.wait_ge(sem("ld_x"), 48)
            for j in range(KT):
                gi = gid("x", j)
                bank_free(pe, gi)
                turn_rows(gi, T, lambda t, n: xtok[0:n, t, :], j)
                if j == 3:
                    pe.wait_ge(sem("ld_norms0"), 16 * 5)
                    parameters(1)
            pe.wait_ge(sem("ld_par0"), 16 * 2)
            parameters(0)

            def narrow(l):
                gi = gid(f"narrow{l}", 0)
                bank_free(pe, gi)
                pe.wait_ge(sem("narrow_split"), 1)
                out = gbank(gi)[0:8, 0:T]
                for k in range(KT):
                    mmul(out, wnH[:, l, k, :], hH[:, k, :], start=k == 0, stop=False)
                    mmul(out, wnH[:, l, k, :], hL[:, k, :], start=False, stop=False)
                    m = mmul(out, wnL[:, l, k, :], hH[:, k, :], start=False, stop=k == KT - 1)
                m.then_inc(bank_done[gi % 4], 1)

            def in_unit(l, i, hook=None, ks=range(8)):
                gi = gid(f"in{l}", i)
                if 0 in ks:
                    bank_free(pe, gi)
                unit(UNITS[f"in{l}"] + i, gbank(gi)[:, 0:T], hH, hL, hook=hook, ks=ks)

            def input_attention():
                ahead([UNITS["in0"] + i for i in range(AHEAD)], [gid("in0", i) for i in range(AHEAD)], hH, hL,
                      lambda k: pe.wait_ge(sem("h_lo"), eights("mixpre0", k)))
                stats("mixpre0")
                in_unit(0, 3, rms_at("mixpre0", 6))
                for i in range(4, 12):
                    for kind, j in TURNS_AT.get(i, []):
                        if kind == "narrow0":
                            narrow(0)
                            continue
                        if kind == "par":
                            if j == 2:
                                pe.wait_ge(sem("ld_par1"), 16 * 8)
                            parameters(j)
                            continue
                        gi = gid(kind, j)
                        bank_free(pe, gi)
                        if kind == "pe":
                            if j == 0:
                                pe.wait_ge(sem("ld_pe"), 64)
                            turn_rows(gi, T, lambda t, n: petok[0:n, j // 2, t, :], j % 2)
                        else:
                            if j == 0:
                                pe.wait_ge(sem("ld_cache"), 16 * 6)
                            for t in range(2 if j < 4 else 1):
                                m = trans(gbank(gi)[:, t * P:(t + 1) * P], kcache[:, t, j * P:(j + 1) * P] if j < 4 else kcs[:], ident[:])
                            m.then_inc(bank_done[gi % 4], 1)
                    if i == 8:
                        turn_forget()
                    elif i == 10:
                        sum_forget()
                    in_unit(0, i)
                for t in range(3):
                    turn_tok(t)
                pe.wait_ge(sem("F_rows"), 1)
                for e in attention_events():
                    if e[0] == "scores":
                        scores(e[1])
                    elif e[0] == "half":
                        in_unit(0, e[1], ks=range(4 * e[2], 4 * e[2] + 4))
                    elif e[0] == "tok":
                        turn_tok(e[1])
                    elif e[0] == "turn":
                        turn(e[1])
                    elif e[0] == "values":
                        values(e[1])

            def turn_forget():
                pe.wait_ge(sem("lf_ready"), 1)
                for t, (t0, n) in enumerate(TOK):
                    m = trans(bank[5][0:n, t * 8:t * 8 + 8], lfz[:, 0, t0:t0 + n], ident[0:8, 0:8])
                m.then_inc(sem("lf_tr"), 1)

            def sum_forget():
                pe.wait_ge(sem("const2"), 1)
                pe.wait_ge(sem("lf_tok"), 1)
                L = [lftok[:, 0, :], lftok[:, 1, :], lftok[0:64, 2, :]]
                Cc = [clf[:, 0, :], clf[:, 1, :]]
                U, N1 = Ut[:], ones[:]

                def run_sum(out, terms):
                    for i, (a, b) in enumerate(terms):
                        m = mmul(out, a, b, start=i == 0, stop=i == len(terms) - 1)
                    return m

                run_sum(bank[6][:, 0:8], [(U, L[0])])
                run_sum(bank[6][:, 8:16], [(N1, L[0]), (U, L[1])])
                run_sum(bank[6][0:64, 16:24], [(N1[:, 0:64], Cc[0]), (N1[:, 0:64], Cc[1]), (Ut[0:64, 0:64], L[2])])
                run_sum(bank[7][0:8, 0:128], [(L[0], U)])
                run_sum(bank[7][0:8, 128:256], [(L[0], N1), (L[1], U)])
                run_sum(bank[5][0:8, 0:128], [(Cc[0], U)])
                run_sum(bank[5][0:8, 128:256], [(Cc[0], N1), (Cc[1], U)])
                run_sum(bank[5][0:8, 256:320], [(Cc[0], N1[:, 0:64]), (Cc[1], N1[:, 0:64]), (L[2], Ut[0:64, 0:64])]).then_inc(sem("F_sums"), 1)

            def turn_tok(i):
                kind, t = i // 3, i % 3
                t0, n = TOK[t]
                gi = gid("tok", i)
                bank_free(pe, gi)
                pe.wait_ge(sem("in_read0"), 12 if kind < 2 else 18)
                srcs = [(sqb, kT)[kind][:, j, t0:t0 + n] for j in range(4)] if kind < 2 else [kplain[:, t0:t0 + n], sqb[:, 4, t0:t0 + n]]
                for j, s in enumerate(srcs):
                    m = trans(gbank(gi)[0:n, j * P:(j + 1) * P], s, ident[:])
                m.then_inc(bank_done[gi % 4], 1)

            def scores(i):
                fox, h, t = TASKS[i]
                t0, n = TOK[t]
                hf = 64 * (h % 2)
                if not fox:
                    pe.wait_ge(sem("in_read0"), 18)
                if i >= 2:
                    pe.wait_ge(sem("s_moved"), i - 1)
                b = bank[4 + i % 2]
                q = mix[hf:hf + 64, (0 if fox else 4) + h // 2, t0:t0 + n]
                if fox and t < 2:
                    segs = [(kT[hf:hf + 64, h // 2, 0:t0 + n], 0, 0)]
                elif fox:
                    segs = [(kcT[hf:hf + 64, h // 2, :], 0, TP), (kT[hf:hf + 64, h // 2, TP:T], PAST, TP + PAST)]
                elif t < 2:
                    segs = [(kdup[hf:hf + 64, h // 4, 0:t0 + n], 0, None)]
                else:
                    segs = [(kcdup[hf:hf + 64, h // 4, :], 0, None), (kdup[hf:hf + 64, h // 4, TP:T], P, None)]
                for k, off, fr in segs:
                    w = k.shape[1]
                    m = mmul(b[0:n, off:off + w], q, k, start=True, stop=fr is None)
                    if fr is not None:
                        m = mmul(b[0:n, off:off + w], selR[hf:hf + 40, h:h + 1].to_broadcast([40, n]), FrowR[hf:hf + 40, fr:fr + w], start=False, stop=True)
                m.then_inc(sem("s_done"), 1)

            def blocks(i):
                fox, h, t = TASKS[i]
                c = h * 64 if fox else (h // 4) * 64
                V = Vtok if fox else Stok[:, :, P:2 * P]
                if t < 2:
                    return [(P, V[:, b, c:c + 64]) for b in range(t + 1)]
                if fox:
                    return [(P, vcache[:, b, c:c + 64]) for b in range(2)] + [(64, V[0:64, 2, c:c + 64])]
                return [(P, vcs[:, c:c + 64]), (64, V[0:64, 2, c:c + 64])]

            def turn(i):
                n = TOK[TASKS[i][2]][1]
                pe.wait_ge(sem("p_ready"), i + 1)
                if i >= 2:
                    pe.wait_ge(sem("pt_moved"), i - 1)
                for b, (rows, _) in enumerate(blocks(i)):
                    m = trans(bank[6 + i % 2][0:rows, b * P:b * P + n], S_sb[0:n, i % 6, b * P:b * P + rows], ident[0:n, 0:n])
                m.then_inc(sem("pt_done"), 1)

            def values(i):
                fox, h, t = TASKS[i]
                t0, n = TOK[t]
                gi = gid("o", i // 6)
                if i % 6 == 0:
                    bank_free(pe, gi)
                if i == 0:
                    pe.wait_ge(sem("tok_read"), 3)
                if i == 24:
                    pe.wait_ge(sem("tok_read"), 9)
                pe.wait_ge(sem("pt_moved"), i + 1)
                hf = 64 * (h % 2)
                bl = blocks(i)
                for b, (rows, v) in enumerate(bl):
                    m = mmul(gbank(gi)[hf:hf + 64, t0:t0 + n], v, PT[0:rows, i % 4, b * P:b * P + n], start=b == 0, stop=b == len(bl) - 1)
                m.then_inc(sem("pv_done"), 1)

            def input_recurrent():
                for e in recurrent_events():
                    name, a = e[0], e[1:]
                    if name == "unit":
                        in_unit(1, a[0], (lambda k: pe.wait_ge(sem("h_lo"), eights("mixpre1", k))) if a[0] == 0 else
                                rms_at("mixpre1", 6) if a[0] == 1 else None)
                    elif name == "half":
                        in_unit(1, a[0], ks=range(4 * a[1], 4 * a[1] + 4))
                    elif name == "stats":
                        stats("mixpre1")
                    elif name == "narrow":
                        narrow(1)
                    elif name == "gates":
                        pe.wait_ge(sem("mgates"), 1)
                        for t, (t0, n) in enumerate(TOK):
                            trans(bank[5][0:n, t * 16:t * 16 + 8], mz[:, 0, t0:t0 + n], ident[0:8, 0:8])
                            m = trans(bank[5][0:n, t * 16 + 8:t * 16 + 16], mz[:, 1, t0:t0 + n], ident[0:8, 0:8])
                        m.then_inc(sem("mgates_tr"), 1)
                    elif name == "sums":
                        pe.wait_ge(sem("mlf"), 1)
                        lf = ml["lf"][:].rearrange("p t h -> p (t h)")
                        mmul(bank[6][:, 0:12], Ub[:], lf, start=True, stop=True)
                        mmul(bank[6][:, 16:28], ones[0:64, :], lf[0:64, :], start=True, stop=True)
                        mmul(bank[7][:, 32:44], ones[64:128, :], lf[64:128, :], start=True, stop=True).then_inc(sem("msums"), 1)
                    elif name == "arow":
                        pe.wait_ge(sem("ma"), 1)
                        trans(bank[7][0:12, 0:P], ml["a"][:].rearrange("p t h -> p (t h)"), ident[:]).then_inc(sem("maT"), 1)
                    elif name == "spread":
                        t = a[0]
                        pe.wait_ge(sem("maT_read"), 1)
                        for h in range(MH):
                            r = 4 * t + h
                            m = mmul(bank[5 + t][:, h * P:(h + 1) * P], ident[0:12, r:r + 1].to_broadcast([12, P]), aT[:], start=True, stop=True)
                        m.then_inc(sem("mspread"), 1)
                    elif name == "ktok":
                        t0, n = TOK[a[0]]
                        gi = gid("ktok", a[0])
                        bank_free(pe, gi)
                        pe.wait_ge(sem("in_read1"), 8)
                        for j in range(4):
                            m = trans(gbank(gi)[0:n, j * P:(j + 1) * P], mix[:, 4 + j, t0:t0 + n], ident[:])
                        m.then_inc(bank_done[gi % 4], 1)
                    elif name == "qk":
                        t = a[0]
                        t0, n = TOK[t]
                        pe.wait_ge(sem("in_read1"), 8)
                        if t:
                            pe.wait_ge(sem("mw"), t)
                        for h in range(MH):
                            m = mmul(bank[4][0:n, h * P:h * P + n], mix[:, h, t0:t0 + n], mix[:, 4 + h, t0:t0 + n], start=True, stop=True)
                        m.then_inc(sem("mqk"), 1)
                    elif name == "wT":
                        t = a[0]
                        n = TOK[t][1]
                        pe.wait_ge(sem("mw"), t + 1)
                        if t:
                            pe.wait_ge(sem("mwT_read"), t)
                        for h in range(MH):
                            m = trans(bank[5][0:n, h * P:h * P + n], Dm[0:n, t, h, 0:n], ident[0:n, 0:n])
                        m.then_inc(sem("mwT"), 1)
                    elif name == "vtok":
                        h, t = a
                        t0, n = TOK[t]
                        gi = gid("vtok", 3 * h + t)
                        bank_free(pe, gi)
                        pe.wait_ge(sem("in_read1"), 16 + 2 * h)
                        for v in range(2):
                            m = trans(gbank(gi)[0:n, v * P:(v + 1) * P], sqb[:, 2 * h + v, t0:t0 + n], ident[:])
                        m.then_inc(bank_done[gi % 4], 1)
                    elif name == "add":
                        h, i = a
                        k, c = 5 * h + i, CHUNKS[i]
                        t, r0 = c // 2, 64 * (c % 2)
                        if k == 0:
                            pe.wait_ge(sem("Kg"), 12)
                            pe.wait_ge(sem("mwT_read"), 3)
                        if i == 0:
                            pe.wait_ge(sem("vtok_read"), 3 * h + 3)
                        if k >= 2:
                            pe.wait_ge(sem("C_new"), k - 1)
                        mmul(bank[(7, 5)[k % 2]][:, 0:DV + 1], KmT[r0:r0 + 64, t, h * P:(h + 1) * P], Vaug[r0:r0 + 64, h % 2, t, :],
                             start=True, stop=True).then_inc(sem("C_add"), 1)
                    elif name == "inter":
                        h, i = a
                        k, c = 5 * h + i, CHUNKS[i]
                        t, r0 = c // 2, 64 * (c % 2)
                        t0 = TOK[t][0] + r0
                        if k == 0:
                            pe.wait_ge(sem("C_init"), 1)
                        if k >= 2:
                            pe.wait_ge(sem("inter_read"), k - 1)
                        if c in (1, 2, 3):
                            pe.wait_ge(sem("C_new"), k - (1 if c == 1 else 0))
                        mmul(bank[(6, 4)[k % 2]][r0:r0 + 64, 0:DV + 1], mix[:, h, t0:t0 + 64], C[:, c // 4, h, :], start=True, stop=True)\
                            .then_inc(sem("inter_done"), 1)
                    elif name == "intra":
                        h, t = a[0], ROWS[a[1]]
                        n = TOK[t][1]
                        gi = gid("intra", 3 * h + a[1])
                        bank_free(pe, gi)
                        pe.wait_ge(sem("mwT_read"), 3)
                        mmul(gbank(gi)[0:n, 0:DV + 1], wT[0:n, t, h * P:h * P + n], Vaug[0:n, h % 2, t, :], start=True, stop=True)\
                            .then_inc(bank_done[gi % 4], 1)
                    elif name == "heads":
                        h = a[0]
                        pe.wait_ge(sem("Yn"), 3 * h + 3)
                        for v in range(2):
                            gi = gid("heads", 2 * h + v)
                            bank_free(pe, gi)
                            turn_rows(gi, T, lambda t, n: Y[0:n, h % 2, t, 0:DV], v)

            for l in range(2):
                if l == 0:
                    input_attention()
                else:
                    input_recurrent()
                for i in range(8):
                    gi = gid(f"out{l}", i)
                    bank_free(pe, gi)
                    unit(UNITS[f"out{l}"] + i, gbank(gi)[:, 0:T], OH, OL,
                         hook=(lambda k: pe.wait_ge(sem(f"o_lo{l}"), k + 1)) if i == 0 else None)
                stats(f"mixpost{l}")
                spread_post(f"mixpost{l}")
                u0, g0 = UNITS[f"up{l}"], gid(f"up{l}", 0)
                ahead(range(u0, u0 + AHEAD), range(g0, g0 + AHEAD), hH, hL,
                      lambda k: pe.wait_ge(sem("h_lo"), eights(f"ffnpre{l}", k)))
                stats(f"ffnpre{l}")
                bank_free(pe, g0 + 3)
                unit(u0 + 3, gbank(g0 + 3)[:, 0:T], hH, hL, hook=rms_at(f"ffnpre{l}", 6))
                with pe.Fori(1, FT // 2) as it:
                    for s in range(4):
                        gi = g0 + s
                        pe.wait_ge(sem(("us" if s % 2 else "gp") + str(l)), it * 2 + (s // 2 - 1))
                        unit(u0 + s, gbank(gi)[:, 0:T], hH, hL, it=it * 4)
                u0 = UNITS[f"down{l}"]
                for i in range(8):
                    gi = gid(f"down{l}", i)
                    bank_free(pe, gi)
                    for q in range(4):
                        unit(u0 + 4 * i + q, gbank(gi)[:, 0:T], FH[:, 8 * q:8 * q + 8, :], FL[:, 8 * q:8 * q + 8, :], q == 0, q == 3,
                             hook=(lambda k: pe.wait_ge(sem(f"f_lo{l}"), 8 * q + k + 1)) if i == 0 else None)
                    if i == 0:
                        gi = gid(f"cs{l}", 0)
                        bank_free(pe, gi)
                        trans(gbank(gi)[:, 0:P], cs[:].rearrange("p a j -> p (a j)"), ident[:]).then_inc(bank_done[gi % 4], 1)
                stats(f"ffnpost{l}")
                for i in range(8):
                    if i == 3:
                        spread_post(f"ffnpost{l}")
                    gi = gid(f"ple{l}", i)
                    bank_free(pe, gi)
                    u = UNITS[f"ple{l}"] + i // 4
                    pe.wait_ge(lo_ready, u + 1)
                    out = gbank(gi)[:, 0:T]
                    for k in range(2):
                        c = k * 512 + (i % 4) * P
                        a, b = wh[:, u % R, c:c + P], wl[:, u % R, c:c + P]
                        mmul(out, a, peH[:, 2 * l + k, :], start=k == 0, stop=False)
                        mmul(out, a, peL[:, 2 * l + k, :], start=False, stop=False)
                        m = mmul(out, b, peH[:, 2 * l + k, :], start=False, stop=k == 1)
                    m.then_inc(unit_used if i % 4 == 3 else bank_done[gi % 4], 1)
                u0 = UNITS[f"gate{l}"]
                ahead(range(u0, u0 + AHEAD), [gid(f"gate{l}", i) for i in range(AHEAD)], OH, OL,
                      lambda k: pe.wait_ge(sem(f"xs_lo{l}"), k + 1))

                def turn_y(half):
                    for t, (t0, n) in enumerate(TOK):
                        gi = gid("y", 3 * half + t)
                        bank_free(pe, gi)
                        pe.wait_ge(sem("x_out1"), 4 * half + 4)
                        for j in range(4):
                            m = trans(gbank(gi)[0:n, j * P:(j + 1) * P], xT[:, 4 * half + j, t0:t0 + n], ident[:])
                        m.then_inc(bank_done[gi % 4], 1)

                for i in range(AHEAD, 8):
                    if l == 1 and i == 7:
                        turn_y(0)
                    gi = gid(f"gate{l}", i)
                    bank_free(pe, gi)
                    unit(u0 + i, gbank(gi)[:, 0:T], OH, OL)
                if l == 1:
                    turn_y(1)

        @block.scalar
        def _(act):
            A = nc.scalar.activation
            par = sem("ld_par0")
            for i, nm in enumerate(("ln_mix_pre", "ln_mix_post", "ln_ffn_pre", "ln_ffn_post")):
                act.dma_start(nrow[64 + 8 * i:72 + 8 * i, 0, :], I[nm][0].rearrange("(j c) -> j c", c=P)).then_inc(sem("ld_norms0"), 16)
            act.dma_start(nrow[0:64, 0, :], I["state_ffn_conv"][0, 0].rearrange("r (j c) -> (r j) c", c=P)).then_inc(sem("ld_norms0"), 16)
            act.dma_start(prow[0:96, 0, :], I["ffn_conv_w"][0].rearrange("t (j c) -> (t j) c", c=P)).then_inc(par, 16)
            act.dma_start(prow[96:128, 0, :], I["ffn_conv_b"][0].rearrange("(j c) -> j c", c=P)).then_inc(par, 16)
            act.dma_start(wnr[:, 0], I["w_att_in"][0][:, 1536:1544].rearrange("(k p) c -> p k c", p=P)).then_inc(sem("ld_narrow"), 16)
            act.dma_start(wnr[:, 1], I["w_rec_in"][0][:, 2048:2056].rearrange("(k p) c -> p k c", p=P)).then_inc(sem("ld_narrow"), 16)

            def hi(u, it=None):
                if it is None:
                    if u >= N_UNITS:
                        return
                    act.wait_ge(raw_landed[u % R], 16 * (u // R + 1))
                    if u >= R:
                        act.wait_ge(unit_used, u - R + 1)
                else:
                    act.wait_ge(raw_landed[u % R], it * 16 + 16 * (u // R + 1))
                    act.wait_ge(unit_used, it * 4 + (u - R + 1))
                A(wh[:, u % R, :], raw[:, u % R, :], ACT.Copy).then_inc(hi_ready, 1)

            def prenorm(l, j, col):
                A(hH[:, j, :], xT[:, j, :], ACT.Copy, scale=NC[:, l, col + j:col + j + 1]).then_inc(sem("h_hi"), 1)
                A(sqb[:, j, :], xT[:, j, :], ACT.Square).then_inc(sem("sq"), 1)

            def rms_for_pool(stage):
                act.wait_ge(sem("rms_again"), NORMS[stage] // 2 + 1)
                A(rstd2[:], bank[7][:, 0:T], ACT.Copy).then_inc(sem("rms_copied"), 1)

            def tok_copy(i):
                kind, t = i // 3, i % 3
                gi = gid("tok", i)
                n = TOK[t][1]
                bank_full(act, gi)
                dst = (Vtok, Ktok, Stok)[kind]
                w = 512 if kind < 2 else 256
                A(dst[0:n, t, :], gbank(gi)[0:n, 0:w], ACT.Copy).then_inc(sem("tok_read"), 1)

            def weights(i):
                n, w, b = TOK[TASKS[i][2]][1], score_width(i), i % 6
                act.wait_ge(sem("s_max"), i + 1)
                A(S_sb[0:n, b, 0:w], S_sb[0:n, b, 0:w], ACT.Exp, bias=amax[0:n, b, :], accum_out=aden[0:n, b, :]).then_inc(sem("s_exp"), 1)

            def pt_copy(i):
                fox, h, t = TASKS[i]
                n = TOK[t][1]
                act.wait_ge(sem("pt_done"), i + 1)
                if i >= 4:
                    act.wait_ge(sem("pv_done"), i - 3)
                full = (t + 1) if t < 2 else (2 if fox else 1)
                if n == P:
                    last = A(PT[:, i % 4, 0:full * P], bank[6 + i % 2][:, 0:full * P], ACT.Copy)
                else:
                    src = bank[6 + i % 2][:, 0:full * P].rearrange("p (b c) -> p b c", c=P)[:, :, 0:n]
                    dst = PT[:, i % 4, 0:full * P].rearrange("p (b c) -> p b c", c=P)[:, :, 0:n]
                    A(dst, src, ACT.Copy)
                    last = A(PT[0:64, i % 4, full * P:full * P + n], bank[6 + i % 2][0:64, full * P:full * P + n], ACT.Copy)
                last.then_inc(sem("pt_moved"), 1)

            def o_hi(j):
                gi = gid("o", j)
                bank_full(act, gi)
                A(OH[:, j, :], gbank(gi)[:, 0:T], ACT.Copy).then_inc(sem("o_hi0"), 1)

            def input_attention():
                for j in range(KT):
                    act.wait_ge(sem("x_in"), j + 1)
                    if j == 0:
                        act.wait_ge(sem("par_in"), 1)
                    prenorm(0, j, 64)
                hi(AHEAD)
                act.wait_ge(sem("ld_narrow"), 32)
                A(wnH[:].rearrange("p a b c -> p (a b c)"), wnr[:].rearrange("p a b c -> p (a b c)"), ACT.Copy).then_inc(sem("narrow_hi"), 1)
                act.wait_ge(sem("const2"), 1)
                for r0 in range(0, P, 32):
                    ins = A(selR[r0:r0 + 8, :], ident[0:8, 0:8], ACT.Copy)
                ins.then_inc(sem("sel"), 1)
                for i in range(12):
                    if i == 11:
                        act.wait_ge(sem("Frow"), 1)
                        A(FrowR[0:8, :], Frow[:], ACT.Copy)
                        A(FrowR[64:72, :], Frow[:], ACT.Copy).then_inc(sem("Frow_hi"), 1)
                    hi(i + R)
                    if i == 8:
                        act.wait_ge(sem("pe_f"), 4)
                        A(peH[:].rearrange("p a t -> p (a t)"), pef[:].rearrange("p a t -> p (a t)"), ACT.Copy).then_inc(sem("pe_hi"), 1)
                    if i == 6:
                        act.wait_ge(sem("lf_abs"), 1)
                        A(lfz[:, 1, :], lfz[:, 1, :], ACT.Exp, scale=-1.0).then_inc(sem("lf_exp"), 1)
                        act.wait_ge(sem("lf_exp"), 1)
                        A(lfz[:, 1, :], lfz[:, 1, :], ACT.Ln, bias=cst[0:8, 1:2]).then_inc(sem("lf_ln"), 1)
                for t in range(3):
                    tok_copy(t)
                for e in attention_events():
                    if e[0] == "scores":
                        weights(e[1])
                    elif e[0] == "half":
                        if e[2]:
                            hi(e[1] + R)
                    elif e[0] == "tok":
                        tok_copy(e[1])
                    elif e[0] == "turn":
                        pt_copy(e[1])
                    elif e[0] == "o_read":
                        o_hi(e[1])
                o_hi(7)

            def input_recurrent():
                u0 = UNITS["in1"]

                def out_gate(j):
                    act.wait_ge(sem("in_read1"), (9 if j < 6 else 17) + j)
                    A(sig[:, j, :], sig[:, j, :], ACT.Sigmoid).then_inc(sem("og"), 1)

                for e in recurrent_events():
                    name, a = e[0], e[1:]
                    if name == "unit":
                        hi(u0 + a[0] + R)
                        if a[0] == 5:
                            act.wait_ge(sem("mlf_abs"), 1)
                            A(mz[:, 2, :], mz[:, 2, :], ACT.Exp, scale=-1.0).then_inc(sem("mlf_exp"), 1)
                            act.wait_ge(sem("mlf_exp"), 1)
                            A(mz[:, 2, :], mz[:, 2, :], ACT.Ln, bias=cst[0:8, 1:2]).then_inc(sem("mlf_ln"), 1)
                        if a[0] == 15:
                            for j in range(6):
                                out_gate(j)
                    elif name == "half":
                        if a[1]:
                            hi(u0 + a[0] + R)
                            if a[0] >= 22:
                                out_gate(a[0] - 16)
                    elif name == "ktok":
                        gi = gid("ktok", a[0])
                        n = TOK[a[0]][1]
                        bank_full(act, gi)
                        A(KmT[0:n, a[0], :], gbank(gi)[0:n, :], ACT.Copy).then_inc(sem("ktok_read"), 1)
                        if a[0] == 2:
                            act.wait_ge(sem("mexp_in"), 1)
                            for nm in ("sdec", "em", "g"):
                                x = ml[nm][:].rearrange("p t h -> p (t h)")
                                A(x, x, ACT.Exp)
                            A(scd[:].rearrange("p c h -> p (c h)"), scd[:].rearrange("p c h -> p (c h)"), ACT.Exp).then_inc(sem("mexp"), 1)
                            for t in range(3):
                                n = TOK[t][1]
                                for h in range(MH):
                                    ins = A(Dm[0:n, t, h, 0:n], Dm[0:n, t, h, 0:n], ACT.Exp, bias=ml["nmu"][0:n, t, h:h + 1])
                                ins.then_inc(sem("mD"), 1)
                    elif name == "wT":
                        t = a[0]
                        n = TOK[t][1]
                        act.wait_ge(sem("mwT"), t + 1)
                        src = bank[5][0:n, :].rearrange("p (h c) -> p h c", h=MH)[:, :, 0:n]
                        dst = wT[0:n, t, :].rearrange("p (h c) -> p h c", h=MH)[:, :, 0:n]
                        A(dst, src, ACT.Copy).then_inc(sem("mwT_read"), 1)
                    elif name == "vtok":
                        h, t = a
                        n = TOK[t][1]
                        gi = gid("vtok", 3 * h + t)
                        bank_full(act, gi)
                        if 3 * h + t == 0:
                            act.wait_ge(sem("C_init"), 1)
                        A(Vaug[0:n, h % 2, t, 0:DV], gbank(gi)[0:n, 0:DV], ACT.Copy).then_inc(sem("vtok_read"), 1)
                    elif name == "inter":
                        h, i = a
                        k, c = 5 * h + i, CHUNKS[i]
                        t, r = c // 2, slice(64 * (c % 2), 64 * (c % 2) + 64)
                        act.wait_ge(sem("inter_done"), k + 1)
                        A(Y[r, h % 2, t, :], bank[(6, 4)[k % 2]][r, 0:DV + 1], ACT.Copy, scale=ml["sdec"][r, t, h:h + 1]).then_inc(sem("inter_read"), 1)
                    elif name == "intra":
                        h, t = a[0], ROWS[a[1]]
                        n = TOK[t][1]
                        k = 3 * h + a[1]
                        act.wait_ge(sem("Y"), k + 1)
                        if k:
                            act.wait_ge(sem("Yss"), k)
                        A(Ysq[0:n, :], Y[0:n, h % 2, t, 0:DV], ACT.Square, accum_out=yf["ss"][0:n, h % 2, t:t + 1]).then_inc(sem("Yss"), 1)
                    elif name == "heads":
                        for v in range(2):
                            j = 2 * a[0] + v
                            act.wait_ge(sem("mo_f"), j + 1)
                            A(OH[:, j, :], obuf[:, v, :], ACT.Copy).then_inc(sem("o_hi1"), 1)

            for u in range(AHEAD):
                hi(u)
            for l in range(2):
                if l == 0:
                    input_attention()
                else:
                    input_recurrent()
                for i in range(8):
                    gi = gid(f"out{l}", i)
                    bank_full(act, gi)
                    A(sqb[:, i, :], gbank(gi)[:, 0:T], ACT.Square).then_inc(sem("sq"), 1)
                    A(mix[:, i, :], gbank(gi)[:, 0:T], ACT.Copy, scale=NC[:, l, 72 + i:73 + i]).then_inc(sem(f"mix_{l}"), 1)
                    hi(UNITS[f"out{l}"] + i + R)
                rms_for_pool(f"mixpost{l}")
                for j in range(KT):
                    x_added(act, f"mixpost{l}", j)
                    prenorm(l, j, 80)
                act.wait_ge(sem(f"scratch_out{l}"), 1)
                u0 = UNITS[f"up{l}"]
                with act.Fori(0, FT // 2) as it:
                    A(mark[:], mark[:], ACT.Gelu_apprx_tanh)
                    for s in range(2):
                        hi(u0 + 2 * s + R, it)
                        act.wait_ge(sem(f"gp{l}"), it * 2 + (s + 1))
                        j = it * 2 + s
                        A(cv[:, s, :], gp[:, s, 2:T + 4], ACT.Identity, scale=PC[:, l, bass.ds(j + 64, 1)],
                          bias=PC[:, l, bass.ds(j + 96, 1)]).then_inc(sem(f"cv{l}"), 1)
                        act.wait_ge(sem(f"conv{l}"), it * 4 + (2 * s + 2))
                        A(cv[:, s, :], cv[:, s, :], ACT.Gelu_apprx_tanh).then_inc(sem(f"gelu{l}"), 1)
                        hi(u0 + 2 * s + 1 + R, it)
                        act.wait_ge(sem(f"f{l}"), it * 2 + (s + 1))
                        A(FH[:, bass.ds(j, 1), :].rearrange("p a t -> p (a t)"), fb[:, s, :], ACT.Copy).then_inc(sem(f"f_hi{l}"), 1)
                u0 = UNITS[f"down{l}"]
                for i in range(8):
                    for q in range(4):
                        if q == 3:
                            gi = gid(f"down{l}", i)
                            bank_full(act, gi)
                            A(sqb[:, i, :], gbank(gi)[:, 0:T], ACT.Square).then_inc(sem("sq"), 1)
                            A(mix[:, i, :], gbank(gi)[:, 0:T], ACT.Copy, scale=NC[:, l, 88 + i:89 + i]).then_inc(sem(f"mixf_{l}"), 1)
                        hi(u0 + 4 * i + q + R)

                def ple_copy(i):
                    gi = gid(f"ple{l}", i)
                    bank_full(act, gi)
                    A(sqb[:, i, :], gbank(gi)[:, 0:T], ACT.Copy).then_inc(sem(f"ple_sb{l}"), 1)

                def x_hi(i):
                    x_added(act, f"ffnpost{l}", i)
                    A(OH[:, i, :], xT[:, i, :], ACT.Copy).then_inc(sem(f"xs_hi{l}"), 1)

                for i in range(3):
                    ple_copy(i)
                rms_for_pool(f"ffnpost{l}")
                ple_copy(3)
                hi(UNITS[f"ple{l}"] + R)
                ple_copy(4)
                ple_copy(5)
                x_hi(0)
                ple_copy(6)
                x_hi(1)
                ple_copy(7)
                hi(UNITS[f"ple{l}"] + 1 + R)
                for i in range(2, 8):
                    x_hi(i)
                for i in range(8):
                    gi = gid(f"gate{l}", i)
                    bank_full(act, gi)
                    if i >= 2:
                        act.wait_ge(sem(f"x_out{l}"), i - 1)
                    A(sgb[:, i % 2, :], gbank(gi)[:, 0:T], ACT.Sigmoid).then_inc(sem(f"sigm{l}"), 1)
                    hi(UNITS[f"gate{l}"] + i + R)
                    if l == 0 and i:
                        act.wait_ge(sem("x_out0"), i)
                        prenorm(1, i - 1, 64)
                    if l == 1 and i == 6:
                        for t in range(3):
                            copy_y(act, t)
                if l == 0:
                    act.wait_ge(sem("x_out0"), 8)
                    prenorm(1, 7, 64)
            copy_y(act, 4)

        @block.vector
        def _(dve):
            V = nc.vector

            def lo(u, it=None):
                if it is None:
                    if u >= N_UNITS:
                        return
                    dve.wait_ge(hi_ready, u + 1)
                else:
                    dve.wait_ge(hi_ready, it * 4 + (u + 1))
                V.tensor_tensor(wl[:, u % R, :], raw[:, u % R, :], wh[:, u % R, :].bitcast(F32), ALU.subtract).then_inc(lo_ready, 1)

            def prenorm_lo(stage, l, j, col):
                dve.wait_ge(sem("h_hi"), eights(stage, j))
                V.scalar_tensor_tensor(out=hL[:, j, :], in0=xT[:, j, :], scalar=NC[:, l, col + j:col + j + 1],
                                       in1=hH[:, j, :].bitcast(F32), op0=ALU.mult, op1=ALU.subtract).then_inc(sem("h_lo"), 1)

            def mean_square(stage):
                dve.wait_ge(sem("sq_sum"), NORMS[stage] + 1)
                V.tensor_scalar(ms[:], bank[4][:, 0:3], 1.0 / D, EPS, ALU.mult, ALU.add).then_inc(sem("ms"), 1)

            def rms_diagonal(stage):
                dve.wait_ge(sem("rcol"), NORMS[stage] + 1)
                for t in range(3):
                    V.tensor_scalar(diag[:, t, :], ident[:], rcol[:, t:t + 1], None, ALU.mult).then_inc(sem("diag"), 1)

            def rms_rows(stage):
                dve.wait_ge(sem("rms_rows"), NORMS[stage] + 1)
                V.tensor_copy(rstd[:], bank[5][:, 0:T]).then_inc(sem("rstd"), 1)
                dve.wait_ge(sem("rstd"), NORMS[stage] // 2 + 1)

            def postnorm(stage, low):
                mean_square(stage)
                rms_diagonal(stage)
                dve.wait_ge(sem("rms_rows"), NORMS[stage] + 1)
                k0 = 4 * (NORMS[stage] // 2)
                for j in range(0, KT, 2):
                    V.tensor_tensor(mix[:, j, :], mix[:, j, :], bank[5][:, 0:T], ALU.mult).then_inc(sem("post_even"), 1)
                    dve.wait_ge(sem("post_even"), k0 + j // 2 + 1)
                    V.tensor_tensor(xT[:, j, :], xT[:, j, :], mix[:, j, :], ALU.add).then_inc(sem("x_even"), 1)
                    if j:
                        low(j - 2)
                        low(j - 1)
                dve.wait_ge(sem("x_odd"), k0 + 4)
                low(6)
                low(7)

            def scaled(l, i, dst, rows=slice(0, P), factor=None, src_rows=None, last=True, name=None):
                sr = src_rows or rows
                src = gbank(gid(name or f"in{l}", i))[sr, 0:T]
                if factor is None:
                    ins = V.tensor_tensor(dst, src, rstd[sr, :], ALU.mult)
                else:
                    ins = V.scalar_tensor_tensor(out=dst, in0=src, scalar=factor, in1=rstd[sr, :], op0=ALU.mult, op1=ALU.mult)
                if last:
                    ins.then_inc(sem(f"in_read{l}"), 1)
                return ins

            def narrow(l, z):
                bank_full(dve, gid(f"narrow{l}", 0))
                s = sem(f"narrow_step{l}")
                scaled(l, 0, z[:, 0, :], rows=slice(0, 8), last=False, name=f"narrow{l}").then_inc(s, 1)
                dve.wait_ge(s, 1)
                if l == 0:
                    dve.wait_ge(sem("ld_bias"), 48)
                V.tensor_scalar(z[:, 0, :], z[:, 0, :], bcol[:, l:l + 1], None, ALU.add).then_inc(s, 1)
                dve.wait_ge(s, 2)
                k = 1 if l == 0 else 2
                V.scalar_tensor_tensor(out=z[:, k, :], in0=z[:, 0, :], scalar=-1.0, in1=z[:, 0, :], op0=ALU.mult, op1=ALU.max)\
                    .then_inc(sem("lf_abs" if l == 0 else "mlf_abs"), 1)
                V.tensor_scalar(z[:, 2 if l == 0 else 1, :], z[:, 0, :], 0.0, None, ALU.min).then_inc(s, 1)

            def in0_read(i):
                bank_full(dve, gid("in0", i))
                if i < 4:
                    scaled(0, i, mix[:, i, :], factor=HD ** -0.5)
                elif i < 8:
                    scaled(0, i, kT[:, i - 4, :])
                elif i < 12:
                    scaled(0, i, sqb[:, i - 8, :])
                elif i < 16:
                    scaled(0, i, mix[:, i - 8, :], factor=HD ** -0.5)
                elif i == 16:
                    for half in range(2):
                        for g in range(2):
                            scaled(0, i, kdup[64 * half:64 * half + 64, g, :], src_rows=slice(64 * g, 64 * g + 64), last=False)
                    scaled(0, i, kplain[:])
                else:
                    scaled(0, i, sqb[:, 4, :])

            def scores_moved(i):
                fox, h, t = TASKS[i]
                n, b, w = TOK[t][1], i % 6, score_width(i)
                dve.wait_ge(sem("s_done"), i + 1)
                if i >= 6:
                    dve.wait_ge(sem("pt_done"), i - 5)
                src = bank[4 + i % 2]
                if fox:
                    m = MFox[0:n, 384 - w:384] if t < 2 else MFox[0:n, 0:w]
                    V.scalar_tensor_tensor(out=S_sb[0:n, b, 0:w], in0=src[0:n, 0:w], scalar=Ftok[0:n, t, h:h + 1], in1=m,
                                           op0=ALU.add, op1=ALU.add).then_inc(sem("s_moved"), 1)
                else:
                    V.tensor_copy(S_sb[0:n, b, w - 1:w], sinkb[0:n, h:h + 1])
                    if t < 2:
                        V.tensor_tensor(S_sb[0:n, b, 0:w - 1], src[0:n, 0:w - 1], MSwa[0:n, 256 - (w - 1):256], ALU.add).then_inc(sem("s_moved"), 1)
                    else:
                        V.tensor_copy(S_sb[0:n, b, 0:w - 1], src[0:n, 0:w - 1]).then_inc(sem("s_moved"), 1)
                dve.wait_ge(sem("s_moved"), i + 1)
                V.tensor_reduce(amax[0:n, b, :], S_sb[0:n, b, 0:w], X, ALU.max, negate=True).then_inc(sem("s_max"), 1)

            def inverse_sum(i):
                n, b = TOK[TASKS[i][2]][1], i % 6
                dve.wait_ge(sem("s_exp"), i + 1)
                V.reciprocal(ainv[0:n, b, :], aden[0:n, b, :]).then_inc(sem("a_inv"), 1)

            def o_lo(j):
                dve.wait_ge(sem("o_hi0"), j + 1)
                V.tensor_tensor(OL[:, j, :], gbank(gid("o", j))[:, 0:T], OH[:, j, :].bitcast(F32), ALU.subtract).then_inc(sem("o_lo0"), 1)

            def input_attention():
                def par_in(i):
                    bank_full(dve, gid("par", i))
                    n = (P, 96 + 8 * (i // 2))[i % 2]
                    V.tensor_copy((PC, NC)[i % 2][:, i // 2, 0:n], gbank(gid("par", i))[:, 0:n]).then_inc(sem("par_in"), 1)

                def x_in(j):
                    gi = gid("x", j)
                    bank_full(dve, gi)
                    V.tensor_copy(xT[:, j, :], gbank(gi)[:, 0:T]).then_inc(sem("x_in"), 1)

                for j in range(4):
                    x_in(j)
                par_in(1)
                x_in(4)
                x_in(5)
                lo(0)
                x_in(6)
                x_in(7)
                lo(1)
                prenorm_lo("mixpre0", 0, 0, 64)
                lo(2)
                for j in range(1, 8):
                    prenorm_lo("mixpre0", 0, j, 64)
                par_in(0)
                lo(AHEAD)
                add_squares(dve, V, "mixpre0")
                dve.wait_ge(sem("narrow_hi"), 1)
                V.tensor_tensor(wnL[:].rearrange("p a b c -> p (a b c)"), wnr[:].rearrange("p a b c -> p (a b c)"),
                                wnH[:].rearrange("p a b c -> p (a b c)").bitcast(F32), ALU.subtract).then_inc(sem("narrow_split"), 1)
                mean_square("mixpre0")
                lo(4)
                rms_diagonal("mixpre0")
                lo(5)
                rms_rows("mixpre0")
                in0_read(0)
                in0_read(1)
                in0_read(2)
                lo(6)
                in0_read(3)
                lo(7)
                for i in range(4, 12):
                    for kind, j in TURNS_AT.get(i, []):
                        if kind == "narrow0":
                            narrow(0, lfz)
                            continue
                        if kind == "par":
                            par_in(j)
                            continue
                        gi = gid(kind, j)
                        bank_full(dve, gi)
                        if kind == "pe":
                            V.tensor_copy(pef[:, j, :], gbank(gi)[:, 0:T]).then_inc(sem("pe_f"), 1)
                        elif j < 4:
                            V.tensor_copy(kcT[:, j, :], gbank(gi)[:, 0:PAST]).then_inc(sem("cache_read"), 1)
                        else:
                            for half in range(2):
                                for g in range(2):
                                    ins = V.tensor_copy(kcdup[64 * half:64 * half + 64, g, :], gbank(gi)[64 * g:64 * g + 64, 0:P])
                            ins.then_inc(sem("cache_read"), 1)
                    if i == 7:
                        dve.wait_ge(sem("lf_ln"), 1)
                        dve.wait_ge(sem("narrow_step0"), 3)
                        V.tensor_tensor(lfz[:, 0, :], lfz[:, 2, :], lfz[:, 1, :], ALU.subtract).then_inc(sem("lf_ready"), 1)
                    elif i == 8:
                        dve.wait_ge(sem("lf_tr"), 1)
                        V.tensor_copy(lftok[:, 0:2, :], bank[5][:, 0:16].rearrange("p (t h) -> p t h", t=2))
                        V.tensor_copy(lftok[0:64, 2, :], bank[5][0:64, 16:24]).then_inc(sem("lf_tok"), 1)
                    elif i == 9:
                        dve.wait_ge(sem("pe_hi"), 1)
                        V.tensor_tensor(peL[:].rearrange("p a t -> p (a t)"), pef[:].rearrange("p a t -> p (a t)"),
                                        peH[:].rearrange("p a t -> p (a t)").bitcast(F32), ALU.subtract).then_inc(sem("pe_split"), 1)
                        dve.wait_ge(sem("pe_split"), 1)
                    elif i == 10:
                        dve.wait_ge(sem("F_sums"), 1)
                        V.tensor_copy(Ftok[:, 0:2, :], bank[6][:, 0:16].rearrange("p (t h) -> p t h", t=2))
                        V.tensor_copy(Ftok[0:64, 2, :], bank[6][0:64, 16:24])
                        V.tensor_scalar(Frow[:, 0:256], bank[7][0:8, 0:256], -1.0, None, ALU.mult)
                        V.tensor_scalar(Frow[:, 256:576], bank[5][0:8, 0:320], -1.0, None, ALU.mult).then_inc(sem("Frow"), 1)
                    elif i == 11:
                        dve.wait_ge(sem("Frow_hi"), 1)
                        dve.wait_ge(sem("sel"), 1)
                        V.tensor_tensor(FrowR[32:40, :], Frow[:], FrowR[0:8, :].bitcast(F32), ALU.subtract)
                        V.tensor_tensor(FrowR[96:104, :], Frow[:], FrowR[64:72, :].bitcast(F32), ALU.subtract).then_inc(sem("F_rows"), 1)
                    in0_read(i)
                    lo(i + R)
                for e in attention_events():
                    if e[0] == "scores":
                        scores_moved(e[1])
                        if e[1]:
                            inverse_sum(e[1] - 1)
                    elif e[0] == "half":
                        if e[2]:
                            in0_read(e[1])
                            lo(e[1] + R)
                    elif e[0] == "turn" and e[1] == len(TASKS) - SKEW_T:
                        inverse_sum(len(TASKS) - 1)
                    elif e[0] == "o_read":
                        o_lo(e[1])
                o_lo(7)

            def input_recurrent():
                st = sem("m_step")
                ns = [0]

                def link(ins):
                    ns[0] += 1
                    ins.then_inc(st, 1)
                    dve.wait_ge(st, ns[0])

                fl = {nm: ml[nm][:].rearrange("p t h -> p (t h)") for nm in ml}
                u0 = UNITS["in1"]

                def in1_read(i):
                    bank_full(dve, gid("in1", i))
                    if i < 4:
                        scaled(1, i, mix[:, i, :])
                    elif i < 8:
                        scaled(1, i, mix[:, i, :], factor=DK ** -0.5)
                    elif i < 14:
                        scaled(1, i, sig[:, i - 8, :])
                    elif i < 22:
                        scaled(1, i, sqb[:, i - 14, :])
                    else:
                        scaled(1, i, sig[:, i - 16, :])

                def maxima(t):
                    dve.wait_ge(sem("mspread"), t + 1)
                    b = bank[5 + t][:, :].rearrange("p (h s) -> p h s", h=MH)
                    V.tensor_reduce(MF[:, t, :, :], bank[5 + t][:, :].rearrange("p (h c s) -> p h c s", h=MH, c=2), X, ALU.max)
                    for h in range(MH):
                        ins = V.tensor_tensor(Dm[:, t, h, :], b[:, h, :], MBlk[:], ALU.add)
                    link(ins)
                    V.tensor_reduce(ml["M"][:, t, :], Dm[:, t], X, ALU.max).then_inc(sem("mD_raw"), 1)

                def running_maxima():
                    dve.wait_ge(sem("mD_raw"), 3)
                    for c in range(5):
                        t, half = c // 2, c % 2
                        link(V.tensor_tensor(muc[:, c, :], mprev[:, c, :], MF[:, t, :, half], ALU.max))
                        if c < 4:
                            dst = mprev[:, c + 1, :] if c < 3 else mprev[:, 5, :]
                            link(V.tensor_tensor(dst, muc[:, c, :], BL[:, half, 4 * t:4 * t + 4], ALU.add))
                        else:
                            link(V.tensor_tensor(mz[:, 3, 0:4], muc[0:8, c, :], BL[0:8, half, 4 * t:4 * t + 4], ALU.add))
                    for t in range(3):
                        for half in range(2):
                            c = min(2 * t + half, 4)
                            rows = slice(64 * half, 64 * half + 64)
                            V.tensor_copy(ml["mp"][rows, t, :], mprev[rows, c, :])
                            ins = V.tensor_copy(ml["muL"][rows, t, :], muc[rows, c, :])
                    link(ins)
                    link(V.tensor_tensor(fl["mu"], fl["mp"], fl["M"], ALU.max))
                    V.tensor_scalar(fl["nmu"], fl["mu"], -1.0, None, ALU.mult)
                    V.tensor_tensor(fl["sdec"], fl["mp"], fl["mu"], ALU.subtract)
                    link(V.tensor_tensor(fl["t0"], fl["bt"], fl["mu"], ALU.add))
                    V.tensor_scalar(fl["em"], fl["t0"], -1.0, None, ALU.mult)
                    V.tensor_tensor(fl["g"], fl["a"], fl["muL"], ALU.subtract)
                    V.tensor_tensor(scd[:], mprev[:, 0:5, :], muc[:], ALU.subtract).then_inc(sem("mexp_in"), 1)

                def head_norm(h):
                    b = h % 2
                    y = Y[:, b]
                    den, r, v, f = (yf[nm][:, b, :] for nm in ("den", "r", "v", "f"))
                    link(V.scalar_tensor_tensor(out=den, in0=y[:, :, DV], scalar=-1.0, in1=y[:, :, DV], op0=ALU.mult, op1=ALU.max))
                    link(V.tensor_tensor(den, den, ml["em"][:, :, h], ALU.max))
                    link(V.reciprocal(r, den))
                    link(V.tensor_tensor(v, r, r, ALU.mult))
                    dve.wait_ge(sem("Yss"), 3 * h + 3)
                    link(V.tensor_tensor(v, v, yf["ss"][:, b, :], ALU.mult))
                    V.tensor_scalar(v, v, 1.0 / DV, EPS, ALU.mult, ALU.add).then_inc(sem("Yvar"), 1)
                    dve.wait_ge(sem("Yroot"), h + 1)
                    link(V.tensor_tensor(f, yf["w"][:, b, :], r, ALU.mult))
                    for t in range(3):
                        n = TOK[t][1]
                        V.tensor_scalar(Y[0:n, b, t, 0:DV], Y[0:n, b, t, 0:DV], f[0:n, t:t + 1], None, ALU.mult).then_inc(sem("Yn"), 1)

                for e in recurrent_events():
                    name, a = e[0], e[1:]
                    if name == "unit":
                        i = a[0]
                        if i == 1:
                            rms_rows("mixpre1")
                            in1_read(0)
                        elif i == 0:
                            lo(u0 + R)
                        if i:
                            in1_read(i)
                            lo(u0 + i + R)
                        if i == 5:
                            dve.wait_ge(sem("mlf_ln"), 1)
                            dve.wait_ge(sem("narrow_step1"), 3)
                            V.tensor_tensor(mz[:, 1, :], mz[:, 1, :], mz[:, 2, :], ALU.subtract).then_inc(sem("mgates"), 1)
                    elif name == "stats":
                        mean_square("mixpre1")
                        rms_diagonal("mixpre1")
                    elif name == "narrow":
                        narrow(1, mz)
                        V.memset(gt[:], 0.0)
                        V.memset(C[:, 0], 0.0)
                        V.memset(mprev[:, 0, :], 0.0)
                        V.memset(Y[:], 1.0)
                        V.memset(yf["ss"][:], 1.0)
                        link(V.memset(Vaug[:, :, :, DV:DV + 1], 1.0))
                        dve.wait_ge(sem("ld_state"), 48)
                        dve.sem_inc(sem("C_init"), 1)
                    elif name == "half":
                        if a[1]:
                            in1_read(a[0])
                            lo(u0 + a[0] + R)
                    elif name == "gates":
                        dve.wait_ge(sem("mgates_tr"), 1)
                        V.tensor_copy(gt[:, 0:2, :], bank[5][:, 0:32].rearrange("p (t c) -> p t c", t=2))
                        link(V.tensor_copy(gt[0:64, 2, :], bank[5][0:64, 32:48]))
                        V.tensor_copy(ml["lf"][:], gt[:, :, 12:16]).then_inc(sem("mlf"), 1)
                    elif name == "sums":
                        dve.wait_ge(sem("msums"), 1)
                        V.tensor_copy(fl["bt"], bank[6][:, 0:12])
                        V.tensor_copy(BL[:, 0, :], bank[6][:, 16:28])
                        link(V.tensor_copy(BL[:, 1, :], bank[7][:, 32:44]))
                        V.tensor_tensor(ml["a"][:], gt[:, :, 0:4], ml["bt"][:], ALU.subtract).then_inc(sem("ma"), 1)
                    elif name == "arow":
                        dve.wait_ge(sem("maT"), 1)
                        V.tensor_copy(aT[:], bank[7][0:12, 0:P]).then_inc(sem("maT_read"), 1)
                    elif name == "spread":
                        maxima(a[0])
                    elif name == "maxima":
                        running_maxima()
                    elif name == "qk":
                        t = a[0]
                        n = TOK[t][1]
                        if t == 0:
                            dve.wait_ge(sem("mexp"), 1)
                            dve.wait_ge(sem("ktok_read"), 3)
                            for tt in range(3):
                                nn = TOK[tt][1]
                                for h in range(MH):
                                    k = KmT[0:nn, tt, h * P:(h + 1) * P]
                                    V.tensor_scalar(k, k, ml["g"][0:nn, tt, h:h + 1], None, ALU.mult).then_inc(sem("Kg"), 1)
                        dve.wait_ge(sem("mD"), t + 1)
                        dve.wait_ge(sem("mqk"), t + 1)
                        src = bank[4][0:n, :].rearrange("p (h c) -> p h c", h=MH)[:, :, 0:n]
                        V.tensor_tensor(Dm[0:n, t, :, 0:n], src, Dm[0:n, t, :, 0:n], ALU.mult).then_inc(sem("mw"), 1)
                    elif name == "inter":
                        h, i = a
                        k, c = 5 * h + i, CHUNKS[i]
                        dve.wait_ge(sem("C_add"), k + 1)
                        dve.wait_ge(sem("inter_done"), k + 1)
                        s = c // 4
                        V.scalar_tensor_tensor(out=C[:, s, h, :], in0=C[:, s, h, :], scalar=scd[:, c, h:h + 1],
                                               in1=bank[(7, 5)[k % 2]][:, 0:DV + 1], op0=ALU.mult, op1=ALU.add).then_inc(sem("C_new"), 1)
                    elif name == "intra":
                        h, t = a[0], ROWS[a[1]]
                        n = TOK[t][1]
                        gi = gid("intra", 3 * h + a[1])
                        bank_full(dve, gi)
                        dve.wait_ge(sem("inter_read"), 5 * h + (2, 3, 5)[a[1]])
                        V.tensor_tensor(Y[0:n, h % 2, t, :], gbank(gi)[0:n, 0:DV + 1], Y[0:n, h % 2, t, :], ALU.add).then_inc(sem("Y"), 1)
                        if a[1] == 2:
                            dve.wait_ge(sem("Y"), 3 * h + 3)
                            head_norm(h)
                    elif name == "heads":
                        h = a[0]
                        dve.wait_ge(sem("og"), 8 if h == MH - 1 else 6)
                        for v in range(2):
                            j = 2 * h + v
                            gi = gid("heads", j)
                            bank_full(dve, gi)
                            V.scalar_tensor_tensor(out=obuf[:, v, :], in0=gbank(gi)[:, 0:T], scalar=NC[:, 1, 96 + j:97 + j],
                                                   in1=sig[:, j, :], op0=ALU.mult, op1=ALU.mult).then_inc(sem("mo_f"), 1)
                        for v in range(2):
                            j = 2 * h + v
                            dve.wait_ge(sem("o_hi1"), j + 1)
                            V.tensor_tensor(OL[:, j, :], obuf[:, v, :], OH[:, j, :].bitcast(F32), ALU.subtract).then_inc(sem("o_lo1"), 1)

            for l in range(2):
                if l == 0:
                    input_attention()
                else:
                    input_recurrent()
                for i in range(8):
                    lo(UNITS[f"out{l}"] + i + R)
                dve.wait_ge(sem(f"mix_{l}"), 8)
                postnorm(f"mixpost{l}", lambda j: prenorm_lo(f"ffnpre{l}", l, j, 80))
                mean_square(f"ffnpre{l}")
                rms_diagonal(f"ffnpre{l}")
                rms_rows(f"ffnpre{l}")
                dve.wait_ge(sem(f"scratch_out{l}"), 1)
                u0, g0 = UNITS[f"up{l}"], gid(f"up{l}", 0)
                with dve.Fori(0, FT // 2) as it:
                    for s in range(2):
                        j = it * 2 + s
                        ga, gu = g0 + 2 * s, g0 + 2 * s + 1
                        hist = NC[:, l, 0:64].rearrange("p (r j) -> p r j", r=2)[:, :, bass.ds(j, 1)].rearrange("p r j -> p (r j)")
                        V.tensor_copy(gp[:, s, 258:260], hist)
                        bank_full(dve, ga, it * 4)
                        V.tensor_tensor(gp[:, s, 2:258], gbank(ga)[:, 0:TP], rstd[:, 0:TP], ALU.mult)
                        V.tensor_tensor(gp[:, s, 260:324], gbank(ga)[:, TP:T], rstd[:, TP:T], ALU.mult).then_inc(sem(f"gp{l}"), 1)
                        lo(u0 + 2 * s + R, it)
                        dve.wait_ge(sem(f"cv{l}"), it * 2 + (s + 1))
                        for tap in (1, 0):
                            V.scalar_tensor_tensor(out=cv[:, s, :], in0=gp[:, s, tap:tap + T + 2], scalar=PC[:, l, bass.ds(j + 32 * tap, 1)],
                                                   in1=cv[:, s, :], op0=ALU.mult, op1=ALU.add).then_inc(sem(f"conv{l}"), 1)
                            if tap:
                                dve.wait_ge(sem(f"conv{l}"), it * 4 + (2 * s + 1))
                        bank_full(dve, gu, it * 4)
                        V.tensor_tensor(us[:, s, :], gbank(gu)[:, 0:T], rstd[:], ALU.mult).then_inc(sem(f"us{l}"), 1)
                        lo(u0 + 2 * s + 1 + R, it)
                        dve.wait_ge(sem(f"f_hi{l}"), it * 2 + (s + 1))
                        V.tensor_tensor(FL[:, bass.ds(j, 1), :].rearrange("p a t -> p (a t)"), fb[:, s, :],
                                        FH[:, bass.ds(j, 1), :].rearrange("p a t -> p (a t)").bitcast(F32), ALU.subtract).then_inc(sem(f"f_lo{l}"), 1)
                for i in range(32):
                    lo(UNITS[f"down{l}"] + i + R)
                    if i == 4:
                        bank_full(dve, gid(f"cs{l}", 0))
                        V.tensor_copy(csT[:], gbank(gid(f"cs{l}", 0))[:, 0:P]).then_inc(sem(f"csT{l}"), 1)
                dve.wait_ge(sem(f"mixf_{l}"), 8)

                def x_lo(j):
                    dve.wait_ge(sem(f"xs_hi{l}"), j + 1)
                    V.tensor_tensor(OL[:, j, :], xT[:, j, :], OH[:, j, :].bitcast(F32), ALU.subtract).then_inc(sem(f"xs_lo{l}"), 1)
                    if j < 2:
                        lo(UNITS[f"ple{l}"] + j + R)

                postnorm(f"ffnpost{l}", x_lo)
                for i in range(8):
                    dve.wait_ge(sem(f"sigm{l}"), i + 1)
                    dve.wait_ge(sem(f"ple_sb{l}"), i + 1)
                    V.tensor_tensor(sgb[:, i % 2, :], sgb[:, i % 2, :], sqb[:, i, :], ALU.mult).then_inc(sem(f"sg{l}"), 1)
                    dve.wait_ge(sem(f"sg{l}"), i + 1)
                    V.tensor_tensor(xT[:, i, :], xT[:, i, :], sgb[:, i % 2, :], ALU.add).then_inc(sem(f"x_out{l}"), 1)
                    lo(UNITS[f"gate{l}"] + i + R)
                    if l == 0 and i:
                        prenorm_lo("mixpre1", 1, i - 1, 64)
                if l == 0:
                    prenorm_lo("mixpre1", 1, 7, 64)
            copy_y(dve, 3)
            copy_y(dve, 5)


_OUTS = [
    ("y_prompt", (1, TP, D)), ("y_sample", (1, TS, D)),
    ("p_fox_k", (1, 1, TP, NH, HD)), ("p_fox_v", (1, 1, TP, NH, HD)), ("p_fox_logf", (1, 1, TP, NH)),
    ("p_swa_k", (1, 1, P, 2, HD)), ("p_swa_v", (1, 1, P, 2, HD)),
    ("p_ml_c", (1, 1, MH, DK, DV)), ("p_ml_n", (1, 1, MH, DK)), ("p_ml_m", (1, 1, MH)), ("p_conv", (2, 1, 2, FF)),
    ("s_fox_k", (1, 1, TS, NH, HD)), ("s_fox_v", (1, 1, TS, NH, HD)), ("s_fox_logf", (1, 1, TS, NH)),
    ("s_swa_k", (1, 1, P, 2, HD)), ("s_swa_v", (1, 1, P, 2, HD)),
    ("s_ml_c", (1, 1, MH, DK, DV)), ("s_ml_n", (1, 1, MH, DK)), ("s_ml_m", (1, 1, MH)), ("s_conv", (2, 1, 2, FF)),
]
_SQUEEZED = {"p_fox_k", "p_fox_v", "p_fox_logf"}


def kernel(**inputs):
    import numpy as np
    import concourse.bacc as bacc
    from concourse.bass_utils import run_bass_kernel_spmd as run

    nc = bacc.Bacc("TRN2", target_bir_lowering=False, num_devices=1)
    arrays, ins = {}, {}
    for name, a in inputs.items():
        a = np.ascontiguousarray(a)
        arrays[f"in_{name}"] = a
        ins[name] = nc.dram_tensor(f"in_{name}", a.shape, F32, kind="ExternalInput").ap()
    outs = {n: nc.dram_tensor(f"out_{n}", s, F32, kind="ExternalOutput").ap() for n, s in _OUTS}
    encoder_step(nc, ins, outs)
    r = run(nc, [arrays], core_ids=[0]).results[0]
    return tuple(r[f"out_{n}"] for n, _ in _OUTS)
```
